# Optimizing a Trainium2 kernel written in Bass

```python
import jax, jax.numpy as jnp
from jax import lax
import numpy as np

D_MODEL = 1024
BATCH = 1
SEQ = 512
DEPTH = 2

GRID_W = 64
CTX_LEN = 256
D_CONV = 512
CONV_K = 31
D_SHORT = 512
SHORT_K = 3
N_Q_HEADS = 8
N_KV_HEADS = 2
HEAD_DIM = 64
WINDOW = 128
BLOCK = 128
D_FOURIER = 512
N_FOURIER_GROUPS = 4
N_BRANCH = 4
N_EXPERTS = 16
CAPACITY_FACTOR = 2
D_EXPERT = 1024
ROPE_BASE = 10000.0
EPS = 1e-6
NEG_INF = -1e30
N_IN = 2 * D_CONV + 3 * D_SHORT + (N_Q_HEADS + 2 * N_KV_HEADS) * HEAD_DIM + D_FOURIER + N_BRANCH * D_MODEL

kernel_name = 'hybrid_gated_parallel_ec_moe_dit'

def rms_norm(x, g):
    xf = x.astype(jnp.float32)
    y = xf * lax.rsqrt(jnp.mean(xf * xf, axis=-1, keepdims=True) + EPS)
    return (y * g.astype(jnp.float32)).astype(x.dtype)

def layer_norm(x, g, b):
    xf = x.astype(jnp.float32)
    mu = jnp.mean(xf, axis=-1, keepdims=True)
    xc = xf - mu
    y = xc * lax.rsqrt(jnp.mean(xc * xc, axis=-1, keepdims=True) + EPS)
    return (y * g.astype(jnp.float32) + b.astype(jnp.float32)).astype(x.dtype)

def modulate(h, shift, scale):
    return h * (1 + scale) + shift

def dwconv(x, w):
    k = w.shape[0]
    return lax.conv_general_dilated(
        x, w[:, None, :].astype(x.dtype), window_strides=(1,),
        padding=[(k // 2, k // 2)], dimension_numbers=('NWC', 'WIO', 'NWC'),
        feature_group_count=x.shape[-1])

def col_offsets():
    sizes = (2 * D_CONV, 3 * D_SHORT, N_Q_HEADS * HEAD_DIM, N_KV_HEADS * HEAD_DIM,
             N_KV_HEADS * HEAD_DIM, D_FOURIER, N_BRANCH * D_MODEL)
    offs = [0]
    for s in sizes:
        offs.append(offs[-1] + s)
    return offs

def split_cols(p):
    o = col_offsets()
    return [p[..., o[i]:o[i + 1]] for i in range(len(o) - 1)]

def to_heads(t, n):
    return t.reshape(t.shape[0], t.shape[1], n, HEAD_DIM)

def axial_rope_tables(length):
    rows = length // GRID_W
    row = jnp.repeat(jnp.arange(rows), GRID_W).astype(jnp.float32)
    col = jnp.tile(jnp.arange(GRID_W), rows).astype(jnp.float32)
    nf = HEAD_DIM // 4
    inv = ROPE_BASE ** (-jnp.arange(nf, dtype=jnp.float32) / nf)
    ar = row[:, None] * inv
    ac = col[:, None] * inv
    return jnp.cos(ar), jnp.sin(ar), jnp.cos(ac), jnp.sin(ac)

def rotate(xp, cs, sn):
    nf = HEAD_DIM // 4
    x1, x2 = xp[..., :nf], xp[..., nf:]
    cs, sn = cs[:, None, :], sn[:, None, :]
    return jnp.concatenate([x1 * cs - x2 * sn, x1 * sn + x2 * cs], axis=-1)

def apply_axial_rope(x, cos_r, sin_r, cos_c, sin_c):
    xf = x.astype(jnp.float32)
    half = HEAD_DIM // 2
    y = jnp.concatenate([rotate(xf[..., :half], cos_r, sin_r),
                         rotate(xf[..., half:], cos_c, sin_c)], axis=-1)
    return y.astype(x.dtype)

def latent_window_attention(qx, kx, vx, kc, vc, sink):
    b, s = qx.shape[0], qx.shape[1]
    nb = s // BLOCK
    g = N_Q_HEADS // N_KV_HEADS
    f32 = jnp.float32
    qb = (qx.astype(f32) * HEAD_DIM ** -0.5).reshape(b, nb, BLOCK, N_KV_HEADS, g, HEAD_DIM)
    pad = ((0, 0), (BLOCK, BLOCK), (0, 0), (0, 0))
    kp = jnp.pad(kx.astype(f32), pad).reshape(b, nb + 2, BLOCK, N_KV_HEADS, HEAD_DIM)
    vp = jnp.pad(vx.astype(f32), pad).reshape(b, nb + 2, BLOCK, N_KV_HEADS, HEAD_DIM)
    kband = jnp.concatenate([kp[:, :-2], kp[:, 1:-1], kp[:, 2:]], axis=2)
    vband = jnp.concatenate([vp[:, :-2], vp[:, 1:-1], vp[:, 2:]], axis=2)
    kcf, vcf = kc.astype(f32), vc.astype(f32)
    s_loc = jnp.einsum('bnqkgd,bnjkd->bnkgqj', qb, kband)
    qi = jnp.arange(BLOCK)[:, None]
    kj = jnp.arange(3 * BLOCK)[None, :]
    kpos = jnp.arange(nb)[:, None, None] * BLOCK - BLOCK + kj[None]
    valid = (jnp.abs(kj - BLOCK - qi) <= WINDOW)[None] & (kpos >= 0) & (kpos < s)
    s_loc = jnp.where(valid[None, :, None, None], s_loc, NEG_INF)
    s_ctx = jnp.einsum('bnqkgd,bckd->bnkgqc', qb, kcf)
    sink_b = jnp.broadcast_to(sink.astype(f32).reshape(1, 1, N_KV_HEADS, g, 1, 1),
                              s_loc.shape[:-1] + (1,))
    p = jax.nn.softmax(jnp.concatenate([s_loc, s_ctx, sink_b], axis=-1), axis=-1)
    n_ctx = kc.shape[1]
    p_loc = p[..., :3 * BLOCK]
    p_ctx = p[..., 3 * BLOCK:3 * BLOCK + n_ctx]
    o = (jnp.einsum('bnkgqj,bnjkd->bnqkgd', p_loc, vband)
         + jnp.einsum('bnkgqc,bckd->bnqkgd', p_ctx, vcf))
    return o.reshape(b, s, N_Q_HEADS * HEAD_DIM).astype(qx.dtype)

def context_attention(qc, kc, vc, sink):
    b, n = qc.shape[0], qc.shape[1]
    g = N_Q_HEADS // N_KV_HEADS
    f32 = jnp.float32
    q = (qc.astype(f32) * HEAD_DIM ** -0.5).reshape(b, n, N_KV_HEADS, g, HEAD_DIM)
    sc = jnp.einsum('bqkgd,bckd->bkgqc', q, kc.astype(f32))
    sink_b = jnp.broadcast_to(sink.astype(f32).reshape(1, N_KV_HEADS, g, 1, 1), sc.shape[:-1] + (1,))
    p = jax.nn.softmax(jnp.concatenate([sc, sink_b], axis=-1), axis=-1)[..., :n]
    o = jnp.einsum('bkgqc,bckd->bqkgd', p, vc.astype(f32))
    return o.reshape(b, n, N_Q_HEADS * HEAD_DIM).astype(qc.dtype)

def conformer_conv(u, conv_w, conv_b, ln_g, ln_b, w_out):
    a, gt = u[..., :D_CONV], u[..., D_CONV:]
    h = a * jax.nn.sigmoid(gt)
    h = dwconv(h, conv_w) + conv_b
    h = jax.nn.silu(layer_norm(h, ln_g, ln_b))
    return h @ w_out

def short_gated_conv(u, conv_w, w_out):
    bg, cg, hv = u[..., :D_SHORT], u[..., D_SHORT:2 * D_SHORT], u[..., 2 * D_SHORT:]
    return (bg * dwconv(cg * hv, conv_w)) @ w_out

def fourier_mix(u, w_out):
    b, n = u.shape[0], u.shape[1]
    ug = u.astype(jnp.float32).reshape(b, n, N_FOURIER_GROUPS, D_FOURIER // N_FOURIER_GROUPS)
    f = jnp.fft.fft2(ug, axes=(1, 3), norm='ortho').real
    return f.reshape(b, n, D_FOURIER).astype(u.dtype) @ w_out

def merge_branches(branches, gate_logits, gate_b, w_o):
    b, n = gate_logits.shape[0], gate_logits.shape[1]
    gates = jax.nn.sigmoid((gate_logits + gate_b).reshape(b, n, N_BRANCH, D_MODEL))
    y = gates[:, :, 0] * branches[0]
    for i in range(1, N_BRANCH):
        y = y + gates[:, :, i] * branches[i]
    return y @ w_o

def mixer_sublayer(hx, hc, ctx_out, rope, w_in, gate_b, conv_a_w, conv_a_b, ln_a_g, ln_a_b,
                   w_a_out, conv_b_w, w_b_out, sink, w_c_out, w_d_out, w_o):
    ax, bx, qx, kx, vx, fx, gx = split_cols(hx @ w_in)
    o = col_offsets()
    if ctx_out:
        ac, bc, qc, kc, vc, fc, gc = split_cols(hc @ w_in)
    else:
        kvc = hc @ w_in[:, o[3]:o[5]]
        kc, vc = kvc[..., :N_KV_HEADS * HEAD_DIM], kvc[..., N_KV_HEADS * HEAD_DIM:]
    kc, vc = to_heads(kc, N_KV_HEADS), to_heads(vc, N_KV_HEADS)
    qx = apply_axial_rope(to_heads(qx, N_Q_HEADS), *rope)
    kx = apply_axial_rope(to_heads(kx, N_KV_HEADS), *rope)
    att_x = latent_window_attention(qx, kx, to_heads(vx, N_KV_HEADS), kc, vc, sink)
    yx = merge_branches([conformer_conv(ax, conv_a_w, conv_a_b, ln_a_g, ln_a_b, w_a_out),
                         short_gated_conv(bx, conv_b_w, w_b_out),
                         att_x @ w_c_out,
                         fourier_mix(fx, w_d_out)], gx, gate_b, w_o)
    if not ctx_out:
        return yx, None
    att_c = context_attention(to_heads(qc, N_Q_HEADS), kc, vc, sink)
    yc = merge_branches([conformer_conv(ac, conv_a_w, conv_a_b, ln_a_g, ln_a_b, w_a_out),
                         short_gated_conv(bc, conv_b_w, w_b_out),
                         att_c @ w_c_out,
                         fourier_mix(fc, w_d_out)], gc, gate_b, w_o)
    return yx, yc

def expert_choice_moe(h, router_w, w1, w3, w2):
    b, n, _ = h.shape
    cap = CAPACITY_FACTOR * n // N_EXPERTS
    aff = jax.nn.softmax((h @ router_w).astype(jnp.float32), axis=-1)
    vals, idx = lax.top_k(jnp.swapaxes(aff, 1, 2), cap)
    bidx = jnp.arange(b)[:, None, None]
    xg = h[bidx, idx]
    hid = jax.nn.silu(jnp.einsum('becd,edf->becf', xg, w1)) * jnp.einsum('becd,edf->becf', xg, w3)
    y = jnp.einsum('becf,efd->becd', hid, w2) * vals[..., None].astype(h.dtype)
    return jnp.zeros_like(h).at[bidx, idx].add(y)

def setup_inputs(seed: int = 0) -> dict:
    key = jax.random.key(seed)
    ks = jax.random.split(key, 32)
    f32 = jnp.float32

    def nrm(k, shape, scale):
        return jax.random.normal(k, shape, f32) * scale

    def gain(k, shape):
        return 1.0 + 0.05 * jax.random.normal(k, shape, f32)

    L, D = DEPTH, D_MODEL
    return {
        'x': nrm(ks[0], (BATCH, SEQ, D), 1.0),
        'c': nrm(ks[1], (BATCH, D), 1.0),
        'ctx': nrm(ks[2], (BATCH, CTX_LEN, D), 1.0),
        'c_ctx': nrm(ks[3], (D,), 1.0),
        'ada_w': nrm(ks[4], (L, D, 6 * D), 0.5 * D ** -0.5),
        'ada_b': nrm(ks[5], (L, 6 * D), 0.02),
        'pre_mix_g': gain(ks[6], (L, D)),
        'post_mix_g': gain(ks[7], (L, D)),
        'pre_ffn_g': gain(ks[8], (L, D)),
        'post_ffn_g': gain(ks[9], (L, D)),
        'w_in': nrm(ks[10], (L, D, N_IN), D ** -0.5),
        'gate_b': nrm(ks[11], (L, N_BRANCH * D), 0.1),
        'conv_a_w': nrm(ks[12], (L, CONV_K, D_CONV), CONV_K ** -0.5),
        'conv_a_b': nrm(ks[13], (L, D_CONV), 0.02),
        'ln_a_g': gain(ks[14], (L, D_CONV)),
        'ln_a_b': nrm(ks[15], (L, D_CONV), 0.02),
        'w_a_out': nrm(ks[16], (L, D_CONV, D), D_CONV ** -0.5),
        'conv_b_w': nrm(ks[17], (L, SHORT_K, D_SHORT), SHORT_K ** -0.5),
        'w_b_out': nrm(ks[18], (L, D_SHORT, D), D_SHORT ** -0.5),
        'sink': nrm(ks[19], (L, N_Q_HEADS), 0.5),
        'w_c_out': nrm(ks[20], (L, N_Q_HEADS * HEAD_DIM, D), (N_Q_HEADS * HEAD_DIM) ** -0.5),
        'w_d_out': nrm(ks[21], (L, D_FOURIER, D), D_FOURIER ** -0.5),
        'w_o': nrm(ks[22], (L, D, D), D ** -0.5),
        'router_w': nrm(ks[23], (L, D, N_EXPERTS), D ** -0.5),
        'exp_w1': nrm(ks[24], (L, N_EXPERTS, D, D_EXPERT), D ** -0.5),
        'exp_w3': nrm(ks[25], (L, N_EXPERTS, D, D_EXPERT), D ** -0.5),
        'exp_w2': nrm(ks[26], (L, N_EXPERTS, D_EXPERT, D), D_EXPERT ** -0.5),
    }

def reference(x, c, ctx, c_ctx, ada_w, ada_b, pre_mix_g, post_mix_g, pre_ffn_g, post_ffn_g,
              w_in, gate_b, conv_a_w, conv_a_b, ln_a_g, ln_a_b, w_a_out, conv_b_w, w_b_out,
              sink, w_c_out, w_d_out, w_o, router_w, exp_w1, exp_w3, exp_w2):
    rope = axial_rope_tables(x.shape[1])
    xs, cs = x, ctx
    for l in range(DEPTH):
        last = l == DEPTH - 1
        mx = jnp.split((jax.nn.silu(c) @ ada_w[l] + ada_b[l])[:, None, :], 6, axis=-1)
        mc = jnp.split((jax.nn.silu(c_ctx) @ ada_w[l] + ada_b[l])[None, None, :], 6, axis=-1)
        hx = modulate(rms_norm(xs, pre_mix_g[l]), mx[0], mx[1])
        hc = modulate(rms_norm(cs, pre_mix_g[l]), mc[0], mc[1])
        yx, yc = mixer_sublayer(hx, hc, not last, rope, w_in[l], gate_b[l], conv_a_w[l], conv_a_b[l],
                                ln_a_g[l], ln_a_b[l], w_a_out[l], conv_b_w[l], w_b_out[l], sink[l],
                                w_c_out[l], w_d_out[l], w_o[l])
        xs = xs + mx[2] * rms_norm(yx, post_mix_g[l])
        hx = modulate(rms_norm(xs, pre_ffn_g[l]), mx[3], mx[4])
        xs = xs + mx[5] * rms_norm(expert_choice_moe(hx, router_w[l], exp_w1[l], exp_w3[l], exp_w2[l]),
                                   post_ffn_g[l])
        if not last:
            cs = cs + mc[2] * rms_norm(yc, post_mix_g[l])
            hc = modulate(rms_norm(cs, pre_ffn_g[l]), mc[3], mc[4])
            cs = cs + mc[5] * rms_norm(expert_choice_moe(hc, router_w[l], exp_w1[l], exp_w3[l], exp_w2[l]),
                                       post_ffn_g[l])
    return xs


_drawn_inputs = setup_inputs


def setup_inputs(seed=0):
    import zlib

    import numpy as np

    out = dict(_drawn_inputs(seed))
    spreads = {}
    factors = {'ln_a_b': 3.218, 'sink': 21.671, 'conv_a_b': 3.043}
    for name, (base, spread) in spreads.items():
        noise = np.random.default_rng([zlib.crc32(name.encode()), seed]).standard_normal(out[name].shape)
        drawn = base * np.exp(spread * noise) if base else spread * noise
        out[name] = __import__('jax').numpy.asarray(drawn.astype(out[name].dtype))
    for name, factor in factors.items():
        out[name] = (out[name] * factor).astype(out[name].dtype)
    return out
```

```python
from contextlib import ExitStack

import numpy as np

import concourse.bass as bass
from concourse import mybir
from concourse.alu_op_type import AluOpType as ALU

F32 = mybir.dt.float32
ACT = mybir.ActivationFunctionType
AX = mybir.AxisListType

P = 128
D = 1024
KT = D // P
SEQ, CTX = 512, 256
TOK = SEQ + CTX
DEPTH = 2
LAT, CON = (0, 0, SEQ), (1, SEQ, CTX)
DC = 512
CT = DC // P
CONV_K, SHORT_K = 31, 3
HC, HS = CONV_K // 2, SHORT_K // 2
HEADS, KVH, HD = 8, 2, 64
GRP = HEADS // KVH
GRID_W = 64
NE = 16
CAP = (2 * SEQ // NE, 2 * CTX // NE)
FX = 1024
EPS = 1e-6
NB = SEQ // P
LT, CTT = SEQ // P, CTX // P
TT = LT + CTT
O_A, O_B, O_Q, O_K, O_V, O_F, O_G = 0, 1024, 2560, 3072, 3200, 3328, 3840
WCHUNKS = [(0, 512), (512, 512), (1024, 512), (1536, 512), (2048, 512), (2560, 512), (3072, 256), (3328, 512)]
C_AV, C_AG, C_BG, C_CG, C_HV, C_Q, C_KV, C_F = range(8)
BANKS = 8
SLOT = 4096
PADC = SEQ + 2 * HC, CTX + 2 * HC
PADS = SEQ + 2 * HS, CTX + 2 * HS
R_ADAB, R_PM, R_QM, R_PF, R_QF, R_GB, R_CB, R_LG, R_LB = 0, 48, 56, 64, 72, 80, 112, 116, 120
NR1, NR2, NR3 = 124, CONV_K * CT, SHORT_K * CT
NPAR = NR1 + NR2 + NR3
PRE_MIX, POST_MIX, PRE_FFN, POST_FFN = range(4)


def parts_of(l, norm=POST_MIX):
    return (LAT, CON) if l == 0 or norm == PRE_MIX else (LAT,)


def att_units(l):
    units = [(0, n, g) for n in range(NB) for g in range(KVH)]
    return units + ([(1, n, g) for n in range(CTT) for g in range(KVH)] if l == 0 else [])


def band(unit):
    con, n, _ = unit
    lo, hi = (0, 0) if con else (max(n - 1, 0), min(n + 2, NB))
    return lo, hi, hi - lo + CTT


def plan_jobs():
    jobs, n = {}, 0

    def add(*key):
        nonlocal n
        jobs[key] = n
        n += 1

    for i in range(TT):
        for h in range(2):
            add("xin", i, h)
    for l in range(DEPTH):
        for r in range(3):
            add("par", l, r)
    add("cin", 0)
    for l in range(DEPTH):
        both = parts_of(l)
        for c in range(12):
            add("mod", l, c)
        for part in (LAT, CON):
            add("ms", l, PRE_MIX, part[0])
        for c in range(C_KV):
            for t in range(CT):
                for part in both:
                    add("win", l, c, t, part[0])
                if c == C_Q:
                    add("rope", l, t)
        for part in (LAT, CON):
            add("k", l, part[0])
        add("rope", l, CT)
        for part in (LAT, CON):
            add("v", l, part[0])
        for i in range(TT if l == 0 else LT):
            add("f", l, i)
        for g in range(CT):
            for part in both:
                add("fc", l, g, part[0])
                add("fs", l, g, part[0])
            if g:
                for part in both:
                    add("fo", l, g - 1, part[0])
        for part in both:
            add("fo", l, CT - 1, part[0])
        units = att_units(l)

        def scores(u):
            for h in range(GRP):
                if not units[u][0]:
                    add("sl", l, u, h)
                add("sc", l, u, h)

        scores(0)
        for u in range(len(units)):
            if u + 1 < len(units):
                scores(u + 1)
            for kt in range(band(units[u])[2]):
                add("pt", l, u, kt)
            add("av", l, u)
        for part in both:
            add("lm", l, part[0])
        for part in both:
            add("lv", l, part[0])
        for dp in range(KT // 2):
            for b in range(4):
                for t in range(2):
                    for part in both:
                        add("g", l, dp, b, t, part[0])
                        add("w", l, dp, b, t, part[0])
        for t in range(KT):
            for part in both:
                add("wo", l, t, part[0])
        for norm in (POST_MIX, PRE_FFN):
            for part in both:
                add("ms", l, norm, part[0])
        add("rl", l)
        add("at", l, 0)
        if l == 0:
            add("at", l, 1)
        for i in range(TT if l == 0 else LT):
            for h in range(2):
                add("ht", l, i, h)
        add("pos", l)
        for k in range(KT):
            add("ga", l, k, 0)
            add("ga", l, k, 1)
            if l == 0:
                add("ga", l, k, 2)
        for e in range(NE):
            for h in range(2):
                add("h1", l, e, h)
                add("h3", l, e, h)
            add("y", l, e, 0)
            add("y", l, e, 1)
        for p in range(NE // 2):
            add("sg", l, p, 0)
        if l == 0:
            for p in range(NE // 4):
                add("sg", l, p, 1)
        for k in range(KT):
            for part in both:
                add("mo", l, k, part[0])
        for part in both:
            add("ms", l, POST_FFN, part[0])
    for i in range(LT):
        for h in range(2):
            add("out", i, h)
    return jobs


def plan_chunks():
    chunks, held, last_in = {}, [0] * 4, [None] * 4

    def add(key, slot, last_job, loads=1):
        held[slot] += loads
        chunks[key] = (slot, held[slot], last_job, last_in[slot])
        last_in[slot] = key

    for l in range(DEPTH):
        last = parts_of(l)[-1][0]
        for c in range(12):
            add(("ada", l, c), c % 2, ("mod", l, c))
        for c in range(C_KV):
            add(("win", l, c), c % 2, ("rope", l, CT - 1) if c == C_Q else ("win", l, c, CT - 1, last))
        add(("win", l, C_KV), 0, ("v", l, 1))
        add(("win", l, C_F), 1, ("f", l, (TT if l == 0 else LT) - 1))
        for dp in range(KT // 2):
            for b in range(4):
                add(("mg", l, dp, b), b % 2, ("w", l, dp, b, 1, last), loads=2)
        for h in range(2):
            add(("wo", l, h), h, ("wo", l, 4 * h + 3, last))
        for e in range(NE):
            for m, (job, h) in enumerate((("h1", 0), ("h3", 0), ("h1", 1), ("h3", 1), ("y", 0), ("y", 1))):
                add(("ex", l, e, m), (6 * e + m) % 4, (job, l, e, h))
    return chunks


def build(nc, A, K, out):
    jobs, chunks = plan_jobs(), plan_chunks()
    ctx = ExitStack()
    with ctx:
        def sb(name, n, rows=P):
            return ctx.enter_context(nc.sbuf_tensor(name, [rows, n], F32))

        def sem(name):
            return ctx.enter_context(nc.semaphore(name))

        x_t = sb("x_t", KT * TOK)[:, :].rearrange("p (k t) -> p k t", k=KT)
        hb = sb("hb", 2 * KT * TOK)
        h_t = hb[:, 0:KT * TOK].rearrange("p (k t) -> p k t", k=KT)
        hb2 = hb[:, KT * TOK:2 * KT * TOK]
        y_t = hb2.rearrange("p (k t) -> p k t", k=KT)
        h_tok = hb2.rearrange("p (i d) -> p i d", i=TT)
        yo_t = h_t
        S_buf = [hb2[:, b * 2560:(b + 1) * 2560].rearrange("p (h k) -> p h k", h=GRP) for b in range(2)]
        c512 = hb2[:, 0:2048].rearrange("p (i n) -> p i n", i=LT)
        s512 = hb2[:, 2048:4096].rearrange("p (i n) -> p i n", i=LT)
        c256 = hb2[:, 4096:4608].rearrange("p (i n) -> p i n", i=CTT)
        s256 = hb2[:, 4608:5120].rearrange("p (i n) -> p i n", i=CTT)
        c128 = hb2[:, 5120:5248]
        s128 = hb2[:, 5248:5376]
        ring0 = sb("ring0", 2 * SLOT)
        slots = [ring0[:, 0:SLOT], ring0[:, SLOT:2 * SLOT], hb[:, 0:SLOT], hb[:, SLOT:2 * SLOT]]
        AR = 20992
        arena = sb("arena", AR)
        at = [0]

        def take(n):
            at[0] += n
            return arena[:, at[0] - n:at[0]]

        cpad = take(CT * sum(PADC)).rearrange("p (t n) -> p t n", t=CT)
        a_t = take(CT * TOK).rearrange("p (t n) -> p t n", t=CT)
        b_t = take(CT * TOK).rearrange("p (t n) -> p t n", t=CT)
        q_t = take(CT * TOK).rearrange("p (t n) -> p t n", t=CT)
        k_t = take(2 * TOK).rearrange("p (s n) -> p s n", s=2)
        v_tok = take(TOK).rearrange("p (i n) -> p i n", i=TT)
        f_tok = take(CT * TOK).rearrange("p (i n) -> p i n", i=TT)
        shared = take(CT * sum(PADS))
        bpad = shared.rearrange("p (t n) -> p t n", t=CT)
        xc = [shared[:, b * 1536:b * 1536 + TOK] for b in range(2)]
        xs = [shared[:, b * 1536 + TOK:b * 1536 + 2 * TOK] for b in range(2)]
        probs_t = shared[:, 0:2560].rearrange("p (k n) -> p k n", k=5)
        assert at[0] == AR
        xgy = arena[:, 0:15360]
        sel_e = arena[:, 0:4 * TOK].rearrange("p (w t) -> p w t", w=4)
        onehot = [arena[:, 15360:19456].rearrange("p (i s) -> p i s", i=LT),
                  arena[:, 19456:20480].rearrange("p (i s) -> p i s", i=CTT)]
        sg = [hb[:, 0:4096].rearrange("p (g t) -> p g t", g=NE // 2),
              hb[:, 4096:5120].rearrange("p (g t) -> p g t", g=NE // 4)]
        rb = sb("rb", TOK)[:, :]
        two = sb("two", 2 * TOK)
        sq = [two[:, 0:TOK], two[:, TOK:2 * TOK]]
        silu_t = [rb[:, 0:384], rb[:, 384:768]]
        hid = [sq[b].rearrange("p (f s) -> p f s", f=KT) for b in range(2)]
        ident = sb("ident", P)[:, :]
        ones_d = sb("ones_d", P)[:, :]
        ones_c = sb("ones_c", P)[:, :]
        perm = sb("perm", P)[:, :]
        cosT = sb("cosT", SEQ)[:, :]
        sinT = sb("sinT", SEQ)[:, :]
        maskT = sb("maskT", 3 * P)[:, :]
        iota = sb("iota", CAP[0])[:, :]
        eps_t = sb("eps_t", 1)[:, :]
        par = [sb(f"par{l}", NPAR)[:, :] for l in range(DEPTH)]
        nsink = sb("nsink", DEPTH * HEADS)[:, :]
        c_t = sb("c_t", 2 * KT)[:, :]
        mods = sb("mods", 96)[:, :].rearrange("p (c w) -> p c w", w=2)
        scl = sb("scl", 4 * KT * 2)[:, :].rearrange("p (m c w) -> p m c w", m=4, w=2)
        rw = sb("rw", KT * NE)[:, :].rearrange("p (k e) -> p k e", k=KT)
        st = sb("st", 64)[:, :].rearrange("p (w h) -> p w h", h=4)
        aff = sb("aff", TT * NE)[:, :].rearrange("p (i e) -> p i e", e=NE)
        rs = sb("rs", 2 * TT)[:, :].rearrange("p (w i) -> p w i", w=2)
        pos_t = sb("pos_t", TT * NE)[:, :].rearrange("p (i e) -> p i e", e=NE)
        top8 = sb("top8", 16)[:, :]
        x_tok = hb[:, 0:TT * D].rearrange("p (i d) -> p i d", i=TT)
        par_rows = hb2[:, 0:7 * P].rearrange("p (r n) -> p r n", n=P)

        ps = [ctx.enter_context(nc.psum_tensor(f"ps{b}", [P, 512], F32)) for b in range(BANKS)]

        full = [sem(f"full{b}") for b in range(BANKS)]
        drained = [sem(f"drained{b}") for b in range(BANKS)]
        loaded = [sem(f"loaded{s}") for s in range(4)]
        x_loaded, par_loaded, const_loaded = sem("x_loaded"), sem("par_loaded"), sem("const_loaded")
        dft_loaded = sem("dft_loaded")
        rw_loaded = sem("rw_loaded")
        set_up = sem("set_up")
        c_ready = sem("c_ready")
        mods_ready = sem("mods_ready")
        sq_ready, sq_used = sem("sq_ready"), sem("sq_used")
        xr_ready, h_ready = sem("xr_ready"), sem("h_ready")
        x_updated = sem("x_updated")
        glu_done = sem("glu_done")
        rope_done = sem("rope_done")
        swapped = sem("swapped")
        short_done = sem("short_done")
        stats_done = sem("stats_done")
        exps_done = sem("exps_done")
        probs_done = sem("probs_done")
        conv_done = sem("conv_done")
        centred = sem("centred")
        lnorm_done = sem("lnorm_done")
        a_done = sem("a_done")
        merged = sem("merged")
        aff_exp, aff_done, pos_done, onehot_done, og_done = (sem(n) for n in (
            "aff_exp", "aff_done", "pos_done", "onehot_done", "og_done"))
        dve_step, act_step = sem("dve_step"), sem("act_step")
        out_stored = sem("out_stored")
        conv_zero = sem("conv_zero")

        def bank(*key):
            return ps[jobs[key] % BANKS]

        def full_of(eng, *key, turn=0):
            eng.wait_ge(full[jobs[key] % BANKS], jobs[key] // BANKS + 1 + 3 * turn)

        def drained_of(eng, *key, turn=0):
            eng.wait_ge(drained[jobs[key] % BANKS], jobs[key] // BANKS + 1 + 3 * turn)

        def free_for(eng, *key, turn=0):
            if jobs[key] >= BANKS:
                eng.wait_ge(drained[jobs[key] % BANKS], jobs[key] // BANKS + 3 * turn)

        def is_full(*key):
            return full[jobs[key] % BANKS]

        def is_drained(*key):
            return drained[jobs[key] % BANKS]

        def chunk_here(eng, *key, turn=0):
            slot, loads, _, _ = chunks[key]
            eng.wait_ge(loaded[slot], 16 * loads + 96 * turn)
            return slots[slot]

        def norm_index(l, norm):
            return 4 * l + norm

        def kmaj(ap, n):
            return ap.rearrange("(k p) n -> p k n", p=P)

        def vec_rows(ap, n=P):
            return ap.rearrange("(r n) -> r n", n=n)

        def SQ0(l, norm):
            return 36 * l + (0, 12, 20, 28)[norm]

        def SQU(l, norm):
            return 31 * l + (0, 10, 17, 24)[norm]

        SQLN, SQLNU = (8, 44), (7, 38)
        PROBS0 = (0, len(att_units(0)))
        ONEHOT, POS, CONV = (TT, TT + LT), (2, 3), (2 * CT, 3 * CT)

        def GLU(l, t, part):
            return 2 * t + part if l == 0 else 2 * CT + t

        def gather_out(eng, l, k, m, ns, copy):
            dst = xgy[:, 4 * KT * ns:(4 + NE) * KT * ns].rearrange("p (e k s) -> p e k s", k=KT, s=ns)
            full_of(eng, "ga", l, k, m)
            if m < 2:
                dst, cap = dst[:, 8 * m:8 * m + 8, k, 0:CAP[0]], CAP[0]
            else:
                dst, cap = dst[:, :, k, CAP[0]:ns], CAP[1]
            copy(dst, bank("ga", l, k, m)[:, :].rearrange("p (e s) -> p e s", s=cap)) \
                .then_inc(is_drained("ga", l, k, m), 1)

        def y_out(eng, l, e, h, turn, copy):
            ns = sum(CAP) if l == 0 else CAP[0]
            full_of(eng, "y", l, e, h, turn=turn)
            col = turn * (4 * KT * ns) + (e // 2 * D + h * 512)
            r = CAP[0] * (e % 2)
            op = copy(xgy[r:r + CAP[0], bass.ds(col, 512)], bank("y", l, e, h)[0:CAP[0], :])
            if l == 0:
                col = turn * (4 * KT * ns) + (2 * D + h * 512)
                op = copy(xgy[CAP[1] * e:CAP[1] * (e + 1), bass.ds(col, 512)], bank("y", l, e, h)[CAP[0]:ns, :])
            op.then_inc(is_drained("y", l, e, h), 1)

        def y_rows(l, part, p):
            ns = sum(CAP) if l == 0 else CAP[0]
            first = p // 2 * 4 * KT * ns + p % 2 * D if part == 0 else p * 4 * KT * ns + 2 * D
            return xgy[:, first:first + D]

        block = ctx.enter_context(nc.Block())

        @block.sync
        def _(sp):
            def slot_free(key, turn=0):
                prev = chunks[key][3]
                if prev is not None:
                    full_of(sp, *chunks[prev][2], turn=turn)

            def load(key, dst, src):
                slot_free(key)
                sp.dma_start(dst, src).then_inc(loaded[chunks[key][0]], 16)

            def slot_view(key, k, n, at=0):
                return slots[chunks[key][0]][:, at:at + k * n].rearrange("p (k n) -> p k n", k=k)

            def expert_src(l, e, m):
                w = A["exp_w1"] if m in (0, 2) else A["exp_w3"] if m in (1, 3) else A["exp_w2"]
                h = m // 2 if m < 4 else m - 4
                return w[l].rearrange("e (k p) n -> e p k n", p=P)[e, :, :, h * 512:(h + 1) * 512]

            for i in range(TT):
                src = A["x"][0, i * P:(i + 1) * P, :] if i < LT else A["ctx"][0, (i - LT) * P:(i - LT + 1) * P, :]
                sp.dma_start(x_tok[:, i, :], src).then_inc(x_loaded, 16)
            for l in range(DEPTH):
                for c in range(12):
                    key = ("ada", l, c)
                    load(key, slot_view(key, KT, 512), kmaj(A["ada_w"][l][:, c * 512:(c + 1) * 512], 512))
                if l == 0:
                    drained_of(sp, "cin", 0)
                    drained_of(sp, "par", 1, 2)
                else:
                    sp.wait_ge(x_updated, 8 * 2 * l)
                sp.dma_start(hb2[:, 0:5376], K["dft"]).then_inc(dft_loaded, 16)
                for c, (lo, n) in enumerate(WCHUNKS):
                    key = ("win", l, c)
                    load(key, slot_view(key, KT, n), kmaj(A["w_in"][l][:, lo:lo + n], n))
                for dp in range(KT // 2):
                    for b in range(4):
                        key = ("mg", l, dp, b)
                        slot_free(key)
                        lo = O_G + b * D + dp * 256
                        sp.dma_start(slot_view(key, KT, 256), kmaj(A["w_in"][l][:, lo:lo + 256], 256)) \
                            .then_inc(loaded[chunks[key][0]], 16)
                        w = A[("w_a_out", "w_b_out", "w_c_out", "w_d_out")[b]]
                        sp.dma_start(slot_view(key, CT, 256, 2048), kmaj(w[l][:, dp * 256:dp * 256 + 256], 256)) \
                            .then_inc(loaded[chunks[key][0]], 16)
                for h in range(2):
                    key = ("wo", l, h)
                    load(key, slot_view(key, KT, 512), kmaj(A["w_o"][l][:, h * 512:(h + 1) * 512], 512))
                for m in range(4):
                    key = ("ex", l, 0, m)
                    if m >= 2:
                        full_of(sp, "ga", l, KT - 1, 2 if l == 0 else 1)
                        sp.dma_start(slot_view(key, KT, 512), expert_src(l, 0, m)).then_inc(loaded[m], 16)
                    else:
                        load(key, slot_view(key, KT, 512), expert_src(l, 0, m))

                def expert_loads(turn, chunks_in_turn):
                    for c in range(chunks_in_turn):
                        e, m = divmod(c, 6)
                        nxt = divmod(c + 4, 6)
                        full_of(sp, *chunks["ex", l, e, m][2], turn=turn)
                        sp.dma_start(slot_view(("ex", l, e, m), KT, 512),
                                     expert_src(l, 4 * turn + nxt[0], nxt[1])).then_inc(loaded[c % 4], 16)

                with sp.Fori(0, NE // 4 - 1) as turn:
                    expert_loads(turn, 24)
                expert_loads(NE // 4 - 1, 20)
            for i in range(LT):
                drained_of(sp, "out", i, 0)
                drained_of(sp, "out", i, 1)
                sp.dma_start(out[0, i * P:(i + 1) * P, :], h_tok[:, i, :]).then_inc(out_stored, 16)
            sp.wait_ge(out_stored, 16 * LT)

        @block.gpsimd
        def _(pool):
            for dst, src in ((ident, "ident"), (ones_d, "ones_d"), (ones_c, "ones_c"), (perm, "perm"),
                             (cosT, "cos"), (sinT, "sin"), (maskT, "mask"), (iota, "iota")):
                pool.dma_start(dst, K[src]).then_inc(const_loaded, 16)
            for l in range(DEPTH):
                r = 3 * l
                for row, name, n in ((R_ADAB, "ada_b", 48), (R_PM, "pre_mix_g", 8), (R_QM, "post_mix_g", 8),
                                     (R_PF, "pre_ffn_g", 8), (R_QF, "post_ffn_g", 8), (R_GB, "gate_b", 32),
                                     (R_CB, "conv_a_b", 4), (R_LG, "ln_a_g", 4), (R_LB, "ln_a_b", 4)):
                    pool.dma_start(par_rows[row:row + n, r, :], vec_rows(A[name][l])).then_inc(par_loaded, 16)
                pool.dma_start(par_rows[0:NR2, r + 1, :],
                               A["conv_a_w"][l].rearrange("k (t n) -> (k t) n", n=P)).then_inc(par_loaded, 16)
                pool.dma_start(par_rows[0:NR3, r + 2, :],
                               A["conv_b_w"][l].rearrange("k (t n) -> (k t) n", n=P)).then_inc(par_loaded, 16)
            pool.dma_start(par_rows[0:KT, 6, :], vec_rows(A["c"][0])).then_inc(par_loaded, 16)
            pool.dma_start(par_rows[KT:2 * KT, 6, :], vec_rows(A["c_ctx"])).then_inc(par_loaded, 16)
            pool.dma_start(nsink, A["sink"].rearrange("(a l) h -> a (l h)", a=1).broadcast_to([P, DEPTH * HEADS])).then_inc(par_loaded, 16)
            pool.memset(eps_t, EPS).then_inc(set_up, 1)
            for l in range(DEPTH):
                if l:
                    full_of(pool, "rl", l - 1)
                pool.dma_start(rw, kmaj(A["router_w"][l], NE)).then_inc(rw_loaded, 16)

        @block.tensor
        def _(pe):
            def chan_sum(l, norm, job, weights, tiles, parts, ready):
                for part in parts:
                    free_for(pe, job, *norm, part[0])
                for k in range(tiles):
                    ready(k)
                    for part in parts:
                        mm = pe.matmul(bank(job, *norm, part[0])[:, 0:part[2]], weights,
                                       sq[k % 2][:, part[1]:part[1] + part[2]], start=(k == 0), stop=(k == tiles - 1))
                        if k == tiles - 1:
                            mm.then_inc(is_full(job, *norm, part[0]), 1)
                    if k < tiles - 1:
                        mm.then_inc(sq_used, 1)

            def mean_square(l, norm):
                ni = norm_index(l, norm)
                chan_sum(l, (l, norm), "ms", ones_d, KT, parts_of(l, norm),
                         lambda k: pe.wait_ge(sq_ready, SQ0(l, norm) + k + 1))

            def product(key, wt, k_tiles, rhs, n, first=True):
                free_for(pe, *key)
                for k in range(k_tiles):
                    mm = pe.matmul(bank(*key)[:, 0:n], wt(k), rhs(k), start=(k == 0), stop=(k == k_tiles - 1))
                mm.then_inc(is_full(*key), 1)

            pe.wait_ge(const_loaded, 16 * 8)
            pe.wait_ge(x_loaded, 16 * TT)
            for i in range(TT):
                for h in range(2):
                    free_for(pe, "xin", i, h)
                    for k in range(4):
                        mm = pe.transpose(bank("xin", i, h)[:, k * P:(k + 1) * P],
                                          x_tok[:, i, (4 * h + k) * P:(4 * h + k + 1) * P], ident)
                    mm.then_inc(is_full("xin", i, h), 1)
            pe.wait_ge(par_loaded, 16 * 25)
            for l in range(DEPTH):
                for r, n in enumerate((NR1, NR2, NR3)):
                    free_for(pe, "par", l, r)
                    pe.transpose(bank("par", l, r)[:, 0:n], par_rows[0:n, 3 * l + r, :], ident[0:n, 0:n]) \
                        .then_inc(is_full("par", l, r), 1)
            free_for(pe, "cin", 0)
            pe.transpose(bank("cin", 0)[:, 0:2 * KT], par_rows[0:2 * KT, 6, :], ident[0:2 * KT, 0:2 * KT]) \
                .then_inc(is_full("cin", 0), 1)
            drained_of(pe, "cin", 0)

            def layer(l):
                both = parts_of(l)
                for c in range(12):
                    w = chunk_here(pe, "ada", l, c).rearrange("p (k n) -> p k n", k=KT)
                    free_for(pe, "mod", l, c)
                    for t in range(4):
                        for k in range(KT):
                            mm = pe.matmul(bank("mod", l, c)[:, 2 * t:2 * t + 2], w[:, k, t * P:(t + 1) * P],
                                           c_t[:, 2 * k:2 * k + 2], start=(k == 0), stop=(k == KT - 1))
                    mm.then_inc(is_full("mod", l, c), 1)
                mean_square(l, PRE_MIX)
                for c in range(C_KV):
                    w = chunk_here(pe, "win", l, c).rearrange("p (k n) -> p k n", k=KT)
                    if c == 0:
                        pe.wait_ge(h_ready, 8 * (2 * l + 1))
                    for t in range(CT):
                        for part in both:
                            product(("win", l, c, t, part[0]), lambda k: w[:, k, t * P:(t + 1) * P], KT,
                                    lambda k: h_t[:, k, part[1]:part[1] + part[2]], part[2])
                        if c == C_Q:
                            drained_of(pe, "win", l, c, t, 0)
                            product(("rope", l, t), lambda k: perm, 1, lambda k: q_t[:, t, 0:SEQ], SEQ)
                w = chunk_here(pe, "win", l, C_KV)[:, 0:KT * 256].rearrange("p (k n) -> p k n", k=KT)
                for part in (LAT, CON):
                    product(("k", l, part[0]), lambda k: w[:, k, 0:P], KT,
                            lambda k: h_t[:, k, part[1]:part[1] + part[2]], part[2])
                drained_of(pe, "k", l, 0)
                product(("rope", l, CT), lambda k: perm, 1, lambda k: k_t[:, 0, 0:SEQ], SEQ)
                for part, first, n in ((0, 0, LT), (1, LT, CTT)):
                    free_for(pe, "v", l, part)
                    for i in range(n):
                        for k in range(KT):
                            mm = pe.matmul(bank("v", l, part)[:, i * P:(i + 1) * P],
                                           h_t[:, k, (first + i) * P:(first + i + 1) * P], w[:, k, P:2 * P],
                                           start=(k == 0), stop=(k == KT - 1))
                    mm.then_inc(is_full("v", l, part), 1)
                w = chunk_here(pe, "win", l, C_F).rearrange("p (k n) -> p k n", k=KT)
                for i in range(TT if l == 0 else LT):
                    product(("f", l, i), lambda k: h_t[:, k, i * P:(i + 1) * P], KT, lambda k: w[:, k, :], DC)
                pe.wait_ge(dft_loaded, 16 * (l + 1))

                def fourier_out(g):
                    for part in both:
                        drained_of(pe, "fc", l, g, part[0])
                        drained_of(pe, "fs", l, g, part[0])
                        key = ("fo", l, g, part[0])
                        free_for(pe, *key)
                        cols = slice(part[1], part[1] + part[2])
                        pe.matmul(bank(*key)[:, 0:part[2]], c128, xc[g % 2][:, cols], start=True, stop=False)
                        pe.matmul(bank(*key)[:, 0:part[2]], s128, xs[g % 2][:, cols], start=False, stop=True) \
                            .then_inc(is_full(*key), 1)

                drained_of(pe, "f", l, (TT if l == 0 else LT) - 1)
                drained_of(pe, "f", l, (TT if l == 0 else LT) - 2)
                for g in range(CT):
                    for part in both:
                        first, n = (0, LT) if part[0] == 0 else (LT, CTT)
                        tabs = (c512, s512) if part[0] == 0 else (c256, s256)
                        for name, tab in zip(("fc", "fs"), tabs):
                            product((name, l, g, part[0]), lambda k: f_tok[:, first + k, g * P:(g + 1) * P], n,
                                    lambda k: tab[:, k, :], part[2])
                    if g:
                        fourier_out(g - 1)
                fourier_out(CT - 1)
                units = att_units(l)
                pe.wait_ge(rope_done, 5 * (l + 1))
                pe.wait_ge(swapped, 2 * (l + 1))
                for t in range(CT):
                    if l == 0:
                        drained_of(pe, "win", l, C_Q, t, 1)
                drained_of(pe, "v", l, 0)
                drained_of(pe, "v", l, 1)

                def scores(u):
                    con, n, g = units[u]
                    lo, hi, _ = band(units[u])
                    col = SEQ * con + n * P
                    for h in range(GRP):
                        head = GRP * g + h
                        r = HD * (head % 2)
                        keys = k_t[r:r + HD, 0 if head % 2 == g else 1, :]
                        q = q_t[r:r + HD, head // 2, col:col + P]
                        if not con:
                            key = ("sl", l, u, h)
                            free_for(pe, *key)
                            pe.matmul(bank(*key)[:, 0:(hi - lo) * P], q, keys[:, lo * P:hi * P],
                                      start=True, stop=True).then_inc(is_full(*key), 1)
                        key = ("sc", l, u, h)
                        free_for(pe, *key)
                        pe.matmul(bank(*key)[:, 0:CTX], q, keys[:, SEQ:TOK],
                                  start=True, stop=True).then_inc(is_full(*key), 1)

                def values(u):
                    con, n, g = units[u]
                    lo, hi, nk = band(units[u])
                    tiles = list(range(lo, hi)) + list(range(LT, TT))
                    for kt in range(nk):
                        free_for(pe, "pt", l, u, kt)
                        if kt == 0:
                            pe.wait_ge(probs_done, PROBS0[l] + u + 1)
                        for h in range(GRP):
                            mm = pe.transpose(bank("pt", l, u, kt)[:, h * P:(h + 1) * P],
                                              S_buf[u % 2][:, h, kt * P:(kt + 1) * P], ident)
                        mm.then_inc(is_full("pt", l, u, kt), 1)
                    free_for(pe, "av", l, u)
                    for kt in range(nk):
                        drained_of(pe, "pt", l, u, kt)
                        mm = pe.matmul(bank("av", l, u)[0:HD, :], v_tok[:, tiles[kt], g * HD:(g + 1) * HD],
                                       probs_t[:, kt, :], start=(kt == 0), stop=(kt == nk - 1))
                    mm.then_inc(is_full("av", l, u), 1)

                scores(0)
                for u in range(len(units)):
                    if u + 1 < len(units):
                        scores(u + 1)
                    values(u)
                pe.wait_ge(conv_done, CONV[l])
                for part in both:
                    product(("lm", l, part[0]), lambda k: ones_c, CT,
                            lambda k: a_t[:, k, part[1]:part[1] + part[2]], part[2])
                chan_sum(l, (l,), "lv", ones_c, CT, both, lambda k: pe.wait_ge(sq_ready, SQLN[l] + k + 1))
                srcs = (a_t, b_t, q_t, None)
                for dp in range(KT // 2):
                    for b in range(4):
                        w = chunk_here(pe, "mg", l, dp, b)
                        wg = w[:, 0:2048].rearrange("p (k n) -> p k n", k=KT)
                        wb = w[:, 2048:3072].rearrange("p (k n) -> p k n", k=CT)
                        if dp == 0 and b == 0:
                            pe.wait_ge(a_done, 4 * (l + 1))
                            pe.wait_ge(short_done, 4 * (l + 1))
                            for u in range(len(units) - 2, len(units)):
                                drained_of(pe, "av", l, u)
                            for part in both:
                                drained_of(pe, "fo", l, CT - 1, part[0])
                        for t in range(2):
                            for part in both:
                                cols = slice(part[1], part[1] + part[2])
                                product(("g", l, dp, b, t, part[0]), lambda k: wg[:, k, t * P:(t + 1) * P], KT,
                                        lambda k: h_t[:, k, cols], part[2])
                                if b < 3:
                                    rhs = lambda k: srcs[b][:, k, cols]
                                else:
                                    i0, i1 = (0, LT) if part[0] == 0 else (LT, TT)
                                    rhs = lambda k: f_tok[:, i0:i1, k * P:(k + 1) * P]
                                product(("w", l, dp, b, t, part[0]), lambda k: wb[:, k, t * P:(t + 1) * P], CT,
                                        rhs, part[2])
                pe.wait_ge(merged, (l + 1) * 8)
                for h in range(2):
                    w = chunk_here(pe, "wo", l, h).rearrange("p (k n) -> p k n", k=KT)
                    for t in range(4):
                        for part in both:
                            product(("wo", l, 4 * h + t, part[0]), lambda k: w[:, k, t * P:(t + 1) * P], KT,
                                    lambda k: y_t[:, k, part[1]:part[1] + part[2]], part[2])
                mean_square(l, POST_MIX)
                mean_square(l, PRE_FFN)
                nt = TT if l == 0 else LT
                pe.wait_ge(h_ready, 8 * (2 * l + 2))
                pe.wait_ge(rw_loaded, 16 * (l + 1))
                free_for(pe, "rl", l)
                for i in range(nt):
                    for k in range(KT):
                        mm = pe.matmul(bank("rl", l)[:, i * NE:(i + 1) * NE], h_t[:, k, i * P:(i + 1) * P],
                                       rw[:, k, :], start=(k == 0), stop=(k == KT - 1))
                mm.then_inc(is_full("rl", l), 1)
                for key, lo, hi in ((("at", l, 0), 0, LT), (("at", l, 1), LT, TT)):
                    if key in jobs:
                        free_for(pe, *key)
                        pe.wait_ge(aff_done, l + 1)
                        for i in range(lo, hi):
                            mm = pe.transpose(bank(*key)[0:NE, (i - lo) * P:(i - lo + 1) * P], aff[:, i, :], ident)
                        mm.then_inc(is_full(*key), 1)
                for i in range(nt):
                    for h in range(2):
                        free_for(pe, "ht", l, i, h)
                        for k in range(4):
                            mm = pe.transpose(bank("ht", l, i, h)[:, k * P:(k + 1) * P],
                                              h_t[:, 4 * h + k, i * P:(i + 1) * P], ident)
                        mm.then_inc(is_full("ht", l, i, h), 1)
                free_for(pe, "pos", l)
                pe.wait_ge(pos_done, POS[l])
                for i in range(nt):
                    mm = pe.transpose(bank("pos", l)[:, i * NE:(i + 1) * NE], sel_e[0:NE, 3, i * P:(i + 1) * P],
                                      ident[0:NE, 0:NE])
                mm.then_inc(is_full("pos", l), 1)
                for i in range(nt):
                    for h in range(2):
                        drained_of(pe, "ht", l, i, h)
                pe.wait_ge(onehot_done, ONEHOT[l])
                for k in range(KT):
                    for m in range(3 if l == 0 else 2):
                        sel = onehot[0][:, :, m * 512:(m + 1) * 512] if m < 2 else onehot[1]
                        first = 0 if m < 2 else LT
                        product(("ga", l, k, m), lambda i: h_tok[:, first + i, k * P:(k + 1) * P],
                                LT if m < 2 else CTT, lambda i: sel[:, i, :], 512)
                for m in range(3 if l == 0 else 2):
                    for k in range(KT - 3, KT):
                        drained_of(pe, "ga", l, k, m)
                ns = sum(CAP) if l == 0 else CAP[0]

                with pe.Fori(0, NE // 4) as turn:
                    for e in range(4):
                        for h in range(2):
                            for m, name in enumerate(("h1", "h3")):
                                w = chunk_here(pe, "ex", l, e, 2 * h + m, turn=turn) \
                                    .rearrange("p (k n) -> p k n", k=KT)
                                free_for(pe, name, l, e, h, turn=turn)
                                for f in range(4):
                                    for k in range(KT):
                                        x0 = (turn * 4 + (e + 4)) * (KT * ns) + k * ns
                                        mm = pe.matmul(bank(name, l, e, h)[:, f * ns:(f + 1) * ns],
                                                       w[:, k, f * P:(f + 1) * P], xgy[:, bass.ds(x0, ns)],
                                                       start=(k == 0), stop=(k == KT - 1))
                                mm.then_inc(is_full(name, l, e, h), 1)
                        for h in range(2):
                            w = chunk_here(pe, "ex", l, e, 4 + h, turn=turn).rearrange("p (k n) -> p k n", k=KT)
                            free_for(pe, "y", l, e, h, turn=turn)
                            for f in range(KT):
                                if h == 0 and f % 4 == 0:
                                    drained_of(pe, "h3", l, e, f // 4, turn=turn)
                                mm = pe.matmul(bank("y", l, e, h)[0:ns, :], hid[e % 2][:, f, 0:ns], w[:, f, :],
                                               start=(f == 0), stop=(f == KT - 1))
                            mm.then_inc(is_full("y", l, e, h), 1)
                pe.wait_ge(og_done, ONEHOT[l])
                for part, npair, ntile, in ((0, NE // 2, LT), (1, NE // 4, CTT))[:len(both)]:
                    for p in range(npair):
                        key = ("sg", l, p, part)
                        free_for(pe, *key)
                        for i in range(ntile):
                            mm = pe.transpose(bank(*key)[:, i * P:(i + 1) * P],
                                              onehot[part][:, i, p * P:(p + 1) * P], ident)
                        mm.then_inc(is_full(*key), 1)
                for part, npair in ((0, NE // 2), (1, NE // 4))[:len(both)]:
                    for p in range(npair):
                        drained_of(pe, "sg", l, p, part)
                for h in range(2):
                    drained_of(pe, "y", l, NE - 1, h)
                    drained_of(pe, "y", l, NE - 2, h)
                for k in range(KT):
                    for part in both:
                        product(("mo", l, k, part[0]),
                                lambda p: y_rows(l, part[0], p)[:, k * P:(k + 1) * P],
                                (NE // 2, NE // 4)[part[0]], lambda p: sg[part[0]][:, p, :], part[2])
                mean_square(l, POST_FFN)

            for l in range(DEPTH):
                layer(l)
            pe.wait_ge(x_updated, 8 * 2 * DEPTH)
            for i in range(LT):
                for h in range(2):
                    free_for(pe, "out", i, h)
                    for k in range(4):
                        mm = pe.transpose(bank("out", i, h)[:, k * P:(k + 1) * P],
                                          x_t[:, 4 * h + k, i * P:(i + 1) * P], ident)
                    mm.then_inc(is_full("out", i, h), 1)

        @block.scalar
        def _(act):
            steps = [0]

            def link(ins):
                steps[0] += 1
                ins.then_inc(act_step, 1)
                act.wait_ge(act_step, steps[0])

            def squares(l, norm, src, ready):
                base = SQ0(l, norm)
                for k in range(KT):
                    ready(k)
                    if k >= 2:
                        act.wait_ge(sq_used, SQU(l, norm) + k - 1)
                    n = TOK if len(parts_of(l, norm)) == 2 else SEQ
                    act.activation(sq[k % 2][:, 0:n], src[:, k, 0:n], ACT.Square).then_inc(sq_ready, 1)
                roots(("ms", l, norm), parts_of(l, norm))

            def roots(key, parts):
                for part in parts:
                    full_of(act, *key, part[0])
                    act.activation(rb[:, part[1]:part[1] + part[2]], bank(*key, part[0])[:, 0:part[2]], ACT.Sqrt,
                                   bias=eps_t).then_inc(is_drained(*key, part[0]), 1)

            def modulated(l, norm):
                mix = norm == PRE_MIX
                pi = 2 * l + (0 if mix else 1)
                for k in range(KT):
                    act.wait_ge(xr_ready, 8 * pi + k + 1)
                    parts = parts_of(l, norm)
                    for part in parts:
                        w, cols = part[0], slice(part[1], part[1] + part[2])
                        op = act.activation(h_t[:, k, cols], sq[k % 2][:, cols], ACT.Identity,
                                            scale=scl[:, 0 if mix else 2, k, w:w + 1],
                                            bias=mods[:, (0 if mix else 24) + k, w:w + 1])
                    op.then_inc(h_ready, 1)

            act.wait_ge(set_up, 1)
            for i in range(TT):
                full_of(act, "xin", i, 0)
                act.activation(x_t[:, 0:4, i * P:(i + 1) * P],
                               bank("xin", i, 0)[:, :].rearrange("p (k t) -> p k t", k=4), ACT.Copy) \
                    .then_inc(is_drained("xin", i, 0), 1)
            full_of(act, "cin", 0)
            act.activation(c_t.rearrange("p (k w) -> p w k", w=2),
                           bank("cin", 0)[:, 0:2 * KT].rearrange("p (w k) -> p w k", w=2), ACT.Silu) \
                .then_inc(is_drained("cin", 0), 1)

            def layer(l):
                both = parts_of(l)

                def ready0(k):
                    if l == 0 and k == 0:
                        for i in range(TT):
                            drained_of(act, "xin", i, 0)
                            drained_of(act, "xin", i, 1)
                    if l:
                        act.wait_ge(x_updated, 8 * 2 * l)

                squares(l, PRE_MIX, x_t, ready0)
                act.wait_ge(mods_ready, l + 1)
                modulated(l, PRE_MIX)
                act.wait_ge(conv_zero, l + 1)
                for c in range(C_KV):
                    for t in range(CT):
                        for part in both:
                            key = ("win", l, c, t, part[0])
                            n = part[2]
                            src = bank(*key)[:, 0:n]
                            if c == C_HV:
                                continue
                            full_of(act, *key)
                            fn = ACT.Copy
                            if c == C_AV:
                                dst = cpad[:, t, PADC[0] * part[0] + HC:PADC[0] * part[0] + HC + n]
                            elif c == C_AG:
                                j = GLU(l, t, part[0])
                                if j >= 2:
                                    act.wait_ge(glu_done, j - 1)
                                dst, fn = sq[j % 2][:, 0:n], ACT.Sigmoid
                            elif c == C_BG:
                                dst = b_t[:, t, part[1]:part[1] + n]
                            elif c == C_CG:
                                dst = bpad[:, t, PADS[0] * part[0] + HS:PADS[0] * part[0] + HS + n]
                            else:
                                dst = q_t[:, t, part[1]:part[1] + n]
                            act.activation(dst, src, fn).then_inc(is_drained(*key), 1)
                for part in (LAT, CON):
                    full_of(act, "k", l, part[0])
                    act.activation(k_t[:, 0, part[1]:part[1] + part[2]], bank("k", l, part[0])[:, 0:part[2]],
                                   ACT.Copy).then_inc(is_drained("k", l, part[0]), 1)
                for part, first, n in ((0, 0, LT), (1, LT, CTT)):
                    full_of(act, "v", l, part)
                    act.activation(v_tok[:, first:first + n, :],
                                   bank("v", l, part)[:, 0:n * P].rearrange("p (i n) -> p i n", n=P),
                                   ACT.Copy).then_inc(is_drained("v", l, part), 1)
                for i in range(TT if l == 0 else LT):
                    full_of(act, "f", l, i)
                    act.activation(f_tok[:, i, :], bank("f", l, i)[:, :], ACT.Copy) \
                        .then_inc(is_drained("f", l, i), 1)

                def fourier_out(g):
                    for part in both:
                        key = ("fo", l, g, part[0])
                        i0, i1 = (0, LT) if part[0] == 0 else (LT, TT)
                        full_of(act, *key)
                        act.activation(f_tok[:, i0:i1, g * P:(g + 1) * P],
                                       bank(*key)[:, 0:part[2]].rearrange("p (i n) -> p i n", n=P), ACT.Copy,
                                       ).then_inc(is_drained(*key), 1)

                act.wait_ge(short_done, 4 * (l + 1))
                for g in range(CT):
                    for part in both:
                        cols = slice(part[1], part[1] + part[2])
                        for name, dst in (("fc", xc), ("fs", xs)):
                            full_of(act, name, l, g, part[0])
                            act.activation(dst[g % 2][:, cols], bank(name, l, g, part[0])[:, 0:part[2]], ACT.Copy) \
                                .then_inc(is_drained(name, l, g, part[0]), 1)
                    if g:
                        fourier_out(g - 1)
                fourier_out(CT - 1)
                units = att_units(l)

                def ctx_scores(u):
                    lo, hi, nk = band(units[u])
                    nl = (hi - lo) * P
                    if u == 0:
                        full_of(act, "fo", l, CT - 1, both[-1][0])
                    for h in range(GRP):
                        full_of(act, "sc", l, u, h)
                        if u >= 2 and h == 0:
                            full_of(act, "pt", l, u - 2, band(units[u - 2])[2] - 1)
                        act.activation(S_buf[u % 2][:, h, nl:nl + CTX], bank("sc", l, u, h)[:, 0:CTX], ACT.Copy) \
                            .then_inc(is_drained("sc", l, u, h), 1)

                def exps(u):
                    nk = band(units[u])[2]
                    g = units[u][2]
                    act.wait_ge(stats_done, PROBS0[l] + u + 1)
                    act.activation(st[:, 4, :], st[:, 2, :], ACT.Exp).then_inc(exps_done, 1)
                    for h in range(GRP):
                        S = S_buf[u % 2][:, h, 0:nk * P]
                        act.activation(S, S, ACT.Exp, bias=st[:, 1, h:h + 1], scale=HD ** -0.5,
                                       accum_out=st[:, 3, h:h + 1]).then_inc(exps_done, 1)

                def turned(u):
                    con, n, g = units[u]
                    nk = band(units[u])[2]
                    for kt in range(nk):
                        if kt % 2 == 0:
                            full_of(act, "pt", l, u, kt)
                            if u:
                                full_of(act, "av", l, u - 1)
                            act.activation(probs_t[:, kt, :], bank("pt", l, u, kt)[:, :], ACT.Copy) \
                                .then_inc(is_drained("pt", l, u, kt), 1)
                    full_of(act, "av", l, u)
                    o = bank("av", l, u)[0:HD, :].rearrange("p (h r q) -> p r h q", r=2, q=P)
                    col = SEQ * con + n * P
                    act.activation(q_t[0:HD, 2 * g:2 * g + 2, col:col + P], o[:, 0], ACT.Copy)
                    act.activation(q_t[HD:P, 2 * g:2 * g + 2, col:col + P], o[:, 1], ACT.Copy) \
                        .then_inc(is_drained("av", l, u), 1)

                ctx_scores(0)
                for u in range(len(units)):
                    exps(u)
                    if u + 1 < len(units):
                        ctx_scores(u + 1)
                    turned(u)
                for k in range(CT):
                    if k < CT - 1:
                        act.wait_ge(centred, (CT - 1) * l + k + 1)
                    else:
                        for part in both:
                            drained_of(act, "lm", l, part[0])
                    if k >= 2:
                        act.wait_ge(sq_used, SQLNU[l] + k - 1)
                    n = TOK if l == 0 else SEQ
                    act.activation(sq[k % 2][:, 0:n], a_t[:, k, 0:n], ACT.Square).then_inc(sq_ready, 1)
                roots(("lv", l), both)
                for k in range(CT):
                    act.wait_ge(lnorm_done, CT * l + k + 1)
                    n = TOK if l == 0 else SEQ
                    act.activation(a_t[:, k, 0:n], a_t[:, k, 0:n], ACT.Silu, scale=par[l][:, R_LG + k:R_LG + k + 1],
                                   bias=par[l][:, R_LB + k:R_LB + k + 1]).then_inc(a_done, 1)
                for dp in range(KT // 2):
                    for b in range(4):
                        for t in range(2):
                            for part in both:
                                key = ("g", l, dp, b, t, part[0])
                                full_of(act, *key)
                                j = b * 2 + t
                                back = [(d, bb, tt) for d in range(KT // 2) for bb in range(4) for tt in range(2)]
                                at_ = back.index((dp, b, t))
                                if at_ >= 2:
                                    drained_of(act, "w", l, *back[at_ - 2], part[0])
                                col = R_GB + b * KT + 2 * dp + t
                                act.activation(sq[at_ % 2][:, part[1]:part[1] + part[2]], bank(*key)[:, 0:part[2]],
                                               ACT.Sigmoid, bias=par[l][:, col:col + 1]) \
                                    .then_inc(is_drained(*key), 1)
                for t in range(KT):
                    for part in both:
                        full_of(act, "wo", l, t, part[0])
                        act.activation(yo_t[:, t, part[1]:part[1] + part[2]], bank("wo", l, t, part[0])[:, 0:part[2]],
                                       ACT.Copy).then_inc(is_drained("wo", l, t, part[0]), 1)

                def ready1(k):
                    for part in both:
                        drained_of(act, "wo", l, k, part[0])
                        if k == 0:
                            for t in range(2):
                                drained_of(act, "w", l, KT // 2 - 1, 3, t, part[0])

                squares(l, POST_MIX, yo_t, ready1)
                squares(l, PRE_FFN, x_t, lambda k: act.wait_ge(x_updated, 8 * (2 * l + 1)))
                modulated(l, PRE_FFN)
                nt = TT if l == 0 else LT
                drained_of(act, "rl", l)
                act.activation(aff[:, 0:nt, :], aff[:, 0:nt, :], ACT.Exp).then_inc(aff_exp, 1)
                for i in range(nt):
                    full_of(act, "ht", l, i, 0)
                    act.activation(h_tok[:, i, 0:512], bank("ht", l, i, 0)[:, :], ACT.Copy) \
                        .then_inc(is_drained("ht", l, i, 0), 1)
                ns = sum(CAP) if l == 0 else CAP[0]
                for k in range(KT):
                    gather_out(act, l, k, 0, ns, lambda o, i: act.activation(o, i, ACT.Copy))
                    if l == 0:
                        gather_out(act, l, k, 2, ns, lambda o, i: act.activation(o, i, ACT.Copy))
                with act.Fori(0, NE // 4) as turn:
                    for e in range(4):
                        for h in range(2):
                            full_of(act, "h1", l, e, h, turn=turn)
                            if e:
                                drained_of(act, "h3", l, e - 1, h, turn=turn)
                            else:
                                drained_of(act, "h3", l, 3, h, turn=turn - 1)
                            act.activation(silu_t[h][:, 0:4 * ns], bank("h1", l, e, h)[:, 0:4 * ns], ACT.Silu) \
                                .then_inc(is_drained("h1", l, e, h), 1)
                        y_out(act, l, e, 0, turn, lambda o, i: act.activation(o, i, ACT.Copy))
                for part, npair in ((0, NE // 2), (1, NE // 4))[:len(both)]:
                    for p in range(0, npair, 2):
                        full_of(act, "sg", l, p, part)
                        act.activation(sg[part][:, p, :], bank("sg", l, p, part)[:, 0:(SEQ, CTX)[part]], ACT.Copy) \
                            .then_inc(is_drained("sg", l, p, part), 1)
                for k in range(KT):
                    for part in both:
                        full_of(act, "mo", l, k, part[0])
                        act.activation(y_t[:, k, part[1]:part[1] + part[2]], bank("mo", l, k, part[0])[:, 0:part[2]],
                                       ACT.Copy).then_inc(is_drained("mo", l, k, part[0]), 1)

                def ready2(k):
                    for part in both:
                        drained_of(act, "mo", l, k, part[0])

                squares(l, POST_FFN, y_t, ready2)

            for l in range(DEPTH):
                layer(l)
            for i in range(LT):
                full_of(act, "out", i, 0)
                act.activation(h_tok[:, i, 0:512], bank("out", i, 0)[:, :], ACT.Copy) \
                    .then_inc(is_drained("out", i, 0), 1)

        @block.vector
        def _(dve):
            steps = [0]

            def link(ins):
                steps[0] += 1
                ins.then_inc(dve_step, 1)
                dve.wait_ge(dve_step, steps[0])

            def mark(ins):
                steps[0] += 1
                ins.then_inc(dve_step, 1)
                return steps[0]

            def reciprocals(key, parts):
                for part in parts:
                    drained_of(dve, *key, part[0])
                    r = rb[:, part[1]:part[1] + part[2]]
                    link(dve.reciprocal(r, r))

            def normed(l, norm):
                reciprocals(("ms", l, norm), parts_of(l, norm))
                pi = 2 * l + (0 if norm == PRE_MIX else 1)
                n = TOK if len(parts_of(l, norm)) == 2 else SEQ
                for k in range(KT):
                    if k >= 2:
                        dve.wait_ge(h_ready, 8 * pi + k - 1)
                    dve.tensor_tensor(sq[k % 2][:, 0:n], x_t[:, k, 0:n], rb[:, 0:n], ALU.mult).then_inc(xr_ready, 1)

            def add_to_stream(l, norm, src):
                parts = parts_of(l, norm)
                reciprocals(("ms", l, norm), parts)
                n = TOK if len(parts) == 2 else SEQ
                m = 1 if norm == POST_MIX else 3
                for k in range(KT):
                    if k >= 2:
                        dve.wait_ge(x_updated, 8 * (2 * l + (norm == POST_FFN)) + k - 1)
                    link(dve.tensor_tensor(sq[k % 2][:, 0:n], src[:, k, 0:n], rb[:, 0:n], ALU.mult))
                    for part in parts:
                        w, cols = part[0], slice(part[1], part[1] + part[2])
                        op = dve.scalar_tensor_tensor(x_t[:, k, cols], sq[k % 2][:, cols], scl[:, m, k, w:w + 1],
                                                      x_t[:, k, cols], ALU.mult, ALU.add)
                    op.then_inc(x_updated, 1)

            for i in range(TT):
                full_of(dve, "xin", i, 1)
                dve.tensor_copy(x_t[:, 4:8, i * P:(i + 1) * P],
                                bank("xin", i, 1)[:, :].rearrange("p (k t) -> p k t", k=4)) \
                    .then_inc(is_drained("xin", i, 1), 1)
            for l in range(DEPTH):
                for r, (first, n) in enumerate(((0, NR1), (NR1, NR2), (NR1 + NR2, NR3))):
                    full_of(dve, "par", l, r)
                    dve.tensor_copy(par[l][:, first:first + n], bank("par", l, r)[:, 0:n]) \
                        .then_inc(is_drained("par", l, r), 1)
            for l in range(DEPTH):
                for r in range(3):
                    drained_of(dve, "par", l, r)
            dve.wait_ge(par_loaded, 16 * 25)
            link(dve.tensor_scalar(nsink, nsink, -1.0, None, ALU.mult))

            def layer(l):
                both = parts_of(l)
                if l:
                    dve.wait_ge(x_updated, 8 * 2 * l)
                for c in range(12):
                    full_of(dve, "mod", l, c)
                    b = par[l][:, R_ADAB + 4 * c:R_ADAB + 4 * c + 4]
                    dve.tensor_tensor(mods[:, 4 * c:4 * c + 4, :],
                                      bank("mod", l, c)[:, 0:8].rearrange("p (c w) -> p c w", w=2),
                                      b.unsqueeze(2).broadcast_to([P, 4, 2]), ALU.add) \
                        .then_inc(is_drained("mod", l, c), 1)
                for c in range(12):
                    drained_of(dve, "mod", l, c)
                gain = {R: par[l][:, R:R + KT].unsqueeze(2).broadcast_to([P, KT, 2]) for R in (R_PM, R_QM, R_PF, R_QF)}
                m = mods.rearrange("p (v c) w -> p v c w", c=KT)
                v1 = mark(dve.tensor_tensor(scl[:, 1], m[:, 2], gain[R_QM], ALU.mult))
                v2 = mark(dve.tensor_tensor(scl[:, 3], m[:, 5], gain[R_QF], ALU.mult))
                link(dve.tensor_scalar(scl[:, 0], m[:, 1], 1.0, None, ALU.add))
                link(dve.tensor_scalar(scl[:, 2], m[:, 4], 1.0, None, ALU.add))
                link(dve.tensor_tensor(scl[:, 0], scl[:, 0], gain[R_PM], ALU.mult))
                dve.tensor_tensor(scl[:, 2], scl[:, 2], gain[R_PF], ALU.mult).then_inc(mods_ready, 1)
                dve.wait_ge(mods_ready, l + 1)
                normed(l, PRE_MIX)
                for pad, sizes, half in ((cpad, PADC, HC), (bpad, PADS, HS)):
                    for w in range(2):
                        first = sizes[0] * w
                        dve.memset(pad[:, :, first:first + half], 0.0)
                        z = dve.memset(pad[:, :, first + sizes[w] - half:first + sizes[w]], 0.0)
                z.then_inc(conv_zero, 1)
                for t in range(CT):
                    for part in both:
                        key = ("win", l, C_AG, t, part[0])
                        drained_of(dve, "win", l, C_AV, t, part[0])
                        drained_of(dve, *key)
                        j = GLU(l, t, part[0])
                        dst = cpad[:, t, PADC[0] * part[0] + HC:PADC[0] * part[0] + HC + part[2]]
                        dve.tensor_tensor(dst, dst, sq[j % 2][:, 0:part[2]], ALU.mult).then_inc(glu_done, 1)
                dve.wait_ge(glu_done, GLU(l, CT - 1, both[-1][0]) + 1)
                dve.wait_ge(conv_zero, l + 1)

                def conv_taps():
                    marks = {}
                    for j in range(CONV_K):
                        for t in range(CT):
                            for part in both:
                                first = PADC[0] * part[0] + j
                                src = cpad[:, t, first:first + part[2]]
                                dst = a_t[:, t, part[1]:part[1] + part[2]]
                                w = par[l][:, NR1 + j * CT + t:NR1 + j * CT + t + 1]
                                if j == 0:
                                    b = par[l][:, R_CB + t:R_CB + t + 1]
                                    op = dve.tensor_scalar(dst, src, w, b, ALU.mult, ALU.add)
                                else:
                                    dve.wait_ge(dve_step, marks[t, part[0]])
                                    op = dve.scalar_tensor_tensor(dst, src, w, dst, ALU.mult, ALU.add)
                                if j < CONV_K - 1:
                                    marks[t, part[0]] = mark(op)
                                else:
                                    op.then_inc(conv_done, 1)
                                yield

                taps = conv_taps()

                def convolve(n):
                    for _ in range(n):
                        next(taps, None)

                for t in range(CT):
                    for part in both:
                        convolve(4)
                        key = ("win", l, C_HV, t, part[0])
                        full_of(dve, *key)
                        drained_of(dve, "win", l, C_CG, t, part[0])
                        dst = bpad[:, t, PADS[0] * part[0] + HS:PADS[0] * part[0] + HS + part[2]]
                        dve.tensor_tensor(dst, bank(*key)[:, 0:part[2]], dst, ALU.mult).then_inc(is_drained(*key), 1)
                for t in range(CT):
                    if t >= 2:
                        dve.wait_ge(short_done, 4 * l + t - 1)
                    for part in both:
                        drained_of(dve, "win", l, C_HV, t, part[0])
                        drained_of(dve, "win", l, C_BG, t, part[0])
                        cols = slice(part[1], part[1] + part[2])
                        for j in range(SHORT_K):
                            first = PADS[0] * part[0] + j
                            src = bpad[:, t, first:first + part[2]]
                            c0 = NR1 + NR2 + j * CT + t
                            w = par[l][:, c0:c0 + 1]
                            if j == 0:
                                link(dve.tensor_scalar(sq[t % 2][:, cols], src, w, None, ALU.mult))
                            else:
                                link(dve.scalar_tensor_tensor(sq[t % 2][:, cols], src, w, sq[t % 2][:, cols], ALU.mult, ALU.add))
                        op = dve.tensor_tensor(b_t[:, t, cols], b_t[:, t, cols], sq[t % 2][:, cols], ALU.mult)
                    op.then_inc(short_done, 1)
                for t in range(CT + 1):
                    convolve(8)
                    if t == 0:
                        dve.wait_ge(short_done, 4 * (l + 1))
                    full_of(dve, "rope", l, t)
                    dst = q_t[:, t, 0:SEQ] if t < CT else k_t[:, 0, 0:SEQ]
                    if t >= 2:
                        dve.wait_ge(rope_done, 5 * l + t - 1)
                    dve.tensor_tensor(sq[t % 2][:, 0:SEQ], bank("rope", l, t)[:, :], sinT, ALU.mult) \
                        .then_inc(is_drained("rope", l, t), 1)
                    link(dve.tensor_tensor(dst, dst, cosT, ALU.mult))
                    drained_of(dve, "rope", l, t)
                    dve.tensor_tensor(dst, dst, sq[t % 2][:, 0:SEQ], ALU.add).then_inc(rope_done, 1)
                dve.wait_ge(rope_done, 5 * (l + 1))
                drained_of(dve, "k", l, 1)
                dve.tensor_copy(k_t[0:HD, 1, :], k_t[HD:P, 0, :]).then_inc(swapped, 1)
                dve.tensor_copy(k_t[HD:P, 1, :], k_t[0:HD, 0, :]).then_inc(swapped, 1)
                convolve(64)
                units = att_units(l)

                def local_scores(u):
                    con, n, g = units[u]
                    lo, hi, _ = band(units[u])
                    if con:
                        return
                    if u == 0:
                        full_of(dve, "fo", l, CT - 1, both[-1][0])
                    for h in range(GRP):
                        full_of(dve, "sl", l, u, h)
                        if u >= 2 and h == 0:
                            full_of(dve, "pt", l, u - 2, band(units[u - 2])[2] - 1)
                        m0 = (lo - (n - 1)) * P
                        nl = (hi - lo) * P
                        dve.tensor_tensor(S_buf[u % 2][:, h, 0:nl], bank("sl", l, u, h)[:, 0:nl],
                                          maskT[:, m0:m0 + nl], ALU.add).then_inc(is_drained("sl", l, u, h), 1)

                def stats(u):
                    con, n, g = units[u]
                    nk = band(units[u])[2] * P
                    for h in range(GRP):
                        if not con:
                            drained_of(dve, "sl", l, u, h)
                        drained_of(dve, "sc", l, u, h)
                    link(dve.tensor_reduce(st[:, 0, :], S_buf[u % 2][:, :, 0:nk], AX.X, ALU.max))
                    ns = nsink[:, l * HEADS + GRP * g:l * HEADS + GRP * g + GRP]
                    link(dve.scalar_tensor_tensor(st[:, 1, :], st[:, 0, :], -(HD ** -0.5), ns, ALU.mult, ALU.min))
                    dve.tensor_tensor(st[:, 2, :], st[:, 1, :], ns, ALU.subtract).then_inc(stats_done, 1)

                def scale(u):
                    nk = band(units[u])[2] * P
                    dve.wait_ge(exps_done, 5 * (PROBS0[l] + u + 1))
                    link(dve.tensor_tensor(st[:, 6, :], st[:, 3, :], st[:, 4, :], ALU.add))
                    link(dve.reciprocal(st[:, 7, :], st[:, 6, :]))
                    for h in range(GRP):
                        S = S_buf[u % 2][:, h, 0:nk]
                        op = dve.tensor_scalar(S, S, st[:, 7, h:h + 1], None, ALU.mult)
                    op.then_inc(probs_done, 1)

                def turned(u):
                    for kt in range(1, band(units[u])[2], 2):
                        full_of(dve, "pt", l, u, kt)
                        if u:
                            full_of(dve, "av", l, u - 1)
                        dve.tensor_copy(probs_t[:, kt, :], bank("pt", l, u, kt)[:, :]) \
                            .then_inc(is_drained("pt", l, u, kt), 1)

                local_scores(0)
                for u in range(len(units)):
                    stats(u)
                    scale(u)
                    if u + 1 < len(units):
                        local_scores(u + 1)
                    turned(u)
                    convolve(4)
                convolve(CONV_K * CT * 2)
                dve.wait_ge(conv_done, CONV[l])
                for part in both:
                    full_of(dve, "lm", l, part[0])
                for k in range(CT):
                    for part in both:
                        cols = slice(part[1], part[1] + part[2])
                        op = dve.tensor_tensor(a_t[:, k, cols], a_t[:, k, cols], bank("lm", l, part[0])[:, 0:part[2]],
                                               ALU.subtract)
                        if k == CT - 1:
                            op.then_inc(is_drained("lm", l, part[0]), 1)
                        elif part is both[-1]:
                            op.then_inc(centred, 1)
                reciprocals(("lv", l), both)
                for k in range(CT):
                    n = TOK if l == 0 else SEQ
                    dve.tensor_tensor(a_t[:, k, 0:n], a_t[:, k, 0:n], rb[:, 0:n], ALU.mult).then_inc(lnorm_done, 1)
                at_ = -1
                for dp in range(KT // 2):
                    for b in range(4):
                        for t in range(2):
                            at_ += 1
                            for part in both:
                                cols = slice(part[1], part[1] + part[2])
                                key = ("w", l, dp, b, t, part[0])
                                full_of(dve, *key)
                                drained_of(dve, "g", l, dp, b, t, part[0])
                                gate, y = sq[at_ % 2][:, cols], y_t[:, 2 * dp + t, cols]
                                dst = y if b == 0 else rb[:, cols]
                                dve.tensor_tensor(dst, gate, bank(*key)[:, 0:part[2]], ALU.mult) \
                                    .then_inc(is_drained(*key), 1)
                                if b:
                                    drained_of(dve, *key)
                                    if b == 3 and part is both[-1]:
                                        dve.tensor_tensor(y, y, rb[:, cols], ALU.add).then_inc(merged, 1)
                                        dve.wait_ge(merged, 8 * l + 2 * dp + t + 1)
                                    else:
                                        link(dve.tensor_tensor(y, y, rb[:, cols], ALU.add))
                                else:
                                    drained_of(dve, *key)
                add_to_stream(l, POST_MIX, yo_t)
                dve.wait_ge(x_updated, 8 * (2 * l + 1))
                normed(l, PRE_FFN)
                nt = TT if l == 0 else LT
                full_of(dve, "rl", l)
                lg = bank("rl", l)[:, 0:nt * NE].rearrange("p (i e) -> p i e", e=NE)
                link(dve.tensor_reduce(rs[:, 0, 0:nt], lg, AX.X, ALU.max))
                dve.tensor_tensor(aff[:, 0:nt, :], lg, rs[:, 0, 0:nt].unsqueeze(2).broadcast_to([P, nt, NE]),
                                  ALU.subtract).then_inc(is_drained("rl", l), 1)
                drained_of(dve, "rl", l)
                dve.wait_ge(aff_exp, l + 1)
                link(dve.tensor_reduce(rs[:, 0, 0:nt], aff[:, 0:nt, :], AX.X, ALU.add))
                link(dve.reciprocal(rs[:, 1, 0:nt], rs[:, 0, 0:nt]))
                dve.tensor_tensor(aff[:, 0:nt, :], aff[:, 0:nt, :],
                                  rs[:, 1, 0:nt].unsqueeze(2).broadcast_to([P, nt, NE]), ALU.mult) \
                    .then_inc(aff_done, 1)
                E = slice(0, NE)
                link(dve.memset(sel_e[E, 0, :], 1.0))
                for w, (_, first, n) in enumerate(both):
                    cols = slice(first, first + n)
                    full_of(dve, "at", l, w)
                    dve.tensor_copy(sel_e[E, 1, cols], bank("at", l, w)[0:NE, 0:n]) \
                        .then_inc(is_drained("at", l, w), 1)
                    drained_of(dve, "at", l, w)
                    for _ in range(CAP[w] // 8):
                        link(dve.max(top8[E, 0:8], sel_e[E, 1, cols]))
                        link(dve.match_replace(sel_e[E, 1, cols], top8[E, 0:8], sel_e[E, 1, cols], -1.0))
                    link(dve.tensor_scalar(sel_e[E, 2, cols], sel_e[E, 1, cols], 0.0, None, ALU.is_lt))
                    link(dve.tensor_tensor_scan(sel_e[E, 3, cols], sel_e[E, 0, cols], sel_e[E, 2, cols], 0.0,
                                                ALU.mult, ALU.add))
                    link(dve.tensor_tensor(sel_e[E, 3, cols], sel_e[E, 3, cols], sel_e[E, 2, cols], ALU.mult))
                    dve.tensor_scalar(sel_e[E, 3, cols], sel_e[E, 3, cols], -1.0, None, ALU.add) \
                        .then_inc(pos_done, 1)
                for i in range(nt):
                    full_of(dve, "ht", l, i, 1)
                    dve.tensor_copy(h_tok[:, i, 512:1024], bank("ht", l, i, 1)[:, :]) \
                        .then_inc(is_drained("ht", l, i, 1), 1)
                full_of(dve, "pos", l)
                dve.tensor_copy(pos_t[:, 0:nt, :], bank("pos", l)[:, 0:nt * NE].rearrange("p (i e) -> p i e", e=NE)) \
                    .then_inc(is_drained("pos", l), 1)
                drained_of(dve, "pos", l)

                def per_tile(i):
                    w = 0 if i < LT else 1
                    return w, onehot[w][:, i - w * LT, :].rearrange("p (e s) -> p e s", e=NE)

                for i in range(nt):
                    w, oh = per_tile(i)
                    dve.tensor_tensor(oh, iota[:, 0:CAP[w]].unsqueeze(1).broadcast_to([P, NE, CAP[w]]),
                                      pos_t[:, i, :].unsqueeze(2).broadcast_to([P, NE, CAP[w]]), ALU.is_equal) \
                        .then_inc(onehot_done, 1)
                ns = sum(CAP) if l == 0 else CAP[0]
                for k in range(KT):
                    gather_out(dve, l, k, 1, ns, dve.tensor_copy)
                full_of(dve, "ga", l, KT - 1, 2 if l == 0 else 1)
                for i in range(nt):
                    w, oh = per_tile(i)
                    dve.tensor_tensor(oh, oh, aff[:, i, :].unsqueeze(2).broadcast_to([P, NE, CAP[w]]), ALU.mult) \
                        .then_inc(og_done, 1)
                with dve.Fori(0, NE // 4) as turn:
                    for e in range(4):
                        for h in range(2):
                            full_of(dve, "h3", l, e, h, turn=turn)
                            drained_of(dve, "h1", l, e, h, turn=turn)
                            if e >= 2:
                                full_of(dve, "y", l, e - 2, 1, turn=turn)
                            else:
                                full_of(dve, "y", l, e + 2, 1, turn=turn - 1)
                            dve.tensor_tensor(hid[e % 2][:, 4 * h:4 * h + 4, 0:ns],
                                              silu_t[h][:, 0:4 * ns].rearrange("p (f s) -> p f s", f=4),
                                              bank("h3", l, e, h)[:, 0:4 * ns].rearrange("p (f s) -> p f s", f=4),
                                              ALU.mult).then_inc(is_drained("h3", l, e, h), 1)
                        y_out(dve, l, e, 1, turn, dve.tensor_copy)
                for part, npair in ((0, NE // 2), (1, NE // 4))[:len(both)]:
                    for p in range(1, npair, 2):
                        full_of(dve, "sg", l, p, part)
                        dve.tensor_copy(sg[part][:, p, :], bank("sg", l, p, part)[:, 0:(SEQ, CTX)[part]]) \
                            .then_inc(is_drained("sg", l, p, part), 1)
                add_to_stream(l, POST_FFN, y_t)

            for l in range(DEPTH):
                layer(l)
            for i in range(LT):
                full_of(dve, "out", i, 1)
                dve.tensor_copy(h_tok[:, i, 512:1024], bank("out", i, 1)[:, :]) \
                    .then_inc(is_drained("out", i, 1), 1)


def tables():
    f = np.float32
    ident = np.eye(P, dtype=f)
    perm = np.zeros((P, P), f)
    for m in range(P):
        if m % 32 < 16:
            perm[m + 16, m] = -1
        else:
            perm[m - 16, m] = 1
    t = np.arange(SEQ)
    inv = (10000.0 ** (-np.arange(16, dtype=f) / f(16))).astype(f)
    ar = ((t // GRID_W).astype(f)[:, None] * inv).astype(f)
    ac = ((t % GRID_W).astype(f)[:, None] * inv).astype(f)
    ang = np.concatenate([ar, ar, ac, ac], 1).T.astype(np.float64)
    ang = np.concatenate([ang, ang], 0)
    kj, qi = np.arange(3 * P)[None, :], np.arange(P)[:, None]
    mask = np.where(np.abs(kj - P - qi) <= P, 0.0, -1e30).astype(f)

    def dft(n, fn, by):
        k = np.arange(n)
        m = fn(2 * np.pi * ((k[:, None] * k[None, :]) % n) / n) * by
        return m.reshape(n // P, P, n).transpose(1, 0, 2).reshape(P, -1)

    d = np.concatenate([dft(SEQ, np.cos, SEQ ** -0.5), dft(SEQ, np.sin, SEQ ** -0.5),
                        dft(CTX, np.cos, CTX ** -0.5), dft(CTX, np.sin, CTX ** -0.5),
                        dft(P, np.cos, P ** -0.5), dft(P, np.sin, -P ** -0.5)], 1).astype(f)
    return {"ident": ident, "ones_d": np.full((P, P), 1 / D, f), "ones_c": np.full((P, P), 1 / DC, f), "perm": perm,
            "cos": np.cos(ang).astype(f), "sin": np.sin(ang).astype(f), "mask": mask,
            "iota": np.broadcast_to(np.arange(CAP[0], dtype=f), (P, CAP[0])).copy(), "dft": d}


def kernel(**inputs):
    import concourse.bacc as bacc
    from concourse.bass_utils import run_bass_kernel_spmd

    nc = bacc.Bacc("TRN2", target_bir_lowering=False, num_devices=1)
    arrays, ins, consts = {}, {}, {}
    for group, prefix, source in ((ins, "in", inputs), (consts, "const", tables())):
        for name, a in source.items():
            a = np.ascontiguousarray(a)
            arrays[f"{prefix}_{name}"] = a
            group[name] = nc.dram_tensor(f"{prefix}_{name}", a.shape, mybir.dt.from_np(a.dtype),
                                         kind="ExternalInput").ap()
    out = nc.dram_tensor("out", (1, SEQ, D), F32, kind="ExternalOutput").ap()
    build(nc, ins, consts, out)
    r = run_bass_kernel_spmd(nc, [arrays], core_ids=[0])
    return r.results[0]["out"]
```

```python
from contextlib import ExitStack

import numpy as np

import concourse.bass as bass
from concourse import mybir
from concourse.alu_op_type import AluOpType as ALU

F32 = mybir.dt.float32
F32R = mybir.dt.float32r
ACT = mybir.ActivationFunctionType
AX = mybir.AxisListType

P = 128
D = 1024
KT = D // P
SEQ, CTX = 512, 256
TOK = SEQ + CTX
DEPTH = 2
LAT, CON = (0, 0, SEQ), (1, SEQ, CTX)
DC = 512
CT = DC // P
CONV_K, SHORT_K = 31, 3
HC, HS = CONV_K // 2, SHORT_K // 2
HEADS, KVH, HD = 8, 2, 64
GRP = HEADS // KVH
GRID_W = 64
NE = 16
CAP = (2 * SEQ // NE, 2 * CTX // NE)
FX = 1024
EPS = 1e-6
NB = SEQ // P
LT, CTT = SEQ // P, CTX // P
TT = LT + CTT
O_A, O_B, O_Q, O_K, O_V, O_F, O_G = 0, 1024, 2560, 3072, 3200, 3328, 3840
WCHUNKS = [(0, 512), (512, 512), (1024, 512), (1536, 512), (2048, 512), (2560, 512), (3072, 256), (3328, 512)]
C_AV, C_AG, C_BG, C_CG, C_HV, C_Q, C_KV, C_F = range(8)
BANKS = 8
HID = KT * sum(CAP) + P - sum(CAP)
SLOT = 4096
PADC = SEQ + 2 * HC, CTX + 2 * HC
PADS = SEQ + 2 * HS, CTX + 2 * HS
R_ADAB, R_PM, R_QM, R_PF, R_QF, R_GB, R_CB, R_LG, R_LB = 0, 48, 56, 64, 72, 80, 112, 116, 120
NR1, NR2, NR3 = 124, CONV_K * CT, SHORT_K * CT
NPAR = NR1 + NR2 + NR3
PRE_MIX, POST_MIX, PRE_FFN, POST_FFN = range(4)
MOD_CHUNKS, MOD_FIRST = 12, 4
MOD_AFTER = {("win", 0, c): (0, MOD_FIRST + c) for c in range(8)}
MOD_AFTER |= {("mg", 0, i // 4, i % 4): (1, i) for i in range(MOD_CHUNKS)}


def parts_of(l, norm=POST_MIX):
    return (LAT, CON) if l == 0 or norm == PRE_MIX else (LAT,)


def att_units(l):
    units = [(0, n, g) for n in range(NB) for g in range(KVH)]
    return units + ([(1, n, g) for n in range(CTT) for g in range(KVH)] if l == 0 else [])


def band(unit):
    con, n, _ = unit
    lo, hi = (0, 0) if con else (max(n - 1, 0), min(n + 2, NB))
    return lo, hi, hi - lo + CTT


def plan_jobs():
    jobs, n = {}, 0

    def add(*key):
        nonlocal n
        jobs[key] = n
        n += 1

    def mod_after(*key):
        if key in MOD_AFTER:
            add("mod", *MOD_AFTER[key])

    for i in range(TT):
        for h in range(2):
            add("xin", i, h)
    for l in range(DEPTH):
        for r in range(3):
            add("par", l, r)
    add("cin", 0)
    for l in range(DEPTH):
        both = parts_of(l)
        for part in (LAT, CON):
            add("ms", l, PRE_MIX, part[0])
        if l == 0:
            for c in range(MOD_FIRST):
                add("mrow", l, c)
                add("mod", l, c)
        for c in range(C_KV):
            for t in range(CT):
                for part in both:
                    add("win", l, c, t, part[0])
                if c == C_Q:
                    add("rope", l, t)
            mod_after("win", l, c)
        for part in (LAT, CON):
            add("k", l, part[0])
        add("rope", l, CT)
        for part in (LAT, CON):
            add("v", l, part[0])
        mod_after("win", l, C_KV)
        for i in range(TT if l == 0 else LT):
            add("f", l, i)
        mod_after("win", l, C_F)
        for g in range(CT):
            for part in both:
                add("fc", l, g, part[0])
                add("fs", l, g, part[0])
            if g:
                for part in both:
                    add("fo", l, g - 1, part[0])
        for part in both:
            add("fo", l, CT - 1, part[0])
        units = att_units(l)

        def scores(u):
            for h in range(GRP):
                if not units[u][0]:
                    add("sl", l, u, h)
                add("sc", l, u, h)

        scores(0)
        for u in range(len(units)):
            if u + 1 < len(units):
                scores(u + 1)
            for kt in range(band(units[u])[2]):
                add("pt", l, u, kt)
            add("av", l, u)
        for part in both:
            add("lm", l, part[0])
        for part in both:
            add("lv", l, part[0])
        for dp in range(KT // 2):
            for b in range(4):
                for t in range(2):
                    for part in both:
                        add("g", l, dp, b, t, part[0])
                        add("w", l, dp, b, t, part[0])
                mod_after("mg", l, dp, b)
        for t in range(KT):
            for part in both:
                add("wo", l, t, part[0])
        for norm in (POST_MIX, PRE_FFN):
            for part in both:
                add("ms", l, norm, part[0])
        add("rl", l)
        add("at", l, 0)
        if l == 0:
            add("at", l, 1)
        for i in range(TT if l == 0 else LT):
            for h in range(2):
                add("ht", l, i, h)
        add("pos", l)
        for k in range(KT):
            add("ga", l, k, 0)
            add("ga", l, k, 1)
            if l == 0:
                add("ga", l, k, 2)
        for e in range(NE):
            for h in range(2):
                add("h1", l, e, h)
                add("h3", l, e, h)
            add("y", l, e, 0)
            add("y", l, e, 1)
        for p in range(NE // 2):
            add("sg", l, p, 0)
        if l == 0:
            for p in range(NE // 4):
                add("sg", l, p, 1)
        for k in range(KT):
            for part in both:
                add("mo", l, k, part[0])
        for part in both:
            add("ms", l, POST_FFN, part[0])
    for i in range(LT):
        for h in range(2):
            add("out", i, h)
    return jobs


def plan_chunks():
    chunks, held, last_in = {}, [0] * 4, [None] * 4

    def add(key, slot, last_job, loads=1):
        held[slot] += loads
        chunks[key] = (slot, held[slot], last_job, last_in[slot])
        last_in[slot] = key

    turn = 0

    def mixer(key, last_job, loads=1):
        nonlocal turn
        add(key, turn % 2, last_job, loads)
        turn += 1
        if key in MOD_AFTER:
            mixer(("ada", *MOD_AFTER[key]), ("mod", *MOD_AFTER[key]))

    for l in range(DEPTH):
        last = parts_of(l)[-1][0]
        if l == 0:
            for c in range(MOD_FIRST):
                mixer(("ada", l, c), ("mrow", l, c))
        for c in range(C_KV):
            mixer(("win", l, c), ("rope", l, CT - 1) if c == C_Q else ("win", l, c, CT - 1, last))
        mixer(("win", l, C_KV), ("v", l, 1))
        mixer(("win", l, C_F), ("f", l, (TT if l == 0 else LT) - 1))
        for dp in range(KT // 2):
            for b in range(4):
                mixer(("mg", l, dp, b), ("w", l, dp, b, 1, last), loads=2)
        for h in range(2):
            mixer(("wo", l, h), ("wo", l, 4 * h + 3, last))
        for e in range(NE):
            for m, (job, h) in enumerate((("h1", 0), ("h3", 0), ("h1", 1), ("h3", 1), ("y", 0), ("y", 1))):
                add(("ex", l, e, m), (6 * e + m) % 4, (job, l, e, h))
    return chunks


def build(nc, A, K, x_dram, out):
    jobs, chunks = plan_jobs(), plan_chunks()
    ctx = ExitStack()
    with ctx:
        def sb(name, n, rows=P):
            t = ctx.enter_context(nc.sbuf_tensor(name, [rows, n], F32))
            where[id(t)] = nc.sbuf_base - 4 * n
            return t

        where = {}

        def over(name, host, first, n):
            return nc.alloc_sbuf_tensor_at(name, [P, n], F32R, offset=where[id(host)] + 4 * first)

        def sem(name):
            return ctx.enter_context(nc.semaphore(name))

        x_all = sb("x_t", KT * TOK)
        x_t = x_all[:, :].rearrange("p (k t) -> p k t", k=KT)
        hb = sb("hb", 2 * KT * TOK)
        h_t = hb[:, 0:KT * TOK].rearrange("p (k t) -> p k t", k=KT)
        hb2 = hb[:, KT * TOK:2 * KT * TOK]
        y_t = hb2.rearrange("p (k t) -> p k t", k=KT)
        h_tok = hb2.rearrange("p (i d) -> p i d", i=TT)
        yo_t = h_t
        S_buf = [hb2[:, b * 2560:(b + 1) * 2560].rearrange("p (h k) -> p h k", h=GRP) for b in range(2)]
        c512 = hb2[:, 0:2048].rearrange("p (i n) -> p i n", i=LT)
        s512 = hb2[:, 2048:4096].rearrange("p (i n) -> p i n", i=LT)
        c256 = hb2[:, 4096:4608].rearrange("p (i n) -> p i n", i=CTT)
        s256 = hb2[:, 4608:5120].rearrange("p (i n) -> p i n", i=CTT)
        c128 = hb2[:, 5120:5248]
        s128 = hb2[:, 5248:5376]
        ring0 = sb("ring0", 2 * SLOT)
        slots = [ring0[:, 0:SLOT], ring0[:, SLOT:2 * SLOT], hb[:, 0:SLOT], hb[:, SLOT:2 * SLOT]]
        hb_r, ring_r = over("hb_r", hb, 0, 2 * KT * TOK), over("ring_r", ring0, 0, 2 * SLOT)
        slots_lo = [(ring_r, hb_r)[b // 2][:, b % 2 * SLOT:(b % 2 + 1) * SLOT] for b in range(4)]
        w2_hi = hb_r[:, 2 * SLOT:3 * SLOT].rearrange("p (k n) -> p k n", k=KT)
        h_hi, h_lo = (hb_r[:, b * KT * TOK:(b + 1) * KT * TOK].rearrange("p (i d) -> p i d", i=TT)
                      for b in range(2))
        mix_lo = over("mix_lo", x_all, 0, KT * TOK)[:, :].rearrange("p (k t) -> p k t", k=KT)
        mix_hi2, mix_hi1 = (hb_r[:, b * KT * TOK:(b + 1) * KT * TOK].rearrange("p (k t) -> p k t", k=KT)
                            for b in range(2))
        AR = 20992
        arena = sb("arena", AR)
        at = [0]

        def take(n):
            at[0] += n
            return arena[:, at[0] - n:at[0]]

        cpad = take(CT * sum(PADC)).rearrange("p (t n) -> p t n", t=CT)
        a_t = take(CT * TOK).rearrange("p (t n) -> p t n", t=CT)
        b_t = take(CT * TOK).rearrange("p (t n) -> p t n", t=CT)
        q_t = take(CT * TOK).rearrange("p (t n) -> p t n", t=CT)
        w_hi_at = at[0]
        k_t = take(2 * TOK).rearrange("p (s n) -> p s n", s=2)
        v_tok = take(TOK).rearrange("p (i n) -> p i n", i=TT)
        f_tok = take(CT * TOK).rearrange("p (i n) -> p i n", i=TT)
        shared = take(CT * sum(PADS))
        bpad = shared.rearrange("p (t n) -> p t n", t=CT)
        xc = [shared[:, b * 1536:b * 1536 + TOK] for b in range(2)]
        xs = [shared[:, b * 1536 + TOK:b * 1536 + 2 * TOK] for b in range(2)]
        probs_t = shared[:, 0:2560].rearrange("p (k n) -> p k n", k=5)
        assert at[0] == AR
        w_hi_r = over("w_hi_r", arena, w_hi_at, CT * D)
        w_hi = [w_hi_r[:, t * D:(t + 1) * D].rearrange("p (k n) -> p k n", k=KT) for t in range(CT)]
        mod_rows = shared[0:2, 0:MOD_FIRST * 512]
        tmp = [arena[:, 3312 + b * TOK:3312 + (b + 1) * TOK] for b in range(2)]
        xgy = arena[:, 0:15360]
        sel_e = arena[:, 0:4 * TOK].rearrange("p (w t) -> p w t", w=4)
        onehot = [arena[:, 15360:19456].rearrange("p (i s) -> p i s", i=LT),
                  arena[:, 19456:20480].rearrange("p (i s) -> p i s", i=CTT)]
        onehot_r = [over("onehot0", arena, 15360, 4096)[:, :].rearrange("p (i s) -> p i s", i=LT),
                    over("onehot1", arena, 19456, 1024)[:, :].rearrange("p (i s) -> p i s", i=CTT)]
        sg = [hb[:, 0:4096].rearrange("p (g t) -> p g t", g=NE // 2),
              hb[:, 4096:5120].rearrange("p (g t) -> p g t", g=NE // 4)]
        work = sb("work", 2 * HID + 2 * 4 * sum(CAP))
        rb = work[:, 0:TOK]
        sq = [work[:, TOK:2 * TOK], work[:, 2 * TOK:3 * TOK]]
        silu_t = [work[:, 2 * HID + b * 384:2 * HID + (b + 1) * 384] for b in range(2)]
        hid_hi, hid_lo = over("hid_hi", work, 0, HID), over("hid_lo", work, HID, HID)
        ident = sb("ident", P)[:, :]
        ones_d = sb("ones_d", P)[:, :]
        ones_c = sb("ones_c", P)[:, :]
        perm = sb("perm", P)[:, :]
        cosT = sb("cosT", SEQ)[:, :]
        sinT = sb("sinT", SEQ)[:, :]
        maskT = sb("maskT", 3 * P)[:, :]
        iota = sb("iota", CAP[0])[:, :]
        eps_t = sb("eps_t", 1)[:, :]
        spare = sb("spare", 1)[:, :]
        par = [sb(f"par{l}", NPAR)[:, :] for l in range(DEPTH)]
        nsink = sb("nsink", DEPTH * HEADS)[:, :]
        c_t = sb("c_t", 2 * KT)[:, :]
        mods = [sb(f"mods{l}", 96)[:, :].rearrange("p (c w) -> p c w", w=2) for l in range(DEPTH)]
        scl = [sb(f"scl{l}", 4 * KT * 2)[:, :].rearrange("p (m c w) -> p m c w", m=4, w=2)
               for l in range(DEPTH)]
        rw = sb("rw", KT * NE)[:, :].rearrange("p (k e) -> p k e", k=KT)
        st = sb("st", 64)[:, :].rearrange("p (w h) -> p w h", h=4)
        aff = sb("aff", TT * NE)[:, :].rearrange("p (i e) -> p i e", e=NE)
        rs = sb("rs", 2 * TT)[:, :].rearrange("p (w i) -> p w i", w=2)
        pos_t = arena[:, 20480:20480 + TT * NE].rearrange("p (i e) -> p i e", e=NE)
        top8 = sb("top8", 16)[:, :]
        x_tok = hb[:, 0:TT * D].rearrange("p (i d) -> p i d", i=TT)
        par_rows = hb2[:, 0:7 * P].rearrange("p (r n) -> p r n", n=P)

        ps = [ctx.enter_context(nc.psum_tensor(f"ps{b}", [P, 512], F32)) for b in range(BANKS)]

        full = [sem(f"full{b}") for b in range(BANKS)]
        drained = [sem(f"drained{b}") for b in range(BANKS)]
        loaded = [sem(f"loaded{s}") for s in range(4)]
        x_loaded, par_loaded, const_loaded = sem("x_loaded"), sem("par_loaded"), sem("const_loaded")
        dft_loaded = sem("dft_loaded")
        rw_loaded = sem("rw_loaded")
        set_up = sem("set_up")
        sq_ready, sq_used = sem("sq_ready"), sem("sq_used")
        xr_ready, h_ready = sem("xr_ready"), sem("h_ready")
        x_updated = sem("x_updated")
        glu_done = sem("glu_done")
        rope_done = sem("rope_done")
        swapped = sem("swapped")
        short_done = sem("short_done")
        stats_done = sem("stats_done")
        exps_done = sem("exps_done")
        probs_done = sem("probs_done")
        conv_done = sem("conv_done")
        centred = sem("centred")
        lnorm_done = sem("lnorm_done")
        a_done = sem("a_done")
        merged = sem("merged")
        aff_exp, aff_done, pos_done, onehot_done, og_done = (sem(n) for n in (
            "aff_exp", "aff_done", "pos_done", "onehot_done", "og_done"))
        dve_step, act_step = sem("dve_step"), sem("act_step")
        out_stored = sem("out_stored")
        conv_zero = sem("conv_zero")
        h_hi_done, h_split = sem("h_hi_done"), sem("h_split")
        w2_hi_done, w2_used = sem("w2_hi_done"), sem("w2_used")
        w2_split = [sem(f"w2_split{h}") for h in range(2)]
        hid_step = sem("hid_step")
        mix_hi_done, mix_split = sem("mix_hi_done"), sem("mix_split")
        mix_moved = sem("mix_moved")
        w_hi_done, w_split = sem("w_hi_done"), sem("w_split")
        x_spilled, x_back = sem("x_spilled"), sem("x_back")

        def bank(*key):
            return ps[jobs[key] % BANKS]

        def full_of(eng, *key, turn=0):
            eng.wait_ge(full[jobs[key] % BANKS], jobs[key] // BANKS + 1 + 3 * turn)

        def drained_of(eng, *key, turn=0):
            eng.wait_ge(drained[jobs[key] % BANKS], jobs[key] // BANKS + 1 + 3 * turn)

        def free_for(eng, *key, turn=0):
            if jobs[key] >= BANKS:
                eng.wait_ge(drained[jobs[key] % BANKS], jobs[key] // BANKS + 3 * turn)

        def is_full(*key):
            return full[jobs[key] % BANKS]

        def is_drained(*key):
            return drained[jobs[key] % BANKS]

        def chunk_here(eng, *key, turn=0):
            slot, loads, _, _ = chunks[key]
            eng.wait_ge(loaded[slot], 16 * loads + 96 * turn)
            return slots[slot]

        def norm_index(l, norm):
            return 4 * l + norm

        def kmaj(ap, n):
            return ap.rearrange("(k p) n -> p k n", p=P)

        def vec_rows(ap, n=P):
            return ap.rearrange("(r n) -> r n", n=n)

        def SQ0(l, norm):
            return 36 * l + (0, 12, 20, 28)[norm]

        def SQU(l, norm):
            return 31 * l + (0, 10, 17, 24)[norm]

        def W_TILE(l, kind, *at):
            return 56 * l + (4 * at[0] + at[1] if kind == "win" else 24 + 8 * at[0] + 2 * at[1] + at[2])

        W2_USED = 8 * NE + 4
        SQLN, SQLNU = (8, 44), (7, 38)
        PROBS0 = (0, len(att_units(0)))
        ONEHOT, POS, CONV = (TT, TT + LT), (2, 3), (2 * CT, 3 * CT)

        def GLU(l, t, part):
            return 2 * t + part if l == 0 else 2 * CT + t

        def gather_out(eng, l, k, m, ns, copy):
            dst = xgy[:, 4 * KT * ns:(4 + NE) * KT * ns].rearrange("p (e k s) -> p e k s", k=KT, s=ns)
            full_of(eng, "ga", l, k, m)
            if m < 2:
                dst, cap = dst[:, 8 * m:8 * m + 8, k, 0:CAP[0]], CAP[0]
            else:
                dst, cap = dst[:, :, k, CAP[0]:ns], CAP[1]
            copy(dst, bank("ga", l, k, m)[:, :].rearrange("p (e s) -> p e s", s=cap)) \
                .then_inc(is_drained("ga", l, k, m), 1)

        def y_out(eng, l, e, h, turn, copy):
            ns = sum(CAP) if l == 0 else CAP[0]
            full_of(eng, "y", l, e, h, turn=turn)
            col = turn * (4 * KT * ns) + (e // 2 * D + h * 512)
            r = CAP[0] * (e % 2)
            op = copy(xgy[r:r + CAP[0], bass.ds(col, 512)], bank("y", l, e, h)[0:CAP[0], :])
            if l == 0:
                col = turn * (4 * KT * ns) + (2 * D + h * 512)
                op = copy(xgy[CAP[1] * e:CAP[1] * (e + 1), bass.ds(col, 512)], bank("y", l, e, h)[CAP[0]:ns, :])
            op.then_inc(is_drained("y", l, e, h), 1)

        def y_rows(l, part, p):
            ns = sum(CAP) if l == 0 else CAP[0]
            first = p // 2 * 4 * KT * ns + p % 2 * D if part == 0 else p * 4 * KT * ns + 2 * D
            return xgy[:, first:first + D]

        def w2_quarter(e, h, q):
            return 8 * e + 4 * h + q, slice(2 * q, 2 * q + 2)

        def w2_slot(l, e, h, of):
            return of[chunks["ex", l, e, 4 + h][0]][:, :].rearrange("p (k n) -> p k n", k=KT)

        def upper_parts(eng, l, e, h, turn):
            chunk_here(eng, "ex", l, e, 4 + h, turn=turn)
            for q in range(4):
                n, rows = w2_quarter(e, h, q)
                eng.wait_ge(w2_used, W2_USED * l + n + 1 + 32 * turn)
                eng.activation(w2_hi[:, rows, :], w2_slot(l, e, h, slots)[:, rows, :], ACT.Copy).then_inc(w2_hi_done, 1)

        def lower_parts(eng, l, e, h, turn):
            chunk_here(eng, "ex", l, e, 4 + h, turn=turn)
            for q in range(4):
                n, rows = w2_quarter(e, h, q)
                eng.wait_ge(w2_hi_done, 8 * NE * l + n + 1 + 32 * turn)
                eng.tensor_tensor(w2_slot(l, e, h, slots_lo)[:, rows, :], w2_slot(l, e, h, slots)[:, rows, :],
                                  w2_hi[:, rows, :].bitcast(F32), ALU.subtract).then_inc(w2_split[h], 1)

        def w2_here(eng, l, e, h, q, turn):
            eng.wait_ge(w2_split[h], 4 * NE * l + 4 * e + q + 1 + 16 * turn)

        def w_tile(key, t, rounded):
            slot = chunks[key][0]
            n = 512 if key[0] == "win" else 256
            cols = slice(t * P, (t + 1) * P)
            full32 = slots[slot][:, 0:KT * n].rearrange("p (k n) -> p k n", k=KT)[:, :, cols]
            if not rounded:
                return full32
            lo = slots_lo[slot][:, 0:KT * n].rearrange("p (k n) -> p k n", k=KT)[:, :, cols]
            if key[0] == "win":
                hi = w_hi[t]
            elif t == 0:
                hi = slots_lo[slot][:, 3072:4096].rearrange("p (k n) -> p k n", k=KT)
            else:
                hi = w_hi[slot]
            return hi, lo

        def same_slot(one, other):
            return chunks[one][0] == chunks[other][0]

        def upper_tile(eng, key, t):
            chunk_here(eng, *key)
            if key[0] == "win" and key[2]:
                full_of(eng, "win", key[1], key[2] - 1, t, parts_of(key[1])[-1][0])
            eng.activation(w_tile(key, t, True)[0], w_tile(key, t, False), ACT.Copy).then_inc(w_hi_done, 1)

        def lower_tile(eng, key, t):
            chunk_here(eng, *key)
            eng.wait_ge(w_hi_done, W_TILE(key[1], key[0], *key[2:], t) + 1)
            hi, lo = w_tile(key, t, True)
            eng.tensor_tensor(lo, w_tile(key, t, False), hi.bitcast(F32), ALU.subtract).then_inc(w_split, 1)

        layer_of_stream = {k: (0 if k[0] == "ada" else k[1]) for k in chunks}
        block = ctx.enter_context(nc.Block())

        def slot_view(key, k, n, at=0):
            return slots[chunks[key][0]][:, at:at + k * n].rearrange("p (k n) -> p k n", k=k)

        def expert_src(l, e, m):
            w = A["exp_w1"] if m in (0, 2) else A["exp_w3"] if m in (1, 3) else A["exp_w2"]
            h = m // 2 if m < 4 else m - 4
            return w[l].rearrange("e (k p) n -> e p k n", p=P)[e, :, :, h * 512:(h + 1) * 512]

        def expert_load(eng, l, turn, c):
            (e, m), nxt = divmod(c, 6), divmod(c + 4, 6)
            full_of(eng, *chunks["ex", l, e, m][2], turn=turn)
            eng.dma_start(slot_view(("ex", l, e, m), KT, 512),
                          expert_src(l, 4 * turn + nxt[0], nxt[1])).then_inc(loaded[c % 4], 16)

        def weight_stream(eng, between):
            def slot_free(key):
                prev = chunks[key][3]
                if prev is not None:
                    full_of(eng, *chunks[prev][2])

            for l in range(DEPTH):
                for key in chunks:
                    kind, at = key[0], key[2:]
                    if kind == "ex" or layer_of_stream[key] != l:
                        continue
                    between(key)
                    slot_free(key)
                    here = loaded[chunks[key][0]]
                    if kind == "ada":
                        src = kmaj(A["ada_w"][key[1]][:, at[0] * 512:(at[0] + 1) * 512], 512)
                    elif kind == "win":
                        lo, n = WCHUNKS[at[0]]
                        src = kmaj(A["w_in"][l][:, lo:lo + n], n)
                    elif kind == "wo":
                        src = kmaj(A["w_o"][l][:, at[0] * 512:(at[0] + 1) * 512], 512)
                    else:
                        dp, b = at
                        lo = O_G + b * D + dp * 256
                        eng.dma_start(slot_view(key, KT, 256), kmaj(A["w_in"][l][:, lo:lo + 256], 256)) \
                            .then_inc(here, 16)
                        w = A[("w_a_out", "w_b_out", "w_c_out", "w_d_out")[b]]
                        eng.dma_start(slot_view(key, CT, 256, 2048), kmaj(w[l][:, dp * 256:dp * 256 + 256], 256)) \
                            .then_inc(here, 16)
                        continue
                    eng.dma_start(slot_view(key, KT, src.shape[2]), src).then_inc(here, 16)
                for m in range(4):
                    slot_free(("ex", l, 0, m))
                    if m == 2:
                        full_of(eng, "ga", l, KT - 1, 2 if l == 0 else 1)
                    eng.dma_start(slot_view(("ex", l, 0, m), KT, 512), expert_src(l, 0, m)).then_inc(loaded[m], 16)
                with eng.Fori(0, NE // 4 - 1) as turn:
                    for c in range(0, 24, 2):
                        expert_load(eng, l, turn, c)
                for c in range(0, 20, 2):
                    expert_load(eng, l, NE // 4 - 1, c)

        @block.sync
        def _(sp):
            for i in range(TT):
                src = A["x"][0, i * P:(i + 1) * P, :] if i < LT else A["ctx"][0, (i - LT) * P:(i - LT + 1) * P, :]
                sp.dma_start(x_tok[:, i, :], src).then_inc(x_loaded, 16)

            def tables(key):
                if key[0] == "win" and key[2] == C_F:
                    full_of(sp, "win", key[1], C_Q, CT - 1, parts_of(key[1])[-1][0])
                    sp.dma_start(hb2[:, 0:5376], K["dft"]).then_inc(dft_loaded, 16)

            weight_stream(sp, tables)
            for i in range(LT):
                drained_of(sp, "out", i, 0)
                drained_of(sp, "out", i, 1)
                sp.dma_start(out[0, i * P:(i + 1) * P, :], h_tok[:, i, :]).then_inc(out_stored, 16)
            sp.wait_ge(out_stored, 16 * LT)

        @block.gpsimd
        def _(pool):
            pool.memset(eps_t, EPS).then_inc(set_up, 1)

            for l in range(DEPTH):
                if l:
                    full_of(pool, "rl", l - 1)
                pool.dma_start(rw, kmaj(A["router_w"][l], NE)).then_inc(rw_loaded, 16)
                both = parts_of(l)
                if l:
                    pool.wait_ge(x_updated, 8 * 2 * l)
                else:
                    for i in range(TT):
                        for h in range(2):
                            drained_of(pool, "xin", i, h)
                n = TOK if l == 0 else SEQ
                pool.dma_start(x_dram[:, :, 0:n], x_t[:, :, 0:n]).then_inc(x_spilled, 16)
                for k in range(KT):
                    pool.wait_ge(mix_hi_done, KT * l + k + 1)
                    if k == 0:
                        pool.wait_ge(x_spilled, 16 * (l + 1))
                    pool.tensor_tensor(mix_lo[:, k, :], h_t[:, k, :], mix_hi1[:, k, :].bitcast(F32), ALU.subtract) \
                        .then_inc(mix_split, 1)
                for c in range(C_KV):
                    for t in range(CT):
                        lower_tile(pool, ("win", l, c), t)
                for dp in range(KT // 2):
                    for b in range(4):
                        for t in range(2):
                            lower_tile(pool, ("mg", l, dp, b), t)
                full_of(pool, "g", l, KT // 2 - 1, 3, 1, both[-1][0])
                pool.dma_start(x_t[:, :, 0:n], x_dram[:, :, 0:n]).then_inc(x_back, 16)
                nt, last = (TT, 2) if l == 0 else (LT, 1)
                for i in range(nt):
                    pool.wait_ge(h_hi_done, TT * l + i + 1)
                    pool.tensor_tensor(h_lo[:, i, :], h_tok[:, i, :], h_hi[:, i, :].bitcast(F32), ALU.subtract) \
                        .then_inc(h_split, 1)
                full_of(pool, "ga", l, KT - 1, last)
                pool.memset(spare, 0.0).then_inc(w2_used, 4)
                with pool.Fori(0, NE // 4) as turn:
                    for e in range(4):
                        lower_parts(pool, l, e, 0, turn)

        @block.tensor
        def _(pe):
            def chan_sum(l, norm, job, weights, tiles, parts, ready):
                for part in parts:
                    free_for(pe, job, *norm, part[0])
                for k in range(tiles):
                    ready(k)
                    for part in parts:
                        mm = pe.matmul(bank(job, *norm, part[0])[:, 0:part[2]], weights,
                                       sq[k % 2][:, part[1]:part[1] + part[2]], start=(k == 0), stop=(k == tiles - 1))
                        if k == tiles - 1:
                            mm.then_inc(is_full(job, *norm, part[0]), 1)
                    if k < tiles - 1:
                        mm.then_inc(sq_used, 1)

            def mean_square(l, norm):
                ni = norm_index(l, norm)
                chan_sum(l, (l, norm), "ms", ones_d, KT, parts_of(l, norm),
                         lambda k: pe.wait_ge(sq_ready, SQ0(l, norm) + k + 1))

            def product(key, wt, k_tiles, rhs, n, first=True):
                free_for(pe, *key)
                for k in range(k_tiles):
                    mm = pe.matmul(bank(*key)[:, 0:n], wt(k), rhs(k), start=(k == 0), stop=(k == k_tiles - 1))
                mm.then_inc(is_full(*key), 1)

            def split_product(key, w, h, n, ready=None):
                (w_up, w_low), (h_up, h_low) = w, h
                free_for(pe, *key)
                for k in range(KT):
                    if ready:
                        ready(k)
                    out_ = bank(*key)[:, 0:n]
                    pe.matmul(out_, w_up[:, k, :], h_up(k), start=(k == 0), stop=False)
                    pe.matmul(out_, w_up[:, k, :], h_low(k), start=False, stop=False)
                    mm = pe.matmul(out_, w_low[:, k, :], h_up(k), start=False, stop=(k == KT - 1))
                mm.then_inc(is_full(*key), 1)

            pe.wait_ge(const_loaded, 16 * 8)
            pe.wait_ge(x_loaded, 16 * TT)
            for i in range(TT):
                for h in range(2):
                    free_for(pe, "xin", i, h)
                    for k in range(4):
                        mm = pe.transpose(bank("xin", i, h)[:, k * P:(k + 1) * P],
                                          x_tok[:, i, (4 * h + k) * P:(4 * h + k + 1) * P], ident)
                    mm.then_inc(is_full("xin", i, h), 1)
            pe.wait_ge(par_loaded, 16 * 25)
            for l in range(DEPTH):
                for r, n in enumerate((NR1, NR2, NR3)):
                    free_for(pe, "par", l, r)
                    pe.transpose(bank("par", l, r)[:, 0:n], par_rows[0:n, 3 * l + r, :], ident[0:n, 0:n]) \
                        .then_inc(is_full("par", l, r), 1)
            free_for(pe, "cin", 0)
            pe.transpose(bank("cin", 0)[:, 0:2 * KT], par_rows[0:2 * KT, 6, :], ident[0:2 * KT, 0:2 * KT]) \
                .then_inc(is_full("cin", 0), 1)
            drained_of(pe, "cin", 0)

            def modulation(*key):
                if key not in MOD_AFTER:
                    return
                l, c = MOD_AFTER[key]
                w = chunk_here(pe, "ada", l, c).rearrange("p (k n) -> p k n", k=KT)
                free_for(pe, "mod", l, c)
                for t in range(4):
                    for k in range(KT):
                        mm = pe.matmul(bank("mod", l, c)[:, 2 * t:2 * t + 2], w[:, k, t * P:(t + 1) * P],
                                       c_t[:, 2 * k:2 * k + 2], start=(k == 0), stop=(k == KT - 1))
                mm.then_inc(is_full("mod", l, c), 1)

            def layer(l):
                both = parts_of(l)
                mean_square(l, PRE_MIX)
                if l == 0:
                    for c in range(MOD_FIRST):
                        w = chunk_here(pe, "ada", l, c).rearrange("p (k n) -> p k n", k=KT)
                        key = ("mrow", l, c)
                        free_for(pe, *key)
                        for k in range(KT):
                            mm = pe.matmul(bank(*key)[0:2, :], c_t[:, 2 * k:2 * k + 2], w[:, k, :],
                                           start=(k == 0), stop=(k == KT - 1))
                        mm.then_inc(is_full(*key), 1)
                        free_for(pe, "mod", l, c)
                        drained_of(pe, *key)
                        for t in range(4):
                            mm = pe.transpose(bank("mod", l, c)[:, 2 * t:2 * t + 2],
                                              mod_rows[:, c * 512 + t * P:c * 512 + (t + 1) * P], ident[0:2, 0:2])
                        mm.then_inc(is_full("mod", l, c), 1)
                for c in range(C_KV):
                    for t in range(CT):
                        pe.wait_ge(w_split, W_TILE(l, "win", c, t) + 1)
                        for part in both:
                            cols = slice(part[1], part[1] + part[2])
                            first = c == 0 and t == 0 and part is LAT
                            split_product(("win", l, c, t, part[0]), w_tile(("win", l, c), t, True),
                                          (lambda k: mix_hi1[:, k, cols], lambda k: mix_lo[:, k, cols]), part[2],
                                          (lambda k: pe.wait_ge(mix_split, KT * l + k + 1)) if first else None)
                        if c == C_Q:
                            drained_of(pe, "win", l, c, t, 0)
                            product(("rope", l, t), lambda k: perm, 1, lambda k: q_t[:, t, 0:SEQ], SEQ)
                    modulation("win", l, c)
                pe.wait_ge(h_ready, 8 * (2 * l + 1))
                w = chunk_here(pe, "win", l, C_KV)[:, 0:KT * 256].rearrange("p (k n) -> p k n", k=KT)
                for part in (LAT, CON):
                    product(("k", l, part[0]), lambda k: w[:, k, 0:P], KT,
                            lambda k: h_t[:, k, part[1]:part[1] + part[2]], part[2])
                drained_of(pe, "k", l, 0)
                product(("rope", l, CT), lambda k: perm, 1, lambda k: k_t[:, 0, 0:SEQ], SEQ)
                for part, first, n in ((0, 0, LT), (1, LT, CTT)):
                    free_for(pe, "v", l, part)
                    for i in range(n):
                        for k in range(KT):
                            mm = pe.matmul(bank("v", l, part)[:, i * P:(i + 1) * P],
                                           h_t[:, k, (first + i) * P:(first + i + 1) * P], w[:, k, P:2 * P],
                                           start=(k == 0), stop=(k == KT - 1))
                    mm.then_inc(is_full("v", l, part), 1)
                modulation("win", l, C_KV)
                w = chunk_here(pe, "win", l, C_F).rearrange("p (k n) -> p k n", k=KT)
                for i in range(TT if l == 0 else LT):
                    product(("f", l, i), lambda k: h_t[:, k, i * P:(i + 1) * P], KT, lambda k: w[:, k, :], DC)
                modulation("win", l, C_F)
                pe.wait_ge(dft_loaded, 16 * (l + 1))

                def fourier_out(g):
                    for part in both:
                        drained_of(pe, "fc", l, g, part[0])
                        drained_of(pe, "fs", l, g, part[0])
                        key = ("fo", l, g, part[0])
                        free_for(pe, *key)
                        cols = slice(part[1], part[1] + part[2])
                        pe.matmul(bank(*key)[:, 0:part[2]], c128, xc[g % 2][:, cols], start=True, stop=False)
                        pe.matmul(bank(*key)[:, 0:part[2]], s128, xs[g % 2][:, cols], start=False, stop=True) \
                            .then_inc(is_full(*key), 1)

                drained_of(pe, "f", l, (TT if l == 0 else LT) - 1)
                drained_of(pe, "f", l, (TT if l == 0 else LT) - 2)
                for g in range(CT):
                    for part in both:
                        first, n = (0, LT) if part[0] == 0 else (LT, CTT)
                        tabs = (c512, s512) if part[0] == 0 else (c256, s256)
                        for name, tab in zip(("fc", "fs"), tabs):
                            product((name, l, g, part[0]), lambda k: f_tok[:, first + k, g * P:(g + 1) * P], n,
                                    lambda k: tab[:, k, :], part[2])
                    if g:
                        fourier_out(g - 1)
                fourier_out(CT - 1)
                units = att_units(l)
                pe.wait_ge(rope_done, 5 * (l + 1))
                pe.wait_ge(swapped, 2 * (l + 1))
                for t in range(CT):
                    if l == 0:
                        drained_of(pe, "win", l, C_Q, t, 1)
                drained_of(pe, "v", l, 0)
                drained_of(pe, "v", l, 1)

                def scores(u):
                    con, n, g = units[u]
                    lo, hi, _ = band(units[u])
                    col = SEQ * con + n * P
                    for h in range(GRP):
                        head = GRP * g + h
                        r = HD * (head % 2)
                        keys = k_t[r:r + HD, 0 if head % 2 == g else 1, :]
                        q = q_t[r:r + HD, head // 2, col:col + P]
                        if not con:
                            key = ("sl", l, u, h)
                            free_for(pe, *key)
                            pe.matmul(bank(*key)[:, 0:(hi - lo) * P], q, keys[:, lo * P:hi * P],
                                      start=True, stop=True).then_inc(is_full(*key), 1)
                        key = ("sc", l, u, h)
                        free_for(pe, *key)
                        pe.matmul(bank(*key)[:, 0:CTX], q, keys[:, SEQ:TOK],
                                  start=True, stop=True).then_inc(is_full(*key), 1)

                def values(u):
                    con, n, g = units[u]
                    lo, hi, nk = band(units[u])
                    tiles = list(range(lo, hi)) + list(range(LT, TT))
                    for kt in range(nk):
                        free_for(pe, "pt", l, u, kt)
                        if kt == 0:
                            pe.wait_ge(probs_done, PROBS0[l] + u + 1)
                        for h in range(GRP):
                            mm = pe.transpose(bank("pt", l, u, kt)[:, h * P:(h + 1) * P],
                                              S_buf[u % 2][:, h, kt * P:(kt + 1) * P], ident)
                        mm.then_inc(is_full("pt", l, u, kt), 1)
                    free_for(pe, "av", l, u)
                    for kt in range(nk):
                        drained_of(pe, "pt", l, u, kt)
                        mm = pe.matmul(bank("av", l, u)[0:HD, :], v_tok[:, tiles[kt], g * HD:(g + 1) * HD],
                                       probs_t[:, kt, :], start=(kt == 0), stop=(kt == nk - 1))
                    mm.then_inc(is_full("av", l, u), 1)

                scores(0)
                for u in range(len(units)):
                    if u + 1 < len(units):
                        scores(u + 1)
                    values(u)
                pe.wait_ge(conv_done, CONV[l])
                for part in both:
                    product(("lm", l, part[0]), lambda k: ones_c, CT,
                            lambda k: a_t[:, k, part[1]:part[1] + part[2]], part[2])
                chan_sum(l, (l,), "lv", ones_c, CT, both, lambda k: pe.wait_ge(sq_ready, SQLN[l] + k + 1))
                srcs = (a_t, b_t, q_t, None)
                for dp in range(KT // 2):
                    for b in range(4):
                        w = chunk_here(pe, "mg", l, dp, b)
                        wb = w[:, 2048:3072].rearrange("p (k n) -> p k n", k=CT)
                        if dp == 0 and b == 0:
                            pe.wait_ge(mix_moved, KT * (l + 1))
                            pe.wait_ge(a_done, 4 * (l + 1))
                            pe.wait_ge(short_done, 4 * (l + 1))
                            for u in range(len(units) - 2, len(units)):
                                drained_of(pe, "av", l, u)
                            for part in both:
                                drained_of(pe, "fo", l, CT - 1, part[0])
                        for t in range(2):
                            pe.wait_ge(w_split, W_TILE(l, "mg", dp, b, t) + 1)
                            for part in both:
                                cols = slice(part[1], part[1] + part[2])
                                split_product(("g", l, dp, b, t, part[0]), w_tile(("mg", l, dp, b), t, True),
                                              (lambda k: mix_hi2[:, k, cols], lambda k: mix_lo[:, k, cols]), part[2])
                                if b < 3:
                                    rhs = lambda k: srcs[b][:, k, cols]
                                else:
                                    i0, i1 = (0, LT) if part[0] == 0 else (LT, TT)
                                    rhs = lambda k: f_tok[:, i0:i1, k * P:(k + 1) * P]
                                product(("w", l, dp, b, t, part[0]), lambda k: wb[:, k, t * P:(t + 1) * P], CT,
                                        rhs, part[2])
                        modulation("mg", l, dp, b)
                pe.wait_ge(merged, (l + 1) * 8)
                for h in range(2):
                    w = chunk_here(pe, "wo", l, h).rearrange("p (k n) -> p k n", k=KT)
                    for t in range(4):
                        for part in both:
                            product(("wo", l, 4 * h + t, part[0]), lambda k: w[:, k, t * P:(t + 1) * P], KT,
                                    lambda k: y_t[:, k, part[1]:part[1] + part[2]], part[2])
                mean_square(l, POST_MIX)
                mean_square(l, PRE_FFN)
                nt = TT if l == 0 else LT
                pe.wait_ge(h_ready, 8 * (2 * l + 2))
                pe.wait_ge(rw_loaded, 16 * (l + 1))
                free_for(pe, "rl", l)
                for i in range(nt):
                    for k in range(KT):
                        mm = pe.matmul(bank("rl", l)[:, i * NE:(i + 1) * NE], h_t[:, k, i * P:(i + 1) * P],
                                       rw[:, k, :], start=(k == 0), stop=(k == KT - 1))
                mm.then_inc(is_full("rl", l), 1)
                for key, lo, hi in ((("at", l, 0), 0, LT), (("at", l, 1), LT, TT)):
                    if key in jobs:
                        free_for(pe, *key)
                        pe.wait_ge(aff_done, l + 1)
                        for i in range(lo, hi):
                            mm = pe.transpose(bank(*key)[0:NE, (i - lo) * P:(i - lo + 1) * P], aff[:, i, :], ident)
                        mm.then_inc(is_full(*key), 1)
                for i in range(nt):
                    for h in range(2):
                        free_for(pe, "ht", l, i, h)
                        for k in range(4):
                            mm = pe.transpose(bank("ht", l, i, h)[:, k * P:(k + 1) * P],
                                              h_t[:, 4 * h + k, i * P:(i + 1) * P], ident)
                        mm.then_inc(is_full("ht", l, i, h), 1)
                free_for(pe, "pos", l)
                pe.wait_ge(pos_done, POS[l])
                for i in range(nt):
                    mm = pe.transpose(bank("pos", l)[:, i * NE:(i + 1) * NE], sel_e[0:NE, 3, i * P:(i + 1) * P],
                                      ident[0:NE, 0:NE])
                mm.then_inc(is_full("pos", l), 1)
                for i in range(nt):
                    for h in range(2):
                        drained_of(pe, "ht", l, i, h)
                pe.wait_ge(onehot_done, ONEHOT[l])
                pe.wait_ge(h_split, TT * l + nt)
                for k in range(KT):
                    for m in range(3 if l == 0 else 2):
                        sel = onehot_r[0][:, :, m * 512:(m + 1) * 512] if m < 2 else onehot_r[1]
                        first = 0 if m < 2 else LT
                        product(("ga", l, k, m),
                                lambda i: (h_hi, h_lo)[i % 2][:, first + i // 2, k * P:(k + 1) * P],
                                2 * (LT if m < 2 else CTT), lambda i: sel[:, i // 2, :], 512)
                for m in range(3 if l == 0 else 2):
                    for k in range(KT - 3, KT):
                        drained_of(pe, "ga", l, k, m)
                ns = sum(CAP) if l == 0 else CAP[0]

                with pe.Fori(0, NE // 4) as turn:
                    for e in range(4):
                        for h in range(2):
                            for m, name in enumerate(("h1", "h3")):
                                w = chunk_here(pe, "ex", l, e, 2 * h + m, turn=turn) \
                                    .rearrange("p (k n) -> p k n", k=KT)
                                free_for(pe, name, l, e, h, turn=turn)
                                for f in range(4):
                                    for k in range(KT):
                                        x0 = (turn * 4 + (e + 4)) * (KT * ns) + k * ns
                                        mm = pe.matmul(bank(name, l, e, h)[:, f * ns:(f + 1) * ns],
                                                       w[:, k, f * P:(f + 1) * P], xgy[:, bass.ds(x0, ns)],
                                                       start=(k == 0), stop=(k == KT - 1))
                                mm.then_inc(is_full(name, l, e, h), 1)
                        for h in range(2):
                            lo = slots_lo[chunks["ex", l, e, 4 + h][0]][:, :].rearrange("p (k n) -> p k n", k=KT)
                            y = bank("y", l, e, h)[:, :]
                            free_for(pe, "y", l, e, h, turn=turn)
                            for f in range(KT):
                                if f % 2 == 0:
                                    w2_here(pe, l, e, h, f // 2, turn)
                                if h == 0 and f in (0, 3):
                                    drained_of(pe, "h3", l, e, f // 3, turn=turn)
                                at_f = slice(f * ns, f * ns + P)
                                pe.matmul(y, hid_hi[:, at_f], w2_hi[:, f, :], start=(f == 0), stop=False)
                                mm = pe.matmul(y, hid_lo[:, at_f], w2_hi[:, f, :], start=False, stop=False)
                                if f % 2:
                                    mm.then_inc(w2_used, 1)
                                mm = pe.matmul(y, hid_hi[:, at_f], lo[:, f, :], start=False, stop=(f == KT - 1))
                            mm.then_inc(is_full("y", l, e, h), 1)
                pe.wait_ge(og_done, ONEHOT[l])
                for part, npair, ntile, in ((0, NE // 2, LT), (1, NE // 4, CTT))[:len(both)]:
                    for p in range(npair):
                        key = ("sg", l, p, part)
                        free_for(pe, *key)
                        for i in range(ntile):
                            mm = pe.transpose(bank(*key)[:, i * P:(i + 1) * P],
                                              onehot[part][:, i, p * P:(p + 1) * P], ident)
                        mm.then_inc(is_full(*key), 1)
                for part, npair in ((0, NE // 2), (1, NE // 4))[:len(both)]:
                    for p in range(npair):
                        drained_of(pe, "sg", l, p, part)
                for h in range(2):
                    drained_of(pe, "y", l, NE - 1, h)
                    drained_of(pe, "y", l, NE - 2, h)
                for k in range(KT):
                    for part in both:
                        product(("mo", l, k, part[0]),
                                lambda p: y_rows(l, part[0], p)[:, k * P:(k + 1) * P],
                                (NE // 2, NE // 4)[part[0]], lambda p: sg[part[0]][:, p, :], part[2])
                mean_square(l, POST_FFN)

            for l in range(DEPTH):
                layer(l)
            pe.wait_ge(x_updated, 8 * 2 * DEPTH)
            for i in range(LT):
                for h in range(2):
                    free_for(pe, "out", i, h)
                    for k in range(4):
                        mm = pe.transpose(bank("out", i, h)[:, k * P:(k + 1) * P],
                                          x_t[:, 4 * h + k, i * P:(i + 1) * P], ident)
                    mm.then_inc(is_full("out", i, h), 1)

        @block.scalar
        def _(act):
            steps = [0]

            def link(ins):
                steps[0] += 1
                ins.then_inc(act_step, 1)
                act.wait_ge(act_step, steps[0])

            def squares(l, norm, src, ready):
                base = SQ0(l, norm)
                for k in range(KT):
                    ready(k)
                    if k >= 2:
                        act.wait_ge(sq_used, SQU(l, norm) + k - 1)
                    n = TOK if len(parts_of(l, norm)) == 2 else SEQ
                    act.activation(sq[k % 2][:, 0:n], src[:, k, 0:n], ACT.Square).then_inc(sq_ready, 1)
                roots(("ms", l, norm), parts_of(l, norm))

            def roots(key, parts):
                for part in parts:
                    full_of(act, *key, part[0])
                    act.activation(rb[:, part[1]:part[1] + part[2]], bank(*key, part[0])[:, 0:part[2]], ACT.Sqrt,
                                   bias=eps_t).then_inc(is_drained(*key, part[0]), 1)

            def modulated(l, norm):
                mix = norm == PRE_MIX
                pi = 2 * l + (0 if mix else 1)
                for k in range(KT):
                    act.wait_ge(xr_ready, 8 * pi + k + 1)
                    parts = parts_of(l, norm)
                    for part in parts:
                        w, cols = part[0], slice(part[1], part[1] + part[2])
                        op = act.activation(h_t[:, k, cols], sq[k % 2][:, cols], ACT.Identity,
                                            scale=scl[l][:, 0 if mix else 2, k, w:w + 1],
                                            bias=mods[l][:, (0 if mix else 24) + k, w:w + 1])
                    op.then_inc(h_ready, 1)
                    if mix:
                        if k == 4:
                            for t in range(CT):
                                upper_tile(act, ("win", l, 0), t)
                        act.wait_ge(h_ready, 8 * pi + k + 1)
                        act.activation(mix_hi1[:, k, :], h_t[:, k, :], ACT.Copy).then_inc(mix_hi_done, 1)

            for dst, src in ((ident, "ident"), (ones_d, "ones_d"), (ones_c, "ones_c"), (perm, "perm"),
                             (cosT, "cos"), (sinT, "sin"), (maskT, "mask"), (iota, "iota")):
                act.dma_start(dst, K[src]).then_inc(const_loaded, 16)
            for l in range(DEPTH):
                r = 3 * l
                for row, name, n in ((R_ADAB, "ada_b", 48), (R_PM, "pre_mix_g", 8), (R_QM, "post_mix_g", 8),
                                     (R_PF, "pre_ffn_g", 8), (R_QF, "post_ffn_g", 8), (R_GB, "gate_b", 32),
                                     (R_CB, "conv_a_b", 4), (R_LG, "ln_a_g", 4), (R_LB, "ln_a_b", 4)):
                    act.dma_start(par_rows[row:row + n, r, :], vec_rows(A[name][l])).then_inc(par_loaded, 16)
                act.dma_start(par_rows[0:NR2, r + 1, :],
                              A["conv_a_w"][l].rearrange("k (t n) -> (k t) n", n=P)).then_inc(par_loaded, 16)
                act.dma_start(par_rows[0:NR3, r + 2, :],
                              A["conv_b_w"][l].rearrange("k (t n) -> (k t) n", n=P)).then_inc(par_loaded, 16)
            act.dma_start(par_rows[0:KT, 6, :], vec_rows(A["c"][0])).then_inc(par_loaded, 16)
            act.dma_start(par_rows[KT:2 * KT, 6, :], vec_rows(A["c_ctx"])).then_inc(par_loaded, 16)
            act.dma_start(nsink, A["sink"].rearrange("(a l) h -> a (l h)", a=1).broadcast_to([P, DEPTH * HEADS])) \
                .then_inc(par_loaded, 16)
            act.wait_ge(set_up, 1)
            for i in range(TT):
                full_of(act, "xin", i, 0)
                act.activation(x_t[:, 0:4, i * P:(i + 1) * P],
                               bank("xin", i, 0)[:, :].rearrange("p (k t) -> p k t", k=4), ACT.Copy) \
                    .then_inc(is_drained("xin", i, 0), 1)
            full_of(act, "cin", 0)
            act.activation(c_t.rearrange("p (k w) -> p w k", w=2),
                           bank("cin", 0)[:, 0:2 * KT].rearrange("p (w k) -> p w k", w=2), ACT.Silu) \
                .then_inc(is_drained("cin", 0), 1)

            def layer(l):
                both = parts_of(l)

                def ready0(k):
                    if l == 0 and k == 0:
                        for i in range(TT):
                            drained_of(act, "xin", i, 0)
                            drained_of(act, "xin", i, 1)
                    if l:
                        act.wait_ge(x_updated, 8 * (2 * l - 1) + k + 1)

                squares(l, PRE_MIX, x_t, ready0)
                if l == 0:
                    for c in range(MOD_FIRST):
                        full_of(act, "mrow", l, c)
                        act.activation(mod_rows[:, c * 512:(c + 1) * 512], bank("mrow", l, c)[0:2, :], ACT.Copy) \
                            .then_inc(is_drained("mrow", l, c), 1)
                modulated(l, PRE_MIX)
                act.wait_ge(conv_zero, l + 1)
                for c in range(C_KV):
                    if c and same_slot(("win", l, c - 1), ("win", l, c)):
                        for t in range(CT):
                            upper_tile(act, ("win", l, c), t)
                    for t in range(CT):
                        for part in both:
                            key = ("win", l, c, t, part[0])
                            n = part[2]
                            src = bank(*key)[:, 0:n]
                            if c == C_HV:
                                continue
                            full_of(act, *key)
                            fn = ACT.Copy
                            if c == C_AV:
                                dst = cpad[:, t, PADC[0] * part[0] + HC:PADC[0] * part[0] + HC + n]
                            elif c == C_AG:
                                j = GLU(l, t, part[0])
                                if j >= 2:
                                    act.wait_ge(glu_done, j - 1)
                                dst, fn = sq[j % 2][:, 0:n], ACT.Sigmoid
                            elif c == C_BG:
                                dst = b_t[:, t, part[1]:part[1] + n]
                            elif c == C_CG:
                                dst = bpad[:, t, PADS[0] * part[0] + HS:PADS[0] * part[0] + HS + n]
                            else:
                                dst = q_t[:, t, part[1]:part[1] + n]
                            act.activation(dst, src, fn).then_inc(is_drained(*key), 1)
                        if c + 1 < C_KV and not same_slot(("win", l, c), ("win", l, c + 1)):
                            upper_tile(act, ("win", l, c + 1), t)
                for part in (LAT, CON):
                    full_of(act, "k", l, part[0])
                    act.activation(k_t[:, 0, part[1]:part[1] + part[2]], bank("k", l, part[0])[:, 0:part[2]],
                                   ACT.Copy).then_inc(is_drained("k", l, part[0]), 1)
                for part, first, n in ((0, 0, LT), (1, LT, CTT)):
                    full_of(act, "v", l, part)
                    act.activation(v_tok[:, first:first + n, :],
                                   bank("v", l, part)[:, 0:n * P].rearrange("p (i n) -> p i n", n=P),
                                   ACT.Copy).then_inc(is_drained("v", l, part), 1)
                for i in range(TT if l == 0 else LT):
                    full_of(act, "f", l, i)
                    act.activation(f_tok[:, i, :], bank("f", l, i)[:, :], ACT.Copy) \
                        .then_inc(is_drained("f", l, i), 1)

                def fourier_out(g):
                    for part in both:
                        key = ("fo", l, g, part[0])
                        i0, i1 = (0, LT) if part[0] == 0 else (LT, TT)
                        full_of(act, *key)
                        act.activation(f_tok[:, i0:i1, g * P:(g + 1) * P],
                                       bank(*key)[:, 0:part[2]].rearrange("p (i n) -> p i n", n=P), ACT.Copy,
                                       ).then_inc(is_drained(*key), 1)

                act.wait_ge(short_done, 4 * (l + 1))
                for g in range(CT):
                    for part in both:
                        cols = slice(part[1], part[1] + part[2])
                        for name, dst in (("fc", xc), ("fs", xs)):
                            full_of(act, name, l, g, part[0])
                            act.activation(dst[g % 2][:, cols], bank(name, l, g, part[0])[:, 0:part[2]], ACT.Copy) \
                                .then_inc(is_drained(name, l, g, part[0]), 1)
                    if g:
                        fourier_out(g - 1)
                fourier_out(CT - 1)
                units = att_units(l)

                def ctx_scores(u):
                    lo, hi, nk = band(units[u])
                    nl = (hi - lo) * P
                    if u == 0:
                        full_of(act, "fo", l, CT - 1, both[-1][0])
                    for h in range(GRP):
                        full_of(act, "sc", l, u, h)
                        if u >= 2 and h == 0:
                            full_of(act, "pt", l, u - 2, band(units[u - 2])[2] - 1)
                        act.activation(S_buf[u % 2][:, h, nl:nl + CTX], bank("sc", l, u, h)[:, 0:CTX], ACT.Copy) \
                            .then_inc(is_drained("sc", l, u, h), 1)

                def exps(u):
                    nk = band(units[u])[2]
                    g = units[u][2]
                    act.wait_ge(stats_done, PROBS0[l] + u + 1)
                    act.activation(st[:, 4, :], st[:, 2, :], ACT.Exp).then_inc(exps_done, 1)
                    for h in range(GRP):
                        S = S_buf[u % 2][:, h, 0:nk * P]
                        act.activation(S, S, ACT.Exp, bias=st[:, 1, h:h + 1], scale=HD ** -0.5,
                                       accum_out=st[:, 3, h:h + 1]).then_inc(exps_done, 1)

                def turned(u):
                    con, n, g = units[u]
                    nk = band(units[u])[2]
                    for kt in range(nk):
                        if kt % 2 == 0:
                            full_of(act, "pt", l, u, kt)
                            if u:
                                full_of(act, "av", l, u - 1)
                            act.activation(probs_t[:, kt, :], bank("pt", l, u, kt)[:, :], ACT.Copy) \
                                .then_inc(is_drained("pt", l, u, kt), 1)
                    full_of(act, "av", l, u)
                    o = bank("av", l, u)[0:HD, :].rearrange("p (h r q) -> p r h q", r=2, q=P)
                    col = SEQ * con + n * P
                    act.activation(q_t[0:HD, 2 * g:2 * g + 2, col:col + P], o[:, 0], ACT.Copy)
                    act.activation(q_t[HD:P, 2 * g:2 * g + 2, col:col + P], o[:, 1], ACT.Copy) \
                        .then_inc(is_drained("av", l, u), 1)

                ctx_scores(0)
                for u in range(len(units)):
                    exps(u)
                    if u + 1 < len(units):
                        ctx_scores(u + 1)
                    turned(u)
                    if u < KT:
                        n = TOK if l == 0 else SEQ
                        act.activation(mix_hi2[:, u, 0:n], h_t[:, u, 0:n], ACT.Copy).then_inc(mix_moved, 1)
                for t in range(2):
                    upper_tile(act, ("mg", l, 0, 0), t)
                for k in range(CT):
                    if k < CT - 1:
                        act.wait_ge(centred, (CT - 1) * l + k + 1)
                    else:
                        for part in both:
                            drained_of(act, "lm", l, part[0])
                    if k >= 2:
                        act.wait_ge(sq_used, SQLNU[l] + k - 1)
                    n = TOK if l == 0 else SEQ
                    act.activation(sq[k % 2][:, 0:n], a_t[:, k, 0:n], ACT.Square).then_inc(sq_ready, 1)
                roots(("lv", l), both)
                for k in range(CT):
                    act.wait_ge(lnorm_done, CT * l + k + 1)
                    n = TOK if l == 0 else SEQ
                    act.activation(a_t[:, k, 0:n], a_t[:, k, 0:n], ACT.Silu, scale=par[l][:, R_LG + k:R_LG + k + 1],
                                   bias=par[l][:, R_LB + k:R_LB + k + 1]).then_inc(a_done, 1)
                gate_chunks = [("mg", l, dp, b) for dp in range(KT // 2) for b in range(4)]
                for dp in range(KT // 2):
                    for b in range(4):
                        i = 4 * dp + b
                        if i and same_slot(*gate_chunks[i - 1:i + 1]):
                            for t in range(2):
                                upper_tile(act, gate_chunks[i], t)
                        for t in range(2):
                            if t and i < 15 and not same_slot(*gate_chunks[i:i + 2]):
                                for tt in range(2):
                                    upper_tile(act, gate_chunks[i + 1], tt)
                            for part in both:
                                key = ("g", l, dp, b, t, part[0])
                                full_of(act, *key)
                                j = b * 2 + t
                                back = [(d, bb, tt) for d in range(KT // 2) for bb in range(4) for tt in range(2)]
                                at_ = back.index((dp, b, t))
                                if at_ >= 2:
                                    drained_of(act, "w", l, *back[at_ - 2], part[0])
                                col = R_GB + b * KT + 2 * dp + t
                                act.activation(sq[at_ % 2][:, part[1]:part[1] + part[2]], bank(*key)[:, 0:part[2]],
                                               ACT.Sigmoid, bias=par[l][:, col:col + 1]) \
                                    .then_inc(is_drained(*key), 1)
                for t in range(KT):
                    for part in both:
                        full_of(act, "wo", l, t, part[0])
                        act.activation(yo_t[:, t, part[1]:part[1] + part[2]], bank("wo", l, t, part[0])[:, 0:part[2]],
                                       ACT.Copy).then_inc(is_drained("wo", l, t, part[0]), 1)

                def ready1(k):
                    for part in both:
                        drained_of(act, "wo", l, k, part[0])
                        if k == 0:
                            for t in range(2):
                                drained_of(act, "w", l, KT // 2 - 1, 3, t, part[0])

                squares(l, POST_MIX, yo_t, ready1)
                squares(l, PRE_FFN, x_t, lambda k: act.wait_ge(x_updated, 8 * 2 * l + k + 1))
                modulated(l, PRE_FFN)
                nt = TT if l == 0 else LT
                drained_of(act, "rl", l)
                act.activation(aff[:, 0:nt, :], aff[:, 0:nt, :], ACT.Exp).then_inc(aff_exp, 1)
                for i in range(nt):
                    for h in range(2):
                        full_of(act, "ht", l, i, h)
                        act.activation(h_tok[:, i, 512 * h:512 * (h + 1)], bank("ht", l, i, h)[:, :], ACT.Copy) \
                            .then_inc(is_drained("ht", l, i, h), 1)
                for i in range(nt):
                    for h in range(2):
                        drained_of(act, "ht", l, i, h)
                    act.activation(h_hi[:, i, :], h_tok[:, i, :], ACT.Copy).then_inc(h_hi_done, 1)
                ns = sum(CAP) if l == 0 else CAP[0]
                for k in range(KT):
                    gather_out(act, l, k, 0, ns, lambda o, i: act.activation(o, i, ACT.Copy))
                    if l == 0:
                        gather_out(act, l, k, 2, ns, lambda o, i: act.activation(o, i, ACT.Copy))
                def experts(turn, loads):
                    for e in range(4):
                        for h in range(2):
                            full_of(act, "h1", l, e, h, turn=turn)
                            if e:
                                drained_of(act, "h3", l, e - 1, h, turn=turn)
                            else:
                                drained_of(act, "h3", l, 3, h, turn=turn - 1)
                            act.activation(silu_t[h][:, 0:4 * ns], bank("h1", l, e, h)[:, 0:4 * ns], ACT.Silu) \
                                .then_inc(is_drained("h1", l, e, h), 1)
                            if 6 * e + 2 * h + 1 < loads:
                                expert_load(act, l, turn, 6 * e + 2 * h + 1)
                            upper_parts(act, l, e, h, turn)
                        y_out(act, l, e, 0, turn, lambda o, i: act.activation(o, i, ACT.Copy))
                        if 6 * e + 5 < loads:
                            expert_load(act, l, turn, 6 * e + 5)

                with act.Fori(0, NE // 4 - 1) as turn:
                    experts(turn, 24)
                experts(NE // 4 - 1, 20)
                for part, npair in ((0, NE // 2), (1, NE // 4))[:len(both)]:
                    for p in range(0, npair, 2):
                        full_of(act, "sg", l, p, part)
                        act.activation(sg[part][:, p, :], bank("sg", l, p, part)[:, 0:(SEQ, CTX)[part]], ACT.Copy) \
                            .then_inc(is_drained("sg", l, p, part), 1)
                for k in range(KT):
                    for part in both:
                        full_of(act, "mo", l, k, part[0])
                        act.activation(y_t[:, k, part[1]:part[1] + part[2]], bank("mo", l, k, part[0])[:, 0:part[2]],
                                       ACT.Copy).then_inc(is_drained("mo", l, k, part[0]), 1)

                def ready2(k):
                    for part in both:
                        drained_of(act, "mo", l, k, part[0])

                squares(l, POST_FFN, y_t, ready2)

            for l in range(DEPTH):
                layer(l)
            for i in range(LT):
                full_of(act, "out", i, 0)
                act.activation(h_tok[:, i, 0:512], bank("out", i, 0)[:, :], ACT.Copy) \
                    .then_inc(is_drained("out", i, 0), 1)

        @block.vector
        def _(dve):
            steps = [0]

            def link(ins):
                steps[0] += 1
                ins.then_inc(dve_step, 1)
                dve.wait_ge(dve_step, steps[0])

            def mark(ins):
                steps[0] += 1
                ins.then_inc(dve_step, 1)
                return steps[0]

            def reciprocals(key, parts):
                for part in parts:
                    drained_of(dve, *key, part[0])
                    r = rb[:, part[1]:part[1] + part[2]]
                    link(dve.reciprocal(r, r))

            def normed(l, norm):
                reciprocals(("ms", l, norm), parts_of(l, norm))
                pi = 2 * l + (0 if norm == PRE_MIX else 1)
                n = TOK if len(parts_of(l, norm)) == 2 else SEQ
                for k in range(KT):
                    if k >= 2:
                        dve.wait_ge(h_ready, 8 * pi + k - 1)
                    dve.tensor_tensor(sq[k % 2][:, 0:n], x_t[:, k, 0:n], rb[:, 0:n], ALU.mult).then_inc(xr_ready, 1)

            def add_to_stream(l, norm, src):
                parts = parts_of(l, norm)
                reciprocals(("ms", l, norm), parts)
                n = TOK if len(parts) == 2 else SEQ
                m = 1 if norm == POST_MIX else 3
                for k in range(KT):
                    if k >= 2:
                        dve.wait_ge(x_updated, 8 * (2 * l + (norm == POST_FFN)) + k - 1)
                    link(dve.tensor_tensor(tmp[k % 2][:, 0:n], src[:, k, 0:n], rb[:, 0:n], ALU.mult))
                    for part in parts:
                        w, cols = part[0], slice(part[1], part[1] + part[2])
                        op = dve.scalar_tensor_tensor(x_t[:, k, cols], tmp[k % 2][:, cols], scl[l][:, m, k, w:w + 1],
                                                      x_t[:, k, cols], ALU.mult, ALU.add)
                    op.then_inc(x_updated, 1)

            for i in range(TT):
                full_of(dve, "xin", i, 1)
                dve.tensor_copy(x_t[:, 4:8, i * P:(i + 1) * P],
                                bank("xin", i, 1)[:, :].rearrange("p (k t) -> p k t", k=4)) \
                    .then_inc(is_drained("xin", i, 1), 1)
            for l in range(DEPTH):
                for r, (first, n) in enumerate(((0, NR1), (NR1, NR2), (NR1 + NR2, NR3))):
                    full_of(dve, "par", l, r)
                    dve.tensor_copy(par[l][:, first:first + n], bank("par", l, r)[:, 0:n]) \
                        .then_inc(is_drained("par", l, r), 1)
            for l in range(DEPTH):
                for r in range(3):
                    drained_of(dve, "par", l, r)
            dve.wait_ge(par_loaded, 16 * 25)
            link(dve.tensor_scalar(nsink, nsink, -1.0, None, ALU.mult))

            def modulation(l, c):
                full_of(dve, "mod", l, c)
                b = par[l][:, R_ADAB + 4 * c:R_ADAB + 4 * c + 4]
                dve.tensor_tensor(mods[l][:, 4 * c:4 * c + 4, :],
                                  bank("mod", l, c)[:, 0:8].rearrange("p (c w) -> p c w", w=2),
                                  b.unsqueeze(2).broadcast_to([P, 4, 2]), ALU.add).then_inc(is_drained("mod", l, c), 1)
                drained_of(dve, "mod", l, c)

            def modulation_after(*key):
                if key in MOD_AFTER:
                    modulation(*MOD_AFTER[key])

            def vectors(l, v):
                return mods[l][:, v * KT:(v + 1) * KT, :]

            def gain(l, row):
                return par[l][:, row:row + KT].unsqueeze(2).broadcast_to([P, KT, 2])

            def norm_scale(l, m, v, row):
                link(dve.tensor_scalar(scl[l][:, m], vectors(l, v), 1.0, None, ALU.add))
                link(dve.tensor_tensor(scl[l][:, m], scl[l][:, m], gain(l, row), ALU.mult))

            def layer(l):
                both = parts_of(l)
                if l == 0:
                    for c in range(MOD_FIRST):
                        modulation(l, c)
                    norm_scale(l, 0, 1, R_PM)
                normed(l, PRE_MIX)
                for pad, sizes, half in ((cpad, PADC, HC), (bpad, PADS, HS)):
                    for w in range(2):
                        first = sizes[0] * w
                        dve.memset(pad[:, :, first:first + half], 0.0)
                        z = dve.memset(pad[:, :, first + sizes[w] - half:first + sizes[w]], 0.0)
                z.then_inc(conv_zero, 1)
                modulation_after("win", l, C_AV)
                for t in range(CT):
                    for part in both:
                        key = ("win", l, C_AG, t, part[0])
                        drained_of(dve, "win", l, C_AV, t, part[0])
                        drained_of(dve, *key)
                        j = GLU(l, t, part[0])
                        dst = cpad[:, t, PADC[0] * part[0] + HC:PADC[0] * part[0] + HC + part[2]]
                        dve.tensor_tensor(dst, dst, sq[j % 2][:, 0:part[2]], ALU.mult).then_inc(glu_done, 1)
                modulation_after("win", l, C_AG)
                dve.wait_ge(glu_done, GLU(l, CT - 1, both[-1][0]) + 1)
                dve.wait_ge(conv_zero, l + 1)

                def conv_taps():
                    marks = {}
                    for j in range(CONV_K):
                        for t in range(CT):
                            for part in both:
                                first = PADC[0] * part[0] + j
                                src = cpad[:, t, first:first + part[2]]
                                dst = a_t[:, t, part[1]:part[1] + part[2]]
                                w = par[l][:, NR1 + j * CT + t:NR1 + j * CT + t + 1]
                                if j == 0:
                                    b = par[l][:, R_CB + t:R_CB + t + 1]
                                    op = dve.tensor_scalar(dst, src, w, b, ALU.mult, ALU.add)
                                else:
                                    dve.wait_ge(dve_step, marks[t, part[0]])
                                    op = dve.scalar_tensor_tensor(dst, src, w, dst, ALU.mult, ALU.add)
                                if j < CONV_K - 1:
                                    marks[t, part[0]] = mark(op)
                                else:
                                    op.then_inc(conv_done, 1)
                                yield

                taps = conv_taps()

                def convolve(n):
                    for _ in range(n):
                        next(taps, None)

                convolve(16)
                modulation_after("win", l, C_BG)
                convolve(16)
                modulation_after("win", l, C_CG)
                for t in range(CT):
                    for part in both:
                        convolve(8)
                        key = ("win", l, C_HV, t, part[0])
                        full_of(dve, *key)
                        drained_of(dve, "win", l, C_CG, t, part[0])
                        dst = bpad[:, t, PADS[0] * part[0] + HS:PADS[0] * part[0] + HS + part[2]]
                        dve.tensor_tensor(dst, bank(*key)[:, 0:part[2]], dst, ALU.mult).then_inc(is_drained(*key), 1)
                modulation_after("win", l, C_HV)
                for t in range(CT):
                    if t >= 2:
                        dve.wait_ge(short_done, 4 * l + t - 1)
                    for part in both:
                        drained_of(dve, "win", l, C_HV, t, part[0])
                        drained_of(dve, "win", l, C_BG, t, part[0])
                        cols = slice(part[1], part[1] + part[2])
                        for j in range(SHORT_K):
                            first = PADS[0] * part[0] + j
                            src = bpad[:, t, first:first + part[2]]
                            c0 = NR1 + NR2 + j * CT + t
                            w = par[l][:, c0:c0 + 1]
                            if j == 0:
                                link(dve.tensor_scalar(sq[t % 2][:, cols], src, w, None, ALU.mult))
                            else:
                                link(dve.scalar_tensor_tensor(sq[t % 2][:, cols], src, w, sq[t % 2][:, cols], ALU.mult, ALU.add))
                        op = dve.tensor_tensor(b_t[:, t, cols], b_t[:, t, cols], sq[t % 2][:, cols], ALU.mult)
                    op.then_inc(short_done, 1)
                for t in range(CT + 1):
                    convolve(8)
                    if t == CT:
                        modulation_after("win", l, C_Q)
                    if t == 0:
                        dve.wait_ge(short_done, 4 * (l + 1))
                    full_of(dve, "rope", l, t)
                    dst = q_t[:, t, 0:SEQ] if t < CT else k_t[:, 0, 0:SEQ]
                    if t >= 2:
                        dve.wait_ge(rope_done, 5 * l + t - 1)
                    dve.tensor_tensor(sq[t % 2][:, 0:SEQ], bank("rope", l, t)[:, :], sinT, ALU.mult) \
                        .then_inc(is_drained("rope", l, t), 1)
                    link(dve.tensor_tensor(dst, dst, cosT, ALU.mult))
                    drained_of(dve, "rope", l, t)
                    dve.tensor_tensor(dst, dst, sq[t % 2][:, 0:SEQ], ALU.add).then_inc(rope_done, 1)
                dve.wait_ge(rope_done, 5 * (l + 1))
                drained_of(dve, "k", l, 1)
                dve.tensor_copy(k_t[0:HD, 1, :], k_t[HD:P, 0, :]).then_inc(swapped, 1)
                dve.tensor_copy(k_t[HD:P, 1, :], k_t[0:HD, 0, :]).then_inc(swapped, 1)
                convolve(16)
                modulation_after("win", l, C_KV)
                convolve(32)
                modulation_after("win", l, C_F)
                convolve(48)
                units = att_units(l)

                def local_scores(u):
                    con, n, g = units[u]
                    lo, hi, _ = band(units[u])
                    if con:
                        return
                    if u == 0:
                        full_of(dve, "fo", l, CT - 1, both[-1][0])
                    for h in range(GRP):
                        full_of(dve, "sl", l, u, h)
                        if u >= 2 and h == 0:
                            full_of(dve, "pt", l, u - 2, band(units[u - 2])[2] - 1)
                        m0 = (lo - (n - 1)) * P
                        nl = (hi - lo) * P
                        dve.tensor_tensor(S_buf[u % 2][:, h, 0:nl], bank("sl", l, u, h)[:, 0:nl],
                                          maskT[:, m0:m0 + nl], ALU.add).then_inc(is_drained("sl", l, u, h), 1)

                def stats(u):
                    con, n, g = units[u]
                    nk = band(units[u])[2] * P
                    for h in range(GRP):
                        if not con:
                            drained_of(dve, "sl", l, u, h)
                        drained_of(dve, "sc", l, u, h)
                    link(dve.tensor_reduce(st[:, 0, :], S_buf[u % 2][:, :, 0:nk], AX.X, ALU.max))
                    ns = nsink[:, l * HEADS + GRP * g:l * HEADS + GRP * g + GRP]
                    link(dve.scalar_tensor_tensor(st[:, 1, :], st[:, 0, :], -(HD ** -0.5), ns, ALU.mult, ALU.min))
                    dve.tensor_tensor(st[:, 2, :], st[:, 1, :], ns, ALU.subtract).then_inc(stats_done, 1)

                def scale(u):
                    nk = band(units[u])[2] * P
                    dve.wait_ge(exps_done, 5 * (PROBS0[l] + u + 1))
                    link(dve.tensor_tensor(st[:, 6, :], st[:, 3, :], st[:, 4, :], ALU.add))
                    link(dve.reciprocal(st[:, 7, :], st[:, 6, :]))
                    for h in range(GRP):
                        S = S_buf[u % 2][:, h, 0:nk]
                        op = dve.tensor_scalar(S, S, st[:, 7, h:h + 1], None, ALU.mult)
                    op.then_inc(probs_done, 1)

                def turned(u):
                    for kt in range(1, band(units[u])[2], 2):
                        full_of(dve, "pt", l, u, kt)
                        if u:
                            full_of(dve, "av", l, u - 1)
                        dve.tensor_copy(probs_t[:, kt, :], bank("pt", l, u, kt)[:, :]) \
                            .then_inc(is_drained("pt", l, u, kt), 1)

                local_scores(0)
                for u in range(len(units)):
                    stats(u)
                    scale(u)
                    if u + 1 < len(units):
                        local_scores(u + 1)
                    turned(u)
                    convolve(4)
                convolve(CONV_K * CT * 2)
                dve.wait_ge(conv_done, CONV[l])
                for part in both:
                    full_of(dve, "lm", l, part[0])
                for k in range(CT):
                    for part in both:
                        cols = slice(part[1], part[1] + part[2])
                        op = dve.tensor_tensor(a_t[:, k, cols], a_t[:, k, cols], bank("lm", l, part[0])[:, 0:part[2]],
                                               ALU.subtract)
                        if k == CT - 1:
                            op.then_inc(is_drained("lm", l, part[0]), 1)
                        elif part is both[-1]:
                            op.then_inc(centred, 1)
                reciprocals(("lv", l), both)
                for k in range(CT):
                    n = TOK if l == 0 else SEQ
                    dve.tensor_tensor(a_t[:, k, 0:n], a_t[:, k, 0:n], rb[:, 0:n], ALU.mult).then_inc(lnorm_done, 1)
                at_ = -1
                for dp in range(KT // 2):
                    for b in range(4):
                        for t in range(2):
                            at_ += 1
                            for part in both:
                                cols = slice(part[1], part[1] + part[2])
                                key = ("w", l, dp, b, t, part[0])
                                full_of(dve, *key)
                                drained_of(dve, "g", l, dp, b, t, part[0])
                                gate, y = sq[at_ % 2][:, cols], y_t[:, 2 * dp + t, cols]
                                dst = y if b == 0 else rb[:, cols]
                                dve.tensor_tensor(dst, gate, bank(*key)[:, 0:part[2]], ALU.mult) \
                                    .then_inc(is_drained(*key), 1)
                                if b:
                                    drained_of(dve, *key)
                                    if b == 3 and part is both[-1]:
                                        dve.tensor_tensor(y, y, rb[:, cols], ALU.add).then_inc(merged, 1)
                                        dve.wait_ge(merged, 8 * l + 2 * dp + t + 1)
                                    else:
                                        link(dve.tensor_tensor(y, y, rb[:, cols], ALU.add))
                                else:
                                    drained_of(dve, *key)
                        modulation_after("mg", l, dp, b)
                v = [mark(dve.tensor_tensor(scl[l][:, m], vectors(l, at), gain(l, row), ALU.mult))
                     for m, at, row in ((1, 2, R_QM), (3, 5, R_QF))]
                dve.wait_ge(dve_step, v[-1])
                norm_scale(l, 2, 4, R_PF)
                if l + 1 < DEPTH:
                    norm_scale(l + 1, 0, 1, R_PM)
                dve.wait_ge(x_back, 16 * (l + 1))
                add_to_stream(l, POST_MIX, yo_t)
                dve.wait_ge(x_updated, 8 * (2 * l + 1))
                normed(l, PRE_FFN)
                nt = TT if l == 0 else LT
                full_of(dve, "rl", l)
                lg = bank("rl", l)[:, 0:nt * NE].rearrange("p (i e) -> p i e", e=NE)
                link(dve.tensor_reduce(rs[:, 0, 0:nt], lg, AX.X, ALU.max))
                dve.tensor_tensor(aff[:, 0:nt, :], lg, rs[:, 0, 0:nt].unsqueeze(2).broadcast_to([P, nt, NE]),
                                  ALU.subtract).then_inc(is_drained("rl", l), 1)
                drained_of(dve, "rl", l)
                dve.wait_ge(aff_exp, l + 1)
                link(dve.tensor_reduce(rs[:, 0, 0:nt], aff[:, 0:nt, :], AX.X, ALU.add))
                link(dve.reciprocal(rs[:, 1, 0:nt], rs[:, 0, 0:nt]))
                dve.tensor_tensor(aff[:, 0:nt, :], aff[:, 0:nt, :],
                                  rs[:, 1, 0:nt].unsqueeze(2).broadcast_to([P, nt, NE]), ALU.mult) \
                    .then_inc(aff_done, 1)
                E = slice(0, NE)
                link(dve.memset(sel_e[E, 0, :], 1.0))
                for w, (_, first, n) in enumerate(both):
                    cols = slice(first, first + n)
                    full_of(dve, "at", l, w)
                    dve.tensor_copy(sel_e[E, 1, cols], bank("at", l, w)[0:NE, 0:n]) \
                        .then_inc(is_drained("at", l, w), 1)
                    drained_of(dve, "at", l, w)
                    for _ in range(CAP[w] // 8):
                        link(dve.max(top8[E, 0:8], sel_e[E, 1, cols]))
                        link(dve.match_replace(sel_e[E, 1, cols], top8[E, 0:8], sel_e[E, 1, cols], -1.0))
                    link(dve.tensor_scalar(sel_e[E, 2, cols], sel_e[E, 1, cols], 0.0, None, ALU.is_lt))
                    link(dve.tensor_tensor_scan(sel_e[E, 3, cols], sel_e[E, 0, cols], sel_e[E, 2, cols], 0.0,
                                                ALU.mult, ALU.add))
                    link(dve.tensor_tensor(sel_e[E, 3, cols], sel_e[E, 3, cols], sel_e[E, 2, cols], ALU.mult))
                    dve.tensor_scalar(sel_e[E, 3, cols], sel_e[E, 3, cols], -1.0, None, ALU.add) \
                        .then_inc(pos_done, 1)
                full_of(dve, "pos", l)
                dve.tensor_copy(pos_t[:, 0:nt, :], bank("pos", l)[:, 0:nt * NE].rearrange("p (i e) -> p i e", e=NE)) \
                    .then_inc(is_drained("pos", l), 1)
                drained_of(dve, "pos", l)

                def per_tile(i):
                    w = 0 if i < LT else 1
                    return w, onehot[w][:, i - w * LT, :].rearrange("p (e s) -> p e s", e=NE)

                for i in range(nt):
                    w, oh = per_tile(i)
                    oh = onehot_r[w][:, i - w * LT, :].rearrange("p (e s) -> p e s", e=NE)
                    dve.tensor_tensor(oh, iota[:, 0:CAP[w]].unsqueeze(1).broadcast_to([P, NE, CAP[w]]),
                                      pos_t[:, i, :].unsqueeze(2).broadcast_to([P, NE, CAP[w]]), ALU.is_equal) \
                        .then_inc(onehot_done, 1)
                ns = sum(CAP) if l == 0 else CAP[0]
                for k in range(KT):
                    gather_out(dve, l, k, 1, ns, dve.tensor_copy)
                full_of(dve, "ga", l, KT - 1, 2 if l == 0 else 1)
                for i in range(nt):
                    w, oh = per_tile(i)
                    ones_zeros = onehot_r[w][:, i - w * LT, :].bitcast(F32).rearrange("p (e s) -> p e s", e=NE)
                    dve.tensor_tensor(oh, ones_zeros, aff[:, i, :].unsqueeze(2).broadcast_to([P, NE, CAP[w]]), ALU.mult) \
                        .then_inc(og_done, 1)
                for t in (hid_hi, hid_lo):
                    dve.tensor_scalar(t[:, KT * ns:(KT - 1) * ns + P], iota[:, 0:P - ns], 0.0, None, ALU.mult)
                with dve.Fori(0, NE // 4) as turn:
                    for e in range(4):
                        for h in range(2):
                            full_of(dve, "h3", l, e, h, turn=turn)
                            drained_of(dve, "h1", l, e, h, turn=turn)
                            if e:
                                full_of(dve, "y", l, e - 1, 1, turn=turn)
                            else:
                                full_of(dve, "y", l, 3, 1, turn=turn - 1)
                            t, cols = silu_t[h][:, 0:4 * ns], slice(4 * ns * h, 4 * ns * (h + 1))
                            n = 16 * NE // 4 * l + 4 * e + 2 * h
                            dve.tensor_tensor(t, t, bank("h3", l, e, h)[:, 0:4 * ns], ALU.mult).then_inc(hid_step, 1)
                            dve.wait_ge(hid_step, n + 1 + 16 * turn)
                            dve.tensor_copy(hid_hi[:, cols], t).then_inc(hid_step, 1)
                            dve.wait_ge(hid_step, n + 2 + 16 * turn)
                            dve.tensor_tensor(hid_lo[:, cols], t, hid_hi[:, cols].bitcast(F32), ALU.subtract) \
                                .then_inc(is_drained("h3", l, e, h), 1)
                        lower_parts(dve, l, e, 1, turn)
                        y_out(dve, l, e, 1, turn, dve.tensor_copy)
                for part, npair in ((0, NE // 2), (1, NE // 4))[:len(both)]:
                    for p in range(1, npair, 2):
                        full_of(dve, "sg", l, p, part)
                        dve.tensor_copy(sg[part][:, p, :], bank("sg", l, p, part)[:, 0:(SEQ, CTX)[part]]) \
                            .then_inc(is_drained("sg", l, p, part), 1)
                add_to_stream(l, POST_FFN, y_t)

            for l in range(DEPTH):
                layer(l)
            for i in range(LT):
                full_of(dve, "out", i, 1)
                dve.tensor_copy(h_tok[:, i, 512:1024], bank("out", i, 1)[:, :]) \
                    .then_inc(is_drained("out", i, 1), 1)


def tables():
    f = np.float32
    ident = np.eye(P, dtype=f)
    perm = np.zeros((P, P), f)
    for m in range(P):
        if m % 32 < 16:
            perm[m + 16, m] = -1
        else:
            perm[m - 16, m] = 1
    t = np.arange(SEQ)
    inv = (10000.0 ** (-np.arange(16, dtype=f) / f(16))).astype(f)
    ar = ((t // GRID_W).astype(f)[:, None] * inv).astype(f)
    ac = ((t % GRID_W).astype(f)[:, None] * inv).astype(f)
    ang = np.concatenate([ar, ar, ac, ac], 1).T.astype(np.float64)
    ang = np.concatenate([ang, ang], 0)
    kj, qi = np.arange(3 * P)[None, :], np.arange(P)[:, None]
    mask = np.where(np.abs(kj - P - qi) <= P, 0.0, -1e30).astype(f)

    def dft(n, fn, by):
        k = np.arange(n)
        m = fn(2 * np.pi * ((k[:, None] * k[None, :]) % n) / n) * by
        return m.reshape(n // P, P, n).transpose(1, 0, 2).reshape(P, -1)

    d = np.concatenate([dft(SEQ, np.cos, SEQ ** -0.5), dft(SEQ, np.sin, SEQ ** -0.5),
                        dft(CTX, np.cos, CTX ** -0.5), dft(CTX, np.sin, CTX ** -0.5),
                        dft(P, np.cos, P ** -0.5), dft(P, np.sin, -P ** -0.5)], 1).astype(f)
    return {"ident": ident, "ones_d": np.full((P, P), 1 / D, f), "ones_c": np.full((P, P), 1 / DC, f), "perm": perm,
            "cos": np.cos(ang).astype(f), "sin": np.sin(ang).astype(f), "mask": mask,
            "iota": np.broadcast_to(np.arange(CAP[0], dtype=f), (P, CAP[0])).copy(), "dft": d}


def kernel(**inputs):
    import concourse.bacc as bacc
    from concourse.bass_utils import run_bass_kernel_spmd

    nc = bacc.Bacc("TRN2", target_bir_lowering=False, num_devices=1)
    arrays, ins, consts = {}, {}, {}
    for group, prefix, source in ((ins, "in", inputs), (consts, "const", tables())):
        for name, a in source.items():
            a = np.ascontiguousarray(a)
            arrays[f"{prefix}_{name}"] = a
            group[name] = nc.dram_tensor(f"{prefix}_{name}", a.shape, mybir.dt.from_np(a.dtype),
                                         kind="ExternalInput").ap()
    out = nc.dram_tensor("out", (1, SEQ, D), F32, kind="ExternalOutput").ap()
    x_dram = nc.dram_tensor("x_dram", (P, KT, TOK), F32, kind="Internal").ap()
    build(nc, ins, consts, x_dram, out)
    r = run_bass_kernel_spmd(nc, [arrays], core_ids=[0])
    return r.results[0]["out"]
```

```python
from contextlib import ExitStack

import numpy as np

import concourse.bass as bass
from concourse import mybir
from concourse.alu_op_type import AluOpType as ALU

F32 = mybir.dt.float32
F32R = mybir.dt.float32r
ACT = mybir.ActivationFunctionType
AX = mybir.AxisListType

P = 128
D = 1024
KT = D // P
SEQ, CTX = 512, 256
TOK = SEQ + CTX
DEPTH = 2
LAT, CON = (0, 0, SEQ), (1, SEQ, CTX)
DC = 512
CT = DC // P
CONV_K, SHORT_K = 31, 3
HC, HS = CONV_K // 2, SHORT_K // 2
HEADS, KVH, HD = 8, 2, 64
GRP = HEADS // KVH
GRID_W = 64
NE = 16
CAP = (2 * SEQ // NE, 2 * CTX // NE)
EPS = 1e-6
NB = SEQ // P
LT, CTT = SEQ // P, CTX // P
TT = LT + CTT
O_A, O_B, O_Q, O_K, O_V, O_F, O_G = 0, 1024, 2560, 3072, 3200, 3328, 3840
WCHUNKS = [(0, 512), (512, 512), (1024, 512), (1536, 512), (2048, 512), (2560, 512), (3072, 256), (3328, 512)]
C_AV, C_AG, C_BG, C_CG, C_HV, C_Q, C_KV, C_F = range(8)
BANKS = 8
HID = KT * sum(CAP) + P - sum(CAP)
SLOT = 4096
PADC = SEQ + 2 * HC, CTX + 2 * HC
PADS = SEQ + 2 * HS, CTX + 2 * HS
R_ADAB, R_PM, R_QM, R_PF, R_QF, R_GB, R_CB, R_LG, R_LB = 0, 48, 56, 64, 72, 80, 112, 116, 120
NR1, NR2, NR3 = 124, CONV_K * CT, SHORT_K * CT
NPAR = NR1 + NR2 + NR3
PRE_MIX, POST_MIX, PRE_FFN, POST_FFN = range(4)
MOD_CHUNKS, MOD_FIRST = 12, 4
MOD_TARGETS = [(0, c) for c in range(MOD_FIRST, MOD_CHUNKS)] + [(1, c) for c in range(MOD_CHUNKS)]
ROW_PLACES = [("fo", 0, g) for g in range(1, CT)] + [("att", 0, u) for u in range((NB + CTT) * KVH)] + [("rows", 0)]
ROW_AT = dict(zip(ROW_PLACES[:-1], MOD_TARGETS))
MOD_AT = dict(zip([("lv", 0), ("post", 0), ("pre", 0, 0), ("pre", 0, 1), ("ht", 0)], MOD_TARGETS[len(ROW_AT):]))


def row_before(place):
    i = ROW_PLACES.index(place) if place in ROW_PLACES else 0
    return ROW_AT[ROW_PLACES[i - 1]] if i else None


def parts_of(l, norm=POST_MIX):
    return (LAT, CON) if l == 0 or norm == PRE_MIX else (LAT,)


def att_units(l):
    units = [(0, n, g) for n in range(NB) for g in range(KVH)]
    return units + ([(1, n, g) for n in range(CTT) for g in range(KVH)] if l == 0 else [])


def band(unit):
    con, n, _ = unit
    lo, hi = (0, 0) if con else (max(n - 1, 0), min(n + 2, NB))
    return lo, hi, hi - lo + CTT


def plan_jobs():
    jobs, n = {}, 0

    def add(*key):
        nonlocal n
        jobs[key] = n
        n += 1

    def mod_at(*key):
        if row_before(key):
            add("mod", *row_before(key))
        if key in ROW_AT:
            add("mrow", *ROW_AT[key])
        if key in MOD_AT:
            add("mod", *MOD_AT[key])

    for i in range(TT):
        for h in range(2):
            add("xin", i, h)
    for l in range(DEPTH):
        for r in range(3):
            add("par", l, r)
    add("cin", 0)
    for l in range(DEPTH):
        both = parts_of(l)
        for part in (LAT, CON):
            add("ms", l, PRE_MIX, part[0])
        if l == 0:
            for c in range(MOD_FIRST):
                add("mrow", l, c)
                add("mod", l, c)
        for c in range(C_KV):
            for t in range(CT):
                for part in both:
                    add("win", l, c, t, part[0])
                if c == C_Q and t:
                    add("rope", l, t - 1)
        for part in (LAT, CON):
            add("k", l, part[0])
            add("rope", l, CT - 1 + part[0])
        for part in (LAT, CON):
            add("v", l, part[0])
        for i in range(TT if l == 0 else LT):
            add("f", l, i)
        for g in range(CT):
            for part in both:
                add("fc", l, g, part[0])
                add("fs", l, g, part[0])
            mod_at("fo", l, g)
            if g:
                for part in both:
                    add("fo", l, g - 1, part[0])
        for part in both:
            add("fo", l, CT - 1, part[0])
        units = att_units(l)

        def scores(u):
            for h in range(GRP):
                if not units[u][0]:
                    add("sl", l, u, h)
                add("sc", l, u, h)

        scores(0)
        for u in range(len(units)):
            if u + 1 < len(units):
                scores(u + 1)
            mod_at("att", l, u)
            for kt in range(band(units[u])[2]):
                add("pt", l, u, kt)
            add("av", l, u)
        mod_at("rows", l)
        for part in both:
            add("lm", l, part[0])
        for part in both:
            add("lv", l, part[0])
        mod_at("lv", l)
        for b in range(4):
            for dp in range(KT // 2):
                for t in range(2):
                    for part in both:
                        add("g", l, dp, b, t, part[0])
                        add("w", l, dp, b, t, part[0])
        for t in range(KT):
            for part in both:
                add("wo", l, t, part[0])
        for norm in (POST_MIX, PRE_FFN):
            for part in both:
                add("ms", l, norm, part[0])
            if norm == POST_MIX:
                mod_at("post", l)
        for i in range(2):
            mod_at("pre", l, i)
        add("rl", l)
        add("at", l, 0)
        if l == 0:
            add("at", l, 1)
        for i in range(TT if l == 0 else LT):
            for h in range(2):
                add("ht", l, i, h)
        mod_at("ht", l)
        add("pos", l)
        for k in range(KT):
            add("ga", l, k, 0)
            add("ga", l, k, 1)
            if l == 0:
                add("ga", l, k, 2)
        for e in range(NE):
            for h in range(2):
                add("h1", l, e, h)
                add("h3", l, e, h)
            add("y", l, e, 0)
            add("y", l, e, 1)
        for p in range(NE // 2):
            add("sg", l, p, 0)
        if l == 0:
            for p in range(NE // 4):
                add("sg", l, p, 1)
        for k in range(KT):
            for part in both:
                add("mo", l, k, part[0])
        for part in both:
            add("ms", l, POST_FFN, part[0])
    for i in range(LT):
        for h in range(2):
            add("out", i, h)
    return jobs


def plan_chunks():
    chunks, held, last_in = {}, [0] * 4, [None] * 4

    def add(key, slot, last_job, loads=1):
        held[slot] += loads
        chunks[key] = (slot, held[slot], last_job, last_in[slot])
        last_in[slot] = key

    turn = 0

    def mixer(key, last_job, loads=1):
        nonlocal turn
        add(key, turn % 2, last_job, loads)
        turn += 1

    def modulation(targets, job):
        for target in targets:
            mixer(("ada", *target), (job, *target))

    for l in range(DEPTH):
        last = parts_of(l)[-1][0]
        if l == 0:
            for c in range(MOD_FIRST):
                mixer(("ada", l, c), ("mrow", l, c))
        for c in range(C_KV):
            mixer(("win", l, c), ("win", l, c, CT - 1, last))
        mixer(("win", l, C_KV), ("v", l, 1))
        mixer(("win", l, C_F), ("f", l, (TT if l == 0 else LT) - 1))
        if l == 0:
            modulation(ROW_AT.values(), "mrow")
            modulation([MOD_AT["lv", 0]], "mod")
        for b in range(4):
            for dp in range(KT // 2):
                mixer(("mg", l, dp, b), ("w", l, dp, b, 1, last), loads=2)
        for h in range(2):
            mixer(("wo", l, h), ("wo", l, 4 * h + 3, last))
        if l == 0:
            modulation(list(MOD_AT.values())[1:], "mod")
        for e in range(NE):
            for m, (job, h) in enumerate((("h1", 0), ("h3", 0), ("h1", 1), ("h3", 1), ("y", 0), ("y", 1))):
                add(("ex", l, e, m), (6 * e + m) % 4, (job, l, e, h))
    return chunks


def build(nc, A, K, x_dram, out):
    jobs, chunks = plan_jobs(), plan_chunks()
    ctx = ExitStack()
    with ctx:
        def sb(name, n, rows=P):
            t = ctx.enter_context(nc.sbuf_tensor(name, [rows, n], F32))
            where[id(t)] = nc.sbuf_base - 4 * n
            return t

        where = {}

        def over(name, host, first, n):
            return nc.alloc_sbuf_tensor_at(name, [P, n], F32R, offset=where[id(host)] + 4 * first)

        def sem(name):
            return ctx.enter_context(nc.semaphore(name))

        x_all = sb("x_t", KT * TOK)
        x_t = x_all[:, :].rearrange("p (k t) -> p k t", k=KT)
        hb = sb("hb", 2 * KT * TOK)
        h_t = hb[:, 0:KT * TOK].rearrange("p (k t) -> p k t", k=KT)
        hb2 = hb[:, KT * TOK:2 * KT * TOK]
        y_t = hb2.rearrange("p (k t) -> p k t", k=KT)
        h_tok = hb2.rearrange("p (i d) -> p i d", i=TT)
        yo_t = h_t
        S_buf = [hb2[:, b * 2560:(b + 1) * 2560].rearrange("p (h k) -> p h k", h=GRP) for b in range(2)]
        c512 = hb2[:, 0:2048].rearrange("p (i n) -> p i n", i=LT)
        s512 = hb2[:, 2048:4096].rearrange("p (i n) -> p i n", i=LT)
        c256 = hb2[:, 4096:4608].rearrange("p (i n) -> p i n", i=CTT)
        s256 = hb2[:, 4608:5120].rearrange("p (i n) -> p i n", i=CTT)
        c128 = hb2[:, 5120:5248]
        s128 = hb2[:, 5248:5376]
        ring0 = sb("ring0", 2 * SLOT)
        slots = [ring0[:, 0:SLOT], ring0[:, SLOT:2 * SLOT], hb[:, 0:SLOT], hb[:, SLOT:2 * SLOT]]
        hb_r, ring_r = over("hb_r", hb, 0, 2 * KT * TOK), over("ring_r", ring0, 0, 2 * SLOT)
        slots_lo = [(ring_r, hb_r)[b // 2][:, b % 2 * SLOT:(b % 2 + 1) * SLOT] for b in range(4)]
        w2_hi = hb_r[:, 2 * SLOT:3 * SLOT].rearrange("p (k n) -> p k n", k=KT)
        h_hi, h_lo = (hb_r[:, b * KT * TOK:(b + 1) * KT * TOK].rearrange("p (i d) -> p i d", i=TT)
                      for b in range(2))
        mix_lo = over("mix_lo", x_all, 0, KT * TOK)[:, :].rearrange("p (k t) -> p k t", k=KT)
        mix_hi2, mix_hi1 = (hb_r[:, b * KT * TOK:(b + 1) * KT * TOK].rearrange("p (k t) -> p k t", k=KT)
                            for b in range(2))
        AR = 20992
        arena = sb("arena", AR)
        at = [0]

        def take(n):
            at[0] += n
            return arena[:, at[0] - n:at[0]]

        cpad = take(CT * sum(PADC)).rearrange("p (t n) -> p t n", t=CT)
        a_at = at[0]
        a_t = take(CT * TOK).rearrange("p (t n) -> p t n", t=CT)
        b_at = at[0]
        b_t = take(CT * TOK).rearrange("p (t n) -> p t n", t=CT)
        q_at = at[0]
        q_t = take(CT * TOK).rearrange("p (t n) -> p t n", t=CT)
        w_hi_at = at[0]
        k_t = take(2 * TOK).rearrange("p (s n) -> p s n", s=2)
        v_tok = take(TOK).rearrange("p (i n) -> p i n", i=TT)
        f_at = at[0]
        f_tok = take(CT * TOK).rearrange("p (i n) -> p i n", i=TT)
        shared = take(CT * sum(PADS))
        bpad = shared.rearrange("p (t n) -> p t n", t=CT)
        xc = [shared[:, b * 1536:b * 1536 + TOK] for b in range(2)]
        xs = [shared[:, b * 1536 + TOK:b * 1536 + 2 * TOK] for b in range(2)]
        probs_t = shared[:, 0:2560].rearrange("p (k n) -> p k n", k=5)
        assert at[0] == AR
        w_hi_r = over("w_hi_r", arena, w_hi_at, CT * D)
        w_hi = [w_hi_r[:, t * D:(t + 1) * D].rearrange("p (k n) -> p k n", k=KT) for t in range(CT)]
        mod_rows = shared[0:2, 0:MOD_FIRST * 512]
        tmp = [arena[:, 3312 + b * TOK:3312 + (b + 1) * TOK] for b in range(2)]
        y_hi_r = [over("y_hi0", arena, b_at, 4 * TOK), over("y_hi1", arena, AR - CT * sum(PADS), 4 * TOK)]
        src_f32 = {1: b_t, 2: q_t, 3: f_tok}
        cpad_r, a_r = over("cpad_r", arena, 0, 4 * TOK), over("a_r", arena, a_at, 2 * D)
        src_lo = {b: over(f"src_lo{b}", arena, at_, 4 * TOK) for b, at_ in ((1, b_at), (2, q_at), (3, f_at))}
        src_hi = {1: cpad_r, 2: y_hi_r[1], 3: cpad_r}
        xgy = arena[:, 0:15360]
        sel_e = arena[:, 0:4 * TOK].rearrange("p (w t) -> p w t", w=4)
        onehot = [arena[:, 15360:19456].rearrange("p (i s) -> p i s", i=LT),
                  arena[:, 19456:20480].rearrange("p (i s) -> p i s", i=CTT)]
        onehot_r = [over("onehot0", arena, 15360, 4096)[:, :].rearrange("p (i s) -> p i s", i=LT),
                    over("onehot1", arena, 19456, 1024)[:, :].rearrange("p (i s) -> p i s", i=CTT)]
        sg = [hb[:, 0:4096].rearrange("p (g t) -> p g t", g=NE // 2),
              hb[:, 4096:5120].rearrange("p (g t) -> p g t", g=NE // 4)]
        work = sb("work", 2 * HID + 2 * 4 * sum(CAP))
        rb = work[:, 0:TOK]
        sq = [work[:, TOK:2 * TOK], work[:, 2 * TOK:3 * TOK]]
        mod_row = rb[0:2, 0:512]
        silu_t = [work[:, 2 * HID + b * 384:2 * HID + (b + 1) * 384] for b in range(2)]
        hid_hi, hid_lo = over("hid_hi", work, 0, HID), over("hid_lo", work, HID, HID)
        ident = sb("ident", P)[:, :]
        ones_d = sb("ones_d", P)[:, :]
        ones_c = sb("ones_c", P)[:, :]
        perm = sb("perm", P)[:, :]
        cosT = sb("cosT", SEQ)[:, :]
        sinT = sb("sinT", SEQ)[:, :]
        maskT = sb("maskT", 3 * P)[:, :]
        iota = sb("iota", CAP[0])[:, :]
        eps_t = sb("eps_t", 1)[:, :]
        spare = sb("spare", 1)[:, :]
        par = [sb(f"par{l}", NPAR)[:, :] for l in range(DEPTH)]
        nsink = sb("nsink", DEPTH * HEADS)[:, :]
        c_t = sb("c_t", 2 * KT)[:, :]
        mods = [sb(f"mods{l}", 96)[:, :].rearrange("p (c w) -> p c w", w=2) for l in range(DEPTH)]
        scl = [sb(f"scl{l}", 4 * KT * 2)[:, :].rearrange("p (m c w) -> p m c w", m=4, w=2)
               for l in range(DEPTH)]
        rw = sb("rw", KT * NE)[:, :].rearrange("p (k e) -> p k e", k=KT)
        st = sb("st", 64)[:, :].rearrange("p (w h) -> p w h", h=4)
        aff = sb("aff", TT * NE)[:, :].rearrange("p (i e) -> p i e", e=NE)
        rs = sb("rs", 2 * TT)[:, :].rearrange("p (w i) -> p w i", w=2)
        pos_t = arena[:, 20480:20480 + TT * NE].rearrange("p (i e) -> p i e", e=NE)
        top8 = sb("top8", 16)[:, :]
        x_tok = hb[:, 0:TT * D].rearrange("p (i d) -> p i d", i=TT)
        par_rows = hb2[:, 0:7 * P].rearrange("p (r n) -> p r n", n=P)

        ps = [ctx.enter_context(nc.psum_tensor(f"ps{b}", [P, 512], F32)) for b in range(BANKS)]

        full = [sem(f"full{b}") for b in range(BANKS)]
        drained = [sem(f"drained{b}") for b in range(BANKS)]
        loaded = [sem(f"loaded{s}") for s in range(4)]
        x_loaded, par_loaded, const_loaded = sem("x_loaded"), sem("par_loaded"), sem("const_loaded")
        ident_loaded = sem("ident_loaded")
        dft_loaded = sem("dft_loaded")
        rw_loaded = sem("rw_loaded")
        set_up = sem("set_up")
        sq_ready, sq_used = sem("sq_ready"), sem("sq_used")
        xr_ready, h_ready = sem("xr_ready"), sem("h_ready")
        x_updated = sem("x_updated")
        glu_done = sem("glu_done")
        rope_done = sem("rope_done")
        swapped = sem("swapped")
        short_done = sem("short_done")
        stats_done = sem("stats_done")
        exps_done = sem("exps_done")
        probs_done = sem("probs_done")
        conv_done = sem("conv_done")
        centred = sem("centred")
        lnorm_done = sem("lnorm_done")
        a_done = sem("a_done")
        merged = sem("merged")
        aff_exp, aff_done, pos_done, onehot_done, og_done = (sem(n) for n in (
            "aff_exp", "aff_done", "pos_done", "onehot_done", "og_done"))
        dve_step = sem("dve_step")
        out_stored = sem("out_stored")
        conv_zero = sem("conv_zero")
        h_hi_done, h_split = sem("h_hi_done"), sem("h_split")
        w2_hi_done, w2_used = sem("w2_hi_done"), sem("w2_used")
        w2_split = [sem(f"w2_split{h}") for h in range(2)]
        hid_step = sem("hid_step")
        mix_hi_done, mix_split = sem("mix_hi_done"), sem("mix_split")
        mix_moved = sem("mix_moved")
        w_hi_done, w_split = sem("w_hi_done"), sem("w_split")
        y_hi_done, y_split = sem("y_hi_done"), sem("y_split")
        src_hi_done, src_split = sem("src_hi_done"), sem("src_split")
        x_spilled, x_back = sem("x_spilled"), sem("x_back")

        def bank(*key):
            return ps[jobs[key] % BANKS]

        def full_of(eng, *key, turn=0):
            eng.wait_ge(full[jobs[key] % BANKS], jobs[key] // BANKS + 1 + 3 * turn)

        def drained_of(eng, *key, turn=0):
            eng.wait_ge(drained[jobs[key] % BANKS], jobs[key] // BANKS + 1 + 3 * turn)

        def free_for(eng, *key, turn=0):
            if jobs[key] >= BANKS:
                eng.wait_ge(drained[jobs[key] % BANKS], jobs[key] // BANKS + 3 * turn)

        def is_full(*key):
            return full[jobs[key] % BANKS]

        def is_drained(*key):
            return drained[jobs[key] % BANKS]

        def chunk_here(eng, *key, turn=0):
            slot, loads, _, _ = chunks[key]
            eng.wait_ge(loaded[slot], 16 * loads + 96 * turn)
            return slots[slot]

        def kmaj(ap, n):
            return ap.rearrange("(k p) n -> p k n", p=P)

        def vec_rows(ap, n=P):
            return ap.rearrange("(r n) -> r n", n=n)

        def SQ0(l, norm):
            return 36 * l + (0, 12, 20, 28)[norm]

        def SQU(l, norm):
            return 31 * l + (0, 10, 17, 24)[norm]

        def W_TILE(l, kind, *at):
            if kind == "win":
                n = 4 * at[0] + at[1]
            elif kind == "wo":
                n = 68 + 4 * at[0] + at[1]
            else:
                dp, b, t = at
                i = KT // 2 * b + dp
                n = 24 + (2 * i + t + max(0, i - 4) if t < 2 else 2 * (i + 1) + i - 4)
            return 76 * l + n

        def src_tile(b, k, l, of):
            a = of[b]
            if of is not src_f32:
                a = a[:, :].rearrange("p (k t) -> p k t", k=CT) if b < 3 else a[:, :].rearrange("p (i n) -> p i n", i=TT)
            if b < 3:
                return a[:, k, 0:TOK if l == 0 else SEQ]
            return a[:, 0:TT if l == 0 else LT, k * P:(k + 1) * P]

        def src_part(b, k, part, of):
            if b < 3:
                return src_tile(b, k, 0, of)[:, part[1]:part[1] + part[2]]
            i0, i1 = (0, LT) if part[0] == 0 else (LT, TT)
            return src_tile(b, k, 0, of)[:, i0:i1, :]

        def y_hi(k):
            return y_hi_r[k // 4][:, k % 4 * TOK:(k % 4 + 1) * TOK]

        W2_USED = 8 * NE + 4
        SQLN, SQLNU = (8, 44), (7, 38)
        PROBS0 = (0, len(att_units(0)))
        ONEHOT, POS, CONV = (TT, TT + LT), (2, 3), (2 * CT, 3 * CT)

        def GLU(l, t, part):
            return 2 * t + part if l == 0 else 2 * CT + t

        def gather_out(eng, l, k, m, ns, copy):
            dst = xgy[:, 4 * KT * ns:(4 + NE) * KT * ns].rearrange("p (e k s) -> p e k s", k=KT, s=ns)
            full_of(eng, "ga", l, k, m)
            if m < 2:
                dst, cap = dst[:, 8 * m:8 * m + 8, k, 0:CAP[0]], CAP[0]
            else:
                dst, cap = dst[:, :, k, CAP[0]:ns], CAP[1]
            copy(dst, bank("ga", l, k, m)[:, :].rearrange("p (e s) -> p e s", s=cap)) \
                .then_inc(is_drained("ga", l, k, m), 1)

        def y_out(eng, l, e, h, turn, copy):
            ns = sum(CAP) if l == 0 else CAP[0]
            full_of(eng, "y", l, e, h, turn=turn)
            col = turn * (4 * KT * ns) + (e // 2 * D + h * 512)
            r = CAP[0] * (e % 2)
            op = copy(xgy[r:r + CAP[0], bass.ds(col, 512)], bank("y", l, e, h)[0:CAP[0], :])
            if l == 0:
                col = turn * (4 * KT * ns) + (2 * D + h * 512)
                op = copy(xgy[CAP[1] * e:CAP[1] * (e + 1), bass.ds(col, 512)], bank("y", l, e, h)[CAP[0]:ns, :])
            op.then_inc(is_drained("y", l, e, h), 1)

        def y_rows(l, part, p):
            ns = sum(CAP) if l == 0 else CAP[0]
            first = p // 2 * 4 * KT * ns + p % 2 * D if part == 0 else p * 4 * KT * ns + 2 * D
            return xgy[:, first:first + D]

        def w2_quarter(e, h, q):
            return 8 * e + 4 * h + q, slice(2 * q, 2 * q + 2)

        def w2_slot(l, e, h, of):
            return of[chunks["ex", l, e, 4 + h][0]][:, :].rearrange("p (k n) -> p k n", k=KT)

        def upper_parts(eng, l, e, h, turn):
            chunk_here(eng, "ex", l, e, 4 + h, turn=turn)
            for q in range(4):
                n, rows = w2_quarter(e, h, q)
                eng.wait_ge(w2_used, W2_USED * l + n + 1 + 32 * turn)
                eng.activation(w2_hi[:, rows, :], w2_slot(l, e, h, slots)[:, rows, :], ACT.Copy).then_inc(w2_hi_done, 1)

        def lower_parts(eng, l, e, h, turn):
            chunk_here(eng, "ex", l, e, 4 + h, turn=turn)
            for q in range(4):
                n, rows = w2_quarter(e, h, q)
                eng.wait_ge(w2_hi_done, 8 * NE * l + n + 1 + 32 * turn)
                eng.tensor_tensor(w2_slot(l, e, h, slots_lo)[:, rows, :], w2_slot(l, e, h, slots)[:, rows, :],
                                  w2_hi[:, rows, :].bitcast(F32), ALU.subtract).then_inc(w2_split[h], 1)

        def w2_here(eng, l, e, h, q, turn):
            eng.wait_ge(w2_split[h], 4 * NE * l + 4 * e + q + 1 + 16 * turn)

        def w_tile(key, t, rounded):
            slot = chunks[key][0]
            if key[0] == "mg" and t == 2:
                full32, lo = (a[slot][:, 2048:3072].rearrange("p (k n) -> p k n", k=CT) for a in (slots, slots_lo))
                hi = a_r[:, slot * D:(slot + 1) * D].rearrange("p (k n) -> p k n", k=CT)
                return (hi, lo) if rounded else full32
            n = 256 if key[0] == "mg" else 512
            cols = slice(t * P, (t + 1) * P)
            full32 = slots[slot][:, 0:KT * n].rearrange("p (k n) -> p k n", k=KT)[:, :, cols]
            if not rounded:
                return full32
            lo = slots_lo[slot][:, 0:KT * n].rearrange("p (k n) -> p k n", k=KT)[:, :, cols]
            if key[0] != "mg":
                hi = w_hi[t]
            elif t == 0:
                hi = slots_lo[slot][:, 3072:4096].rearrange("p (k n) -> p k n", k=KT)
            else:
                hi = w_hi[slot]
            return hi, lo

        def upper_tile(eng, key, t):
            chunk_here(eng, *key)
            if key[0] == "win" and key[2]:
                full_of(eng, "win", key[1], key[2] - 1, t, parts_of(key[1])[-1][0])
            if key[0] == "wo" and key[2]:
                full_of(eng, "wo", key[1], t, parts_of(key[1])[-1][0])
            elif key[0] == "wo" and t:
                full_of(eng, "w", key[1], KT // 2 - 1, 3, 1, parts_of(key[1])[-1][0])
            if key[0] == "mg" and t == 2 and key[2:] == (0, 1):
                full_of(eng, "w", key[1], KT // 2 - 1, 0, 1, parts_of(key[1])[-1][0])
            eng.activation(w_tile(key, t, True)[0], w_tile(key, t, False), ACT.Copy).then_inc(w_hi_done, 1)

        def lower_tile(eng, key, t):
            chunk_here(eng, *key)
            eng.wait_ge(w_hi_done, W_TILE(key[1], key[0], *key[2:], t) + 1)
            hi, lo = w_tile(key, t, True)
            eng.tensor_tensor(lo, w_tile(key, t, False), hi.bitcast(F32), ALU.subtract).then_inc(w_split, 1)

        def upper_src(eng, l, b, k):
            if b == 3:
                full_of(eng, "w", l, KT // 2 - 1, 1, 1, parts_of(l)[-1][0])
            eng.activation(src_tile(b, k, l, src_hi), src_tile(b, k, l, src_f32), ACT.Copy).then_inc(src_hi_done, 1)

        def lower_src(eng, l, b, k):
            eng.wait_ge(src_hi_done, 3 * CT * l + CT * (b - 1) + k + 1)
            eng.tensor_tensor(src_tile(b, k, l, src_lo), src_tile(b, k, l, src_f32),
                              src_tile(b, k, l, src_hi).bitcast(F32), ALU.subtract).then_inc(src_split, 1)

        layer_of_stream = {k: (0 if k[0] == "ada" else k[1]) for k in chunks}
        block = ctx.enter_context(nc.Block())

        def slot_view(key, k, n, at=0):
            return slots[chunks[key][0]][:, at:at + k * n].rearrange("p (k n) -> p k n", k=k)

        def expert_src(l, e, m):
            w = A["exp_w1"] if m in (0, 2) else A["exp_w3"] if m in (1, 3) else A["exp_w2"]
            h = m // 2 if m < 4 else m - 4
            return w[l].rearrange("e (k p) n -> e p k n", p=P)[e, :, :, h * 512:(h + 1) * 512]

        def expert_load(eng, l, turn, c):
            (e, m), nxt = divmod(c, 6), divmod(c + 4, 6)
            full_of(eng, *chunks["ex", l, e, m][2], turn=turn)
            eng.dma_start(slot_view(("ex", l, e, m), KT, 512),
                          expert_src(l, 4 * turn + nxt[0], nxt[1])).then_inc(loaded[c % 4], 16)

        def weight_stream(eng, between):
            def slot_free(key):
                prev = chunks[key][3]
                if prev is not None:
                    full_of(eng, *chunks[prev][2])

            for l in range(DEPTH):
                for key in chunks:
                    kind, at = key[0], key[2:]
                    if kind == "ex" or layer_of_stream[key] != l:
                        continue
                    between(key)
                    slot_free(key)
                    here = loaded[chunks[key][0]]
                    if kind == "ada":
                        src = kmaj(A["ada_w"][key[1]][:, at[0] * 512:(at[0] + 1) * 512], 512)
                    elif kind == "win":
                        lo, n = WCHUNKS[at[0]]
                        src = kmaj(A["w_in"][l][:, lo:lo + n], n)
                    elif kind == "wo":
                        src = kmaj(A["w_o"][l][:, at[0] * 512:(at[0] + 1) * 512], 512)
                    else:
                        dp, b = at
                        lo = O_G + b * D + dp * 256
                        eng.dma_start(slot_view(key, KT, 256), kmaj(A["w_in"][l][:, lo:lo + 256], 256)) \
                            .then_inc(here, 16)
                        w = A[("w_a_out", "w_b_out", "w_c_out", "w_d_out")[b]]
                        eng.dma_start(slot_view(key, CT, 256, 2048), kmaj(w[l][:, dp * 256:dp * 256 + 256], 256)) \
                            .then_inc(here, 16)
                        continue
                    eng.dma_start(slot_view(key, KT, src.shape[2]), src).then_inc(here, 16)
                for m in range(4):
                    slot_free(("ex", l, 0, m))
                    if m == 2:
                        full_of(eng, "ga", l, KT - 1, 2 if l == 0 else 1)
                    eng.dma_start(slot_view(("ex", l, 0, m), KT, 512), expert_src(l, 0, m)).then_inc(loaded[m], 16)
                with eng.Fori(0, NE // 4 - 1) as turn:
                    for c in range(0, 24, 2):
                        expert_load(eng, l, turn, c)
                for c in range(0, 20, 2):
                    expert_load(eng, l, NE // 4 - 1, c)

        @block.sync
        def _(sp):
            for i in range(TT):
                src = A["x"][0, i * P:(i + 1) * P, :] if i < LT else A["ctx"][0, (i - LT) * P:(i - LT + 1) * P, :]
                sp.dma_start(x_tok[:, i, :], src).then_inc(x_loaded, 16)

            def tables(key):
                if key[0] == "win" and key[2] == C_F:
                    full_of(sp, "win", key[1], C_Q, CT - 1, parts_of(key[1])[-1][0])
                    sp.dma_start(hb2[:, 0:5376], K["dft"]).then_inc(dft_loaded, 16)

            weight_stream(sp, tables)
            for i in range(LT):
                drained_of(sp, "out", i, 0)
                drained_of(sp, "out", i, 1)
                sp.dma_start(out[0, i * P:(i + 1) * P, :], h_tok[:, i, :]).then_inc(out_stored, 16)
            sp.wait_ge(out_stored, 16 * LT)

        @block.gpsimd
        def _(pool):
            pool.memset(eps_t, EPS).then_inc(set_up, 1)

            for l in range(DEPTH):
                if l:
                    full_of(pool, "rl", l - 1)
                pool.dma_start(rw, kmaj(A["router_w"][l], NE)).then_inc(rw_loaded, 16)
                both = parts_of(l)
                if l:
                    pool.wait_ge(x_updated, 8 * 2 * l)
                else:
                    for i in range(TT):
                        for h in range(2):
                            drained_of(pool, "xin", i, h)
                n = TOK if l == 0 else SEQ
                lower_tile(pool, ("win", l, 0), 0)
                pool.dma_start(x_dram[:, :, 0:n], x_t[:, :, 0:n]).then_inc(x_spilled, 16)
                for k in range(KT):
                    pool.wait_ge(mix_hi_done, KT * l + k + 1)
                    if k == 0:
                        pool.wait_ge(x_spilled, 16 * (l + 1))
                    pool.tensor_tensor(mix_lo[:, k, :], h_t[:, k, :], mix_hi1[:, k, :].bitcast(F32), ALU.subtract) \
                        .then_inc(mix_split, 1)
                for c in range(C_KV):
                    for t in range(0 if c else 1, CT):
                        lower_tile(pool, ("win", l, c), t)

                def y_lower(dp):
                    for k in (2 * dp, 2 * dp + 1):
                        pool.wait_ge(y_hi_done, KT * l + k + 1)
                        pool.tensor_tensor(mix_hi1[:, k, 0:n], y_t[:, k, 0:n], y_hi(k)[:, 0:n].bitcast(F32),
                                           ALU.subtract).then_inc(y_split, 1)

                for t in range(2):
                    lower_tile(pool, ("mg", l, 0, 0), t)
                for b in range(4):
                    for dp in range(KT // 2):
                        if b:
                            lower_tile(pool, ("mg", l, dp, b), 2)
                        if b < 3:
                            lower_src(pool, l, b + 1, dp)
                        if (dp, b) != (KT // 2 - 1, 3):
                            for t in range(2):
                                lower_tile(pool, ("mg", l, (dp + 1) % 4, b + (dp == 3)), t)
                        if b == 3 and dp:
                            y_lower(dp - 1)
                lower_tile(pool, ("wo", l, 0), 0)
                y_lower(KT // 2 - 1)
                full_of(pool, "g", l, KT // 2 - 1, 3, 1, both[-1][0])
                pool.dma_start(x_t[:, :, 0:n], x_dram[:, :, 0:n]).then_inc(x_back, 16)
                for h in range(2):
                    for t in range(CT):
                        if h or t:
                            lower_tile(pool, ("wo", l, h), t)
                nt, last = (TT, 2) if l == 0 else (LT, 1)
                for i in range(nt):
                    pool.wait_ge(h_hi_done, TT * l + i + 1)
                    pool.tensor_tensor(h_lo[:, i, :], h_tok[:, i, :], h_hi[:, i, :].bitcast(F32), ALU.subtract) \
                        .then_inc(h_split, 1)
                full_of(pool, "ga", l, KT - 1, last)
                pool.memset(spare, 0.0).then_inc(w2_used, 4)
                with pool.Fori(0, NE // 4) as turn:
                    for e in range(4):
                        lower_parts(pool, l, e, 0, turn)

        @block.tensor
        def _(pe):
            def chan_sum(l, norm, job, weights, tiles, parts, ready):
                for part in parts:
                    free_for(pe, job, *norm, part[0])
                for k in range(tiles):
                    ready(k)
                    for part in parts:
                        mm = pe.matmul(bank(job, *norm, part[0])[:, 0:part[2]], weights,
                                       sq[k % 2][:, part[1]:part[1] + part[2]], start=(k == 0), stop=(k == tiles - 1))
                        if k == tiles - 1:
                            mm.then_inc(is_full(job, *norm, part[0]), 1)
                    if k < tiles - 1:
                        mm.then_inc(sq_used, 1)

            def mean_square(l, norm):
                if norm in (POST_MIX, POST_FFN):
                    pe.wait_ge(sq_used, SQU(l, norm) + KT - 1)
                    for part in parts_of(l, norm):
                        product(("ms", l, norm, part[0]), lambda k: ones_d, 1,
                                lambda k: rb[:, part[1]:part[1] + part[2]], part[2])
                    return
                chan_sum(l, (l, norm), "ms", ones_d, KT, parts_of(l, norm),
                         lambda k: pe.wait_ge(sq_ready, SQ0(l, norm) + k + 1))

            def product(key, wt, k_tiles, rhs, n, first=True):
                free_for(pe, *key)
                for k in range(k_tiles):
                    mm = pe.matmul(bank(*key)[:, 0:n], wt(k), rhs(k), start=(k == 0), stop=(k == k_tiles - 1))
                mm.then_inc(is_full(*key), 1)

            def split_product(key, w, h, n, ready=None, k_tiles=KT):
                (w_up, w_low), (h_up, h_low) = w, h
                free_for(pe, *key)
                for k in range(k_tiles):
                    if ready:
                        ready(k)
                    out_ = bank(*key)[:, 0:n]
                    pe.matmul(out_, w_up[:, k, :], h_up(k), start=(k == 0), stop=False)
                    pe.matmul(out_, w_up[:, k, :], h_low(k), start=False, stop=False)
                    mm = pe.matmul(out_, w_low[:, k, :], h_up(k), start=False, stop=(k == k_tiles - 1))
                mm.then_inc(is_full(*key), 1)

            pe.wait_ge(ident_loaded, 16)
            pe.wait_ge(x_loaded, 16 * TT)
            for i in range(TT):
                for h in range(2):
                    free_for(pe, "xin", i, h)
                    for k in range(4):
                        mm = pe.transpose(bank("xin", i, h)[:, k * P:(k + 1) * P],
                                          x_tok[:, i, (4 * h + k) * P:(4 * h + k + 1) * P], ident)
                    mm.then_inc(is_full("xin", i, h), 1)
            pe.wait_ge(par_loaded, 16 * 25)
            pe.wait_ge(const_loaded, 16 * 7)
            for l in range(DEPTH):
                for r, n in enumerate((NR1, NR2, NR3)):
                    free_for(pe, "par", l, r)
                    pe.transpose(bank("par", l, r)[:, 0:n], par_rows[0:n, 3 * l + r, :], ident[0:n, 0:n]) \
                        .then_inc(is_full("par", l, r), 1)
            free_for(pe, "cin", 0)
            pe.transpose(bank("cin", 0)[:, 0:2 * KT], par_rows[0:2 * KT, 6, :], ident[0:2 * KT, 0:2 * KT]) \
                .then_inc(is_full("cin", 0), 1)
            drained_of(pe, "cin", 0)

            def modulation_row(l, c):
                w = chunk_here(pe, "ada", l, c).rearrange("p (k n) -> p k n", k=KT)
                free_for(pe, "mrow", l, c)
                for k in range(KT):
                    mm = pe.matmul(bank("mrow", l, c)[0:2, :], c_t[:, 2 * k:2 * k + 2], w[:, k, :],
                                   start=(k == 0), stop=(k == KT - 1))
                mm.then_inc(is_full("mrow", l, c), 1)

            def turn_row(l, c, row):
                free_for(pe, "mod", l, c)
                drained_of(pe, "mrow", l, c)
                for t in range(4):
                    mm = pe.transpose(bank("mod", l, c)[:, 2 * t:2 * t + 2], row[:, t * P:(t + 1) * P], ident[0:2, 0:2])
                mm.then_inc(is_full("mod", l, c), 1)

            def modulation(*key):
                if row_before(key):
                    turn_row(*row_before(key), mod_row)
                if key in ROW_AT:
                    modulation_row(*ROW_AT[key])
                if key not in MOD_AT:
                    return
                l, c = MOD_AT[key]
                w = chunk_here(pe, "ada", l, c).rearrange("p (k n) -> p k n", k=KT)
                free_for(pe, "mod", l, c)
                for t in range(4):
                    for k in range(KT):
                        mm = pe.matmul(bank("mod", l, c)[:, 2 * t:2 * t + 2], w[:, k, t * P:(t + 1) * P],
                                       c_t[:, 2 * k:2 * k + 2], start=(k == 0), stop=(k == KT - 1))
                mm.then_inc(is_full("mod", l, c), 1)

            def layer(l):
                both = parts_of(l)
                mean_square(l, PRE_MIX)
                if l == 0:
                    for c in range(MOD_FIRST):
                        modulation_row(l, c)
                        turn_row(l, c, mod_rows[:, c * 512:(c + 1) * 512])
                def rotary(t):
                    drained_of(pe, *(("win", l, C_Q, t, 0) if t < CT else ("k", l, 0)))
                    product(("rope", l, t), lambda k: perm, 1,
                            lambda k: q_t[:, t, 0:SEQ] if t < CT else k_t[:, 0, 0:SEQ], SEQ)

                for c in range(C_KV):
                    for t in range(CT):
                        pe.wait_ge(w_split, W_TILE(l, "win", c, t) + 1)
                        for part in both:
                            cols = slice(part[1], part[1] + part[2])
                            first = c == 0 and t == 0 and part is LAT
                            split_product(("win", l, c, t, part[0]), w_tile(("win", l, c), t, True),
                                          (lambda k: mix_hi1[:, k, cols], lambda k: mix_lo[:, k, cols]), part[2],
                                          (lambda k: pe.wait_ge(mix_split, KT * l + k + 1)) if first else None)
                        if c == C_Q and t:
                            rotary(t - 1)
                pe.wait_ge(h_ready, 8 * (2 * l + 1))
                w = chunk_here(pe, "win", l, C_KV)[:, 0:KT * 256].rearrange("p (k n) -> p k n", k=KT)
                for part in (LAT, CON):
                    product(("k", l, part[0]), lambda k: w[:, k, 0:P], KT,
                            lambda k: h_t[:, k, part[1]:part[1] + part[2]], part[2])
                    rotary(CT - 1 + part[0])
                for part, first, n in ((0, 0, LT), (1, LT, CTT)):
                    free_for(pe, "v", l, part)
                    for i in range(n):
                        for k in range(KT):
                            mm = pe.matmul(bank("v", l, part)[:, i * P:(i + 1) * P],
                                           h_t[:, k, (first + i) * P:(first + i + 1) * P], w[:, k, P:2 * P],
                                           start=(k == 0), stop=(k == KT - 1))
                    mm.then_inc(is_full("v", l, part), 1)
                w = chunk_here(pe, "win", l, C_F).rearrange("p (k n) -> p k n", k=KT)
                for i in range(TT if l == 0 else LT):
                    product(("f", l, i), lambda k: h_t[:, k, i * P:(i + 1) * P], KT, lambda k: w[:, k, :], DC)
                pe.wait_ge(dft_loaded, 16 * (l + 1))

                def fourier_out(g):
                    for part in both:
                        drained_of(pe, "fc", l, g, part[0])
                        drained_of(pe, "fs", l, g, part[0])
                        key = ("fo", l, g, part[0])
                        free_for(pe, *key)
                        cols = slice(part[1], part[1] + part[2])
                        pe.matmul(bank(*key)[:, 0:part[2]], c128, xc[g % 2][:, cols], start=True, stop=False)
                        pe.matmul(bank(*key)[:, 0:part[2]], s128, xs[g % 2][:, cols], start=False, stop=True) \
                            .then_inc(is_full(*key), 1)

                drained_of(pe, "f", l, (TT if l == 0 else LT) - 1)
                drained_of(pe, "f", l, (TT if l == 0 else LT) - 2)
                for g in range(CT):
                    for part in both:
                        first, n = (0, LT) if part[0] == 0 else (LT, CTT)
                        tabs = (c512, s512) if part[0] == 0 else (c256, s256)
                        for name, tab in zip(("fc", "fs"), tabs):
                            product((name, l, g, part[0]), lambda k: f_tok[:, first + k, g * P:(g + 1) * P], n,
                                    lambda k: tab[:, k, :], part[2])
                    modulation("fo", l, g)
                    if g:
                        fourier_out(g - 1)
                fourier_out(CT - 1)
                units = att_units(l)
                pe.wait_ge(rope_done, 5 * (l + 1))
                pe.wait_ge(swapped, 2 * (l + 1))
                for t in range(CT):
                    if l == 0:
                        drained_of(pe, "win", l, C_Q, t, 1)
                drained_of(pe, "v", l, 0)
                drained_of(pe, "v", l, 1)

                def scores(u):
                    con, n, g = units[u]
                    lo, hi, _ = band(units[u])
                    col = SEQ * con + n * P
                    for h in range(GRP):
                        head = GRP * g + h
                        r = HD * (head % 2)
                        keys = k_t[r:r + HD, 0 if head % 2 == g else 1, :]
                        q = q_t[r:r + HD, head // 2, col:col + P]
                        if not con:
                            key = ("sl", l, u, h)
                            free_for(pe, *key)
                            pe.matmul(bank(*key)[:, 0:(hi - lo) * P], q, keys[:, lo * P:hi * P],
                                      start=True, stop=True).then_inc(is_full(*key), 1)
                        key = ("sc", l, u, h)
                        free_for(pe, *key)
                        pe.matmul(bank(*key)[:, 0:CTX], q, keys[:, SEQ:TOK],
                                  start=True, stop=True).then_inc(is_full(*key), 1)

                def values(u):
                    con, n, g = units[u]
                    lo, hi, nk = band(units[u])
                    tiles = list(range(lo, hi)) + list(range(LT, TT))
                    for kt in range(nk):
                        free_for(pe, "pt", l, u, kt)
                        if kt == 0:
                            pe.wait_ge(probs_done, PROBS0[l] + u + 1)
                        for h in range(GRP):
                            mm = pe.transpose(bank("pt", l, u, kt)[:, h * P:(h + 1) * P],
                                              S_buf[u % 2][:, h, kt * P:(kt + 1) * P], ident)
                        mm.then_inc(is_full("pt", l, u, kt), 1)
                    free_for(pe, "av", l, u)
                    for kt in range(nk):
                        drained_of(pe, "pt", l, u, kt)
                        mm = pe.matmul(bank("av", l, u)[0:HD, :], v_tok[:, tiles[kt], g * HD:(g + 1) * HD],
                                       probs_t[:, kt, :], start=(kt == 0), stop=(kt == nk - 1))
                    mm.then_inc(is_full("av", l, u), 1)

                scores(0)
                for u in range(len(units)):
                    if u + 1 < len(units):
                        scores(u + 1)
                    modulation("att", l, u)
                    values(u)
                modulation("rows", l)
                pe.wait_ge(conv_done, CONV[l])
                for part in both:
                    product(("lm", l, part[0]), lambda k: ones_c, CT,
                            lambda k: a_t[:, k, part[1]:part[1] + part[2]], part[2])
                chan_sum(l, (l,), "lv", ones_c, CT, both, lambda k: pe.wait_ge(sq_ready, SQLN[l] + k + 1))
                modulation("lv", l)
                for b in range(4):
                    for dp in range(KT // 2):
                        w = chunk_here(pe, "mg", l, dp, b)
                        wb = w[:, 2048:3072].rearrange("p (k n) -> p k n", k=CT)
                        if dp == 0 and b == 0:
                            pe.wait_ge(mix_moved, KT * (l + 1))
                            pe.wait_ge(a_done, 4 * (l + 1))
                            pe.wait_ge(short_done, 4 * (l + 1))
                            for u in range(len(units) - 2, len(units)):
                                drained_of(pe, "av", l, u)
                            for part in both:
                                drained_of(pe, "fo", l, CT - 1, part[0])
                        for t in range(2):
                            pe.wait_ge(w_split, W_TILE(l, "mg", dp, b, t) + 1)
                            for part in both:
                                cols = slice(part[1], part[1] + part[2])
                                split_product(("g", l, dp, b, t, part[0]), w_tile(("mg", l, dp, b), t, True),
                                              (lambda k: mix_hi2[:, k, cols], lambda k: mix_lo[:, k, cols]), part[2])
                                key = ("w", l, dp, b, t, part[0])
                                at_t = slice(t * P, (t + 1) * P)
                                if b == 0:
                                    product(key, lambda k: wb[:, k, at_t], CT, lambda k: a_t[:, k, cols], part[2])
                                    continue
                                pe.wait_ge(w_split, W_TILE(l, "mg", dp, b, 2) + 1)
                                pe.wait_ge(src_split, 3 * CT * l + CT * b)
                                split_product(key, [a[:, :, at_t] for a in w_tile(("mg", l, dp, b), 2, True)],
                                              (lambda k: src_part(b, k, part, src_hi),
                                               lambda k: src_part(b, k, part, src_lo)), part[2], k_tiles=CT)
                for h in range(2):
                    for t in range(CT):
                        pe.wait_ge(w_split, W_TILE(l, "wo", h, t) + 1)
                        for part in both:
                            cols = slice(part[1], part[1] + part[2])
                            first = h == 0 and t == 0 and part is LAT
                            split_product(("wo", l, CT * h + t, part[0]), w_tile(("wo", l, h), t, True),
                                          (lambda k: y_hi(k)[:, cols], lambda k: mix_hi1[:, k, cols]), part[2],
                                          (lambda k: pe.wait_ge(y_split, KT * l + k + 1)) if first else None)
                mean_square(l, POST_MIX)
                modulation("post", l)
                mean_square(l, PRE_FFN)
                modulation("pre", l, 0)
                modulation("pre", l, 1)
                nt = TT if l == 0 else LT
                pe.wait_ge(h_ready, 8 * (2 * l + 2))
                pe.wait_ge(rw_loaded, 16 * (l + 1))
                free_for(pe, "rl", l)
                for i in range(nt):
                    for k in range(KT):
                        mm = pe.matmul(bank("rl", l)[:, i * NE:(i + 1) * NE], h_t[:, k, i * P:(i + 1) * P],
                                       rw[:, k, :], start=(k == 0), stop=(k == KT - 1))
                mm.then_inc(is_full("rl", l), 1)
                for key, lo, hi in ((("at", l, 0), 0, LT), (("at", l, 1), LT, TT)):
                    if key in jobs:
                        free_for(pe, *key)
                        pe.wait_ge(aff_done, l + 1)
                        for i in range(lo, hi):
                            mm = pe.transpose(bank(*key)[0:NE, (i - lo) * P:(i - lo + 1) * P], aff[:, i, :], ident)
                        mm.then_inc(is_full(*key), 1)
                for i in range(nt):
                    for h in range(2):
                        free_for(pe, "ht", l, i, h)
                        for k in range(4):
                            mm = pe.transpose(bank("ht", l, i, h)[:, k * P:(k + 1) * P],
                                              h_t[:, 4 * h + k, i * P:(i + 1) * P], ident)
                        mm.then_inc(is_full("ht", l, i, h), 1)
                modulation("ht", l)
                free_for(pe, "pos", l)
                pe.wait_ge(pos_done, POS[l])
                for i in range(nt):
                    mm = pe.transpose(bank("pos", l)[:, i * NE:(i + 1) * NE], sel_e[0:NE, 3, i * P:(i + 1) * P],
                                      ident[0:NE, 0:NE])
                mm.then_inc(is_full("pos", l), 1)
                for i in range(nt):
                    for h in range(2):
                        drained_of(pe, "ht", l, i, h)
                pe.wait_ge(onehot_done, ONEHOT[l])
                pe.wait_ge(h_split, TT * l + nt)
                for k in range(KT):
                    for m in range(3 if l == 0 else 2):
                        sel = onehot_r[0][:, :, m * 512:(m + 1) * 512] if m < 2 else onehot_r[1]
                        first = 0 if m < 2 else LT
                        product(("ga", l, k, m),
                                lambda i: (h_hi, h_lo)[i % 2][:, first + i // 2, k * P:(k + 1) * P],
                                2 * (LT if m < 2 else CTT), lambda i: sel[:, i // 2, :], 512)
                for m in range(3 if l == 0 else 2):
                    for k in range(KT - 3, KT):
                        drained_of(pe, "ga", l, k, m)
                ns = sum(CAP) if l == 0 else CAP[0]

                with pe.Fori(0, NE // 4) as turn:
                    for e in range(4):
                        for h in range(2):
                            for m, name in enumerate(("h1", "h3")):
                                w = chunk_here(pe, "ex", l, e, 2 * h + m, turn=turn) \
                                    .rearrange("p (k n) -> p k n", k=KT)
                                free_for(pe, name, l, e, h, turn=turn)
                                for f in range(4):
                                    for k in range(KT):
                                        x0 = (turn * 4 + (e + 4)) * (KT * ns) + k * ns
                                        mm = pe.matmul(bank(name, l, e, h)[:, f * ns:(f + 1) * ns],
                                                       w[:, k, f * P:(f + 1) * P], xgy[:, bass.ds(x0, ns)],
                                                       start=(k == 0), stop=(k == KT - 1))
                                mm.then_inc(is_full(name, l, e, h), 1)
                        for h in range(2):
                            lo = slots_lo[chunks["ex", l, e, 4 + h][0]][:, :].rearrange("p (k n) -> p k n", k=KT)
                            y = bank("y", l, e, h)[:, :]
                            free_for(pe, "y", l, e, h, turn=turn)
                            for f in range(KT):
                                if f % 2 == 0:
                                    w2_here(pe, l, e, h, f // 2, turn)
                                if h == 0 and f in (0, 3):
                                    drained_of(pe, "h3", l, e, f // 3, turn=turn)
                                at_f = slice(f * ns, f * ns + P)
                                pe.matmul(y, hid_hi[:, at_f], w2_hi[:, f, :], start=(f == 0), stop=False)
                                mm = pe.matmul(y, hid_lo[:, at_f], w2_hi[:, f, :], start=False, stop=False)
                                if f % 2:
                                    mm.then_inc(w2_used, 1)
                                mm = pe.matmul(y, hid_hi[:, at_f], lo[:, f, :], start=False, stop=(f == KT - 1))
                            mm.then_inc(is_full("y", l, e, h), 1)
                pe.wait_ge(og_done, ONEHOT[l])
                for part, npair, ntile, in ((0, NE // 2, LT), (1, NE // 4, CTT))[:len(both)]:
                    for p in range(npair):
                        key = ("sg", l, p, part)
                        free_for(pe, *key)
                        for i in range(ntile):
                            mm = pe.transpose(bank(*key)[:, i * P:(i + 1) * P],
                                              onehot[part][:, i, p * P:(p + 1) * P], ident)
                        mm.then_inc(is_full(*key), 1)
                for part, npair in ((0, NE // 2), (1, NE // 4))[:len(both)]:
                    for p in range(npair):
                        drained_of(pe, "sg", l, p, part)
                for h in range(2):
                    drained_of(pe, "y", l, NE - 1, h)
                    drained_of(pe, "y", l, NE - 2, h)
                for k in range(KT):
                    for part in both:
                        product(("mo", l, k, part[0]),
                                lambda p: y_rows(l, part[0], p)[:, k * P:(k + 1) * P],
                                (NE // 2, NE // 4)[part[0]], lambda p: sg[part[0]][:, p, :], part[2])
                mean_square(l, POST_FFN)

            for l in range(DEPTH):
                layer(l)
            pe.wait_ge(x_updated, 8 * 2 * DEPTH)
            for i in range(LT):
                for h in range(2):
                    free_for(pe, "out", i, h)
                    for k in range(4):
                        mm = pe.transpose(bank("out", i, h)[:, k * P:(k + 1) * P],
                                          x_t[:, 4 * h + k, i * P:(i + 1) * P], ident)
                    mm.then_inc(is_full("out", i, h), 1)

        @block.scalar
        def _(act):
            def square(l, norm, src, k):
                if k >= 2:
                    act.wait_ge(sq_used, SQU(l, norm) + (k - 1 if norm in (PRE_MIX, PRE_FFN) else max(k - 2, 1)))
                n = TOK if len(parts_of(l, norm)) == 2 else SEQ
                act.activation(sq[k % 2][:, 0:n], src[:, k, 0:n], ACT.Square).then_inc(sq_ready, 1)

            def squares(l, norm, src, ready):
                for k in range(KT):
                    ready(k)
                    square(l, norm, src, k)
                roots(("ms", l, norm), parts_of(l, norm))

            def roots(key, parts):
                for part in parts:
                    full_of(act, *key, part[0])
                    act.activation(rb[:, part[1]:part[1] + part[2]], bank(*key, part[0])[:, 0:part[2]], ACT.Sqrt,
                                   bias=eps_t).then_inc(is_drained(*key, part[0]), 1)

            def row_out(*key):
                if key in ROW_AT:
                    full_of(act, "mrow", *ROW_AT[key])
                    act.activation(mod_row, bank("mrow", *ROW_AT[key])[0:2, :], ACT.Copy) \
                        .then_inc(is_drained("mrow", *ROW_AT[key]), 1)

            def modulated(l, norm):
                mix = norm == PRE_MIX
                pi = 2 * l + (0 if mix else 1)
                if mix:
                    for t in range(CT):
                        upper_tile(act, ("win", l, 0), t)
                    for k in range(KT):
                        act.wait_ge(h_ready, 8 * pi + k + 1)
                        act.activation(mix_hi1[:, k, :], h_t[:, k, :], ACT.Copy).then_inc(mix_hi_done, 1)
                    return
                for k in range(KT):
                    act.wait_ge(xr_ready, 8 * pi + k + 1)
                    parts = parts_of(l, norm)
                    for part in parts:
                        w, cols = part[0], slice(part[1], part[1] + part[2])
                        op = act.activation(h_t[:, k, cols], sq[k % 2][:, cols], ACT.Identity,
                                            scale=scl[l][:, 2, k, w:w + 1], bias=mods[l][:, 24 + k, w:w + 1])
                    op.then_inc(h_ready, 1)

            act.dma_start(ident, K["ident"]).then_inc(ident_loaded, 16)
            act.dma_start(ones_d, K["ones_d"]).then_inc(const_loaded, 16)
            for l in range(DEPTH):
                r = 3 * l
                for row, name, n in ((R_ADAB, "ada_b", 48), (R_PM, "pre_mix_g", 8), (R_QM, "post_mix_g", 8),
                                     (R_PF, "pre_ffn_g", 8), (R_QF, "post_ffn_g", 8), (R_GB, "gate_b", 32),
                                     (R_CB, "conv_a_b", 4), (R_LG, "ln_a_g", 4), (R_LB, "ln_a_b", 4)):
                    act.dma_start(par_rows[row:row + n, r, :], vec_rows(A[name][l])).then_inc(par_loaded, 16)
                act.dma_start(par_rows[0:NR2, r + 1, :],
                              A["conv_a_w"][l].rearrange("k (t n) -> (k t) n", n=P)).then_inc(par_loaded, 16)
                act.dma_start(par_rows[0:NR3, r + 2, :],
                              A["conv_b_w"][l].rearrange("k (t n) -> (k t) n", n=P)).then_inc(par_loaded, 16)
            act.dma_start(par_rows[0:KT, 6, :], vec_rows(A["c"][0])).then_inc(par_loaded, 16)
            act.dma_start(par_rows[KT:2 * KT, 6, :], vec_rows(A["c_ctx"])).then_inc(par_loaded, 16)
            act.dma_start(nsink, A["sink"].rearrange("(a l) h -> a (l h)", a=1).broadcast_to([P, DEPTH * HEADS])) \
                .then_inc(par_loaded, 16)
            for dst, src in ((ones_c, "ones_c"), (perm, "perm"), (cosT, "cos"), (sinT, "sin"), (maskT, "mask"),
                             (iota, "iota")):
                act.dma_start(dst, K[src]).then_inc(const_loaded, 16)
            act.wait_ge(set_up, 1)
            for i in range(TT):
                full_of(act, "xin", i, 0)
                act.activation(x_t[:, 0:4, i * P:(i + 1) * P],
                               bank("xin", i, 0)[:, :].rearrange("p (k t) -> p k t", k=4), ACT.Copy) \
                    .then_inc(is_drained("xin", i, 0), 1)
            full_of(act, "cin", 0)
            act.activation(c_t.rearrange("p (k w) -> p w k", w=2),
                           bank("cin", 0)[:, 0:2 * KT].rearrange("p (w k) -> p w k", w=2), ACT.Silu) \
                .then_inc(is_drained("cin", 0), 1)

            def layer(l):
                both = parts_of(l)

                def ready0(k):
                    if l == 0 and k == 0:
                        for i in range(TT):
                            drained_of(act, "xin", i, 0)
                            drained_of(act, "xin", i, 1)
                    if l:
                        act.wait_ge(x_updated, 8 * (2 * l - 1) + k + 1)

                squares(l, PRE_MIX, x_t, ready0)
                if l == 0:
                    for c in range(MOD_FIRST):
                        full_of(act, "mrow", l, c)
                        act.activation(mod_rows[:, c * 512:(c + 1) * 512], bank("mrow", l, c)[0:2, :], ACT.Copy) \
                            .then_inc(is_drained("mrow", l, c), 1)
                modulated(l, PRE_MIX)
                act.wait_ge(conv_zero, l + 1)
                for c in range(C_KV):
                    for t in range(CT):
                        for part in both:
                            key = ("win", l, c, t, part[0])
                            n = part[2]
                            src = bank(*key)[:, 0:n]
                            if c == C_HV:
                                continue
                            full_of(act, *key)
                            fn = ACT.Copy
                            if c == C_AV:
                                dst = cpad[:, t, PADC[0] * part[0] + HC:PADC[0] * part[0] + HC + n]
                            elif c == C_AG:
                                j = GLU(l, t, part[0])
                                if j >= 2:
                                    act.wait_ge(glu_done, j - 1)
                                dst, fn = sq[j % 2][:, 0:n], ACT.Sigmoid
                            elif c == C_BG:
                                dst = b_t[:, t, part[1]:part[1] + n]
                            elif c == C_CG:
                                dst = bpad[:, t, PADS[0] * part[0] + HS:PADS[0] * part[0] + HS + n]
                            else:
                                dst = q_t[:, t, part[1]:part[1] + n]
                            act.activation(dst, src, fn).then_inc(is_drained(*key), 1)
                        if c + 1 < C_KV:
                            upper_tile(act, ("win", l, c + 1), t)
                for part in (LAT, CON):
                    full_of(act, "k", l, part[0])
                    act.activation(k_t[:, 0, part[1]:part[1] + part[2]], bank("k", l, part[0])[:, 0:part[2]],
                                   ACT.Copy).then_inc(is_drained("k", l, part[0]), 1)
                for part, first, n in ((0, 0, LT), (1, LT, CTT)):
                    full_of(act, "v", l, part)
                    act.activation(v_tok[:, first:first + n, :],
                                   bank("v", l, part)[:, 0:n * P].rearrange("p (i n) -> p i n", n=P),
                                   ACT.Copy).then_inc(is_drained("v", l, part), 1)
                for i in range(TT if l == 0 else LT):
                    full_of(act, "f", l, i)
                    act.activation(f_tok[:, i, :], bank("f", l, i)[:, :], ACT.Copy) \
                        .then_inc(is_drained("f", l, i), 1)

                def fourier_out(g):
                    for part in both:
                        key = ("fo", l, g, part[0])
                        i0, i1 = (0, LT) if part[0] == 0 else (LT, TT)
                        full_of(act, *key)
                        act.activation(f_tok[:, i0:i1, g * P:(g + 1) * P],
                                       bank(*key)[:, 0:part[2]].rearrange("p (i n) -> p i n", n=P), ACT.Copy,
                                       ).then_inc(is_drained(*key), 1)

                act.wait_ge(short_done, 4 * (l + 1))
                for g in range(CT):
                    for part in both:
                        cols = slice(part[1], part[1] + part[2])
                        for name, dst in (("fc", xc), ("fs", xs)):
                            full_of(act, name, l, g, part[0])
                            act.activation(dst[g % 2][:, cols], bank(name, l, g, part[0])[:, 0:part[2]], ACT.Copy) \
                                .then_inc(is_drained(name, l, g, part[0]), 1)
                    row_out("fo", l, g)
                    if g:
                        fourier_out(g - 1)
                fourier_out(CT - 1)
                units = att_units(l)

                def ctx_scores(u):
                    lo, hi, nk = band(units[u])
                    nl = (hi - lo) * P
                    if u == 0:
                        full_of(act, "fo", l, CT - 1, both[-1][0])
                    for h in range(GRP):
                        full_of(act, "sc", l, u, h)
                        if u >= 2 and h == 0:
                            full_of(act, "pt", l, u - 2, band(units[u - 2])[2] - 1)
                        act.activation(S_buf[u % 2][:, h, nl:nl + CTX], bank("sc", l, u, h)[:, 0:CTX], ACT.Copy) \
                            .then_inc(is_drained("sc", l, u, h), 1)

                def exps(u):
                    nk = band(units[u])[2]
                    g = units[u][2]
                    act.wait_ge(stats_done, PROBS0[l] + u + 1)
                    act.activation(st[:, 4, :], st[:, 2, :], ACT.Exp).then_inc(exps_done, 1)
                    for h in range(GRP):
                        S = S_buf[u % 2][:, h, 0:nk * P]
                        act.activation(S, S, ACT.Exp, bias=st[:, 1, h:h + 1], scale=HD ** -0.5,
                                       accum_out=st[:, 3, h:h + 1]).then_inc(exps_done, 1)

                def turned(u):
                    con, n, g = units[u]
                    nk = band(units[u])[2]
                    for kt in range(nk):
                        if kt % 2 == 0:
                            full_of(act, "pt", l, u, kt)
                            if u:
                                full_of(act, "av", l, u - 1)
                            act.activation(probs_t[:, kt, :], bank("pt", l, u, kt)[:, :], ACT.Copy) \
                                .then_inc(is_drained("pt", l, u, kt), 1)
                    full_of(act, "av", l, u)
                    o = bank("av", l, u)[0:HD, :].rearrange("p (h r q) -> p r h q", r=2, q=P)
                    col = SEQ * con + n * P
                    act.activation(q_t[0:HD, 2 * g:2 * g + 2, col:col + P], o[:, 0], ACT.Copy)
                    act.activation(q_t[HD:P, 2 * g:2 * g + 2, col:col + P], o[:, 1], ACT.Copy) \
                        .then_inc(is_drained("av", l, u), 1)

                ctx_scores(0)
                for u in range(len(units)):
                    exps(u)
                    if u + 1 < len(units):
                        ctx_scores(u + 1)
                    row_out("att", l, u)
                    turned(u)
                    if u < KT:
                        n = TOK if l == 0 else SEQ
                        act.activation(mix_hi2[:, u, 0:n], h_t[:, u, 0:n], ACT.Copy).then_inc(mix_moved, 1)
                for t in range(2):
                    upper_tile(act, ("mg", l, 0, 0), t)
                for k in range(CT):
                    if k < CT - 1:
                        act.wait_ge(centred, (CT - 1) * l + k + 1)
                    else:
                        for part in both:
                            drained_of(act, "lm", l, part[0])
                    if k >= 2:
                        act.wait_ge(sq_used, SQLNU[l] + k - 1)
                    n = TOK if l == 0 else SEQ
                    act.activation(sq[k % 2][:, 0:n], a_t[:, k, 0:n], ACT.Square).then_inc(sq_ready, 1)
                roots(("lv", l), both)
                for k in range(CT):
                    act.wait_ge(lnorm_done, CT * l + k + 1)
                    n = TOK if l == 0 else SEQ
                    act.activation(a_t[:, k, 0:n], a_t[:, k, 0:n], ACT.Silu, scale=par[l][:, R_LG + k:R_LG + k + 1],
                                   bias=par[l][:, R_LB + k:R_LB + k + 1]).then_inc(a_done, 1)
                def y_upper(dp):
                    n = TOK if l == 0 else SEQ
                    for k in (2 * dp, 2 * dp + 1):
                        act.wait_ge(merged, KT * l + k + 1)
                        act.activation(y_hi(k)[:, 0:n], y_t[:, k, 0:n], ACT.Copy).then_inc(y_hi_done, 1)

                order = [(dp, b, t) for b in range(4) for dp in range(KT // 2) for t in range(2)]
                for b in range(4):
                    for dp in range(KT // 2):
                        if b:
                            upper_tile(act, ("mg", l, dp, b), 2)
                        if b < 3:
                            upper_src(act, l, b + 1, dp)
                        for t in range(2):
                            if t and (dp, b) != (KT // 2 - 1, 3):
                                for tt in range(2):
                                    upper_tile(act, ("mg", l, (dp + 1) % 4, b + (dp == 3)), tt)
                                if b == 3 and dp:
                                    y_upper(dp - 1)
                            elif t:
                                y_upper(dp - 1)
                            for part in both:
                                key = ("g", l, dp, b, t, part[0])
                                full_of(act, *key)
                                at_ = order.index((dp, b, t))
                                if at_ >= 2:
                                    drained_of(act, "w", l, *order[at_ - 2], part[0])
                                col = R_GB + b * KT + 2 * dp + t
                                act.activation(sq[at_ % 2][:, part[1]:part[1] + part[2]], bank(*key)[:, 0:part[2]],
                                               ACT.Sigmoid, bias=par[l][:, col:col + 1]) \
                                    .then_inc(is_drained(*key), 1)
                upper_tile(act, ("wo", l, 0), 0)
                y_upper(KT // 2 - 1)
                for t in range(1, CT):
                    upper_tile(act, ("wo", l, 0), t)
                def ready1(k):
                    for part in both:
                        drained_of(act, "wo", l, k, part[0])
                        if k == 0:
                            for t in range(2):
                                drained_of(act, "w", l, KT // 2 - 1, 3, t, part[0])

                for t in range(KT):
                    for part in both:
                        full_of(act, "wo", l, t, part[0])
                        act.activation(yo_t[:, t, part[1]:part[1] + part[2]], bank("wo", l, t, part[0])[:, 0:part[2]],
                                       ACT.Copy).then_inc(is_drained("wo", l, t, part[0]), 1)
                    if t < CT:
                        upper_tile(act, ("wo", l, 1), t)
                    if t:
                        ready1(t - 1)
                        square(l, POST_MIX, yo_t, t - 1)
                ready1(KT - 1)
                square(l, POST_MIX, yo_t, KT - 1)
                roots(("ms", l, POST_MIX), both)
                squares(l, PRE_FFN, x_t, lambda k: act.wait_ge(x_updated, 8 * 2 * l + k + 1))
                modulated(l, PRE_FFN)
                nt = TT if l == 0 else LT
                drained_of(act, "rl", l)
                act.activation(aff[:, 0:nt, :], aff[:, 0:nt, :], ACT.Exp).then_inc(aff_exp, 1)
                for i in range(nt):
                    for h in range(2):
                        full_of(act, "ht", l, i, h)
                        act.activation(h_tok[:, i, 512 * h:512 * (h + 1)], bank("ht", l, i, h)[:, :], ACT.Copy) \
                            .then_inc(is_drained("ht", l, i, h), 1)
                for i in range(nt):
                    for h in range(2):
                        drained_of(act, "ht", l, i, h)
                    act.activation(h_hi[:, i, :], h_tok[:, i, :], ACT.Copy).then_inc(h_hi_done, 1)
                ns = sum(CAP) if l == 0 else CAP[0]
                for k in range(KT):
                    gather_out(act, l, k, 0, ns, lambda o, i: act.activation(o, i, ACT.Copy))
                    if l == 0:
                        gather_out(act, l, k, 2, ns, lambda o, i: act.activation(o, i, ACT.Copy))
                def experts(turn, loads):
                    for e in range(4):
                        for h in range(2):
                            full_of(act, "h1", l, e, h, turn=turn)
                            if e:
                                drained_of(act, "h3", l, e - 1, h, turn=turn)
                            else:
                                drained_of(act, "h3", l, 3, h, turn=turn - 1)
                            act.activation(silu_t[h][:, 0:4 * ns], bank("h1", l, e, h)[:, 0:4 * ns], ACT.Silu) \
                                .then_inc(is_drained("h1", l, e, h), 1)
                            if 6 * e + 2 * h + 1 < loads:
                                expert_load(act, l, turn, 6 * e + 2 * h + 1)
                            upper_parts(act, l, e, h, turn)
                        y_out(act, l, e, 0, turn, lambda o, i: act.activation(o, i, ACT.Copy))
                        if 6 * e + 5 < loads:
                            expert_load(act, l, turn, 6 * e + 5)

                with act.Fori(0, NE // 4 - 1) as turn:
                    experts(turn, 24)
                experts(NE // 4 - 1, 20)
                for part, npair in ((0, NE // 2), (1, NE // 4))[:len(both)]:
                    for p in range(0, npair, 2):
                        full_of(act, "sg", l, p, part)
                        act.activation(sg[part][:, p, :], bank("sg", l, p, part)[:, 0:(SEQ, CTX)[part]], ACT.Copy) \
                            .then_inc(is_drained("sg", l, p, part), 1)

                def ready2(k):
                    for part in both:
                        drained_of(act, "mo", l, k, part[0])

                for k in range(KT):
                    for part in both:
                        full_of(act, "mo", l, k, part[0])
                        act.activation(y_t[:, k, part[1]:part[1] + part[2]], bank("mo", l, k, part[0])[:, 0:part[2]],
                                       ACT.Copy).then_inc(is_drained("mo", l, k, part[0]), 1)
                    if k:
                        ready2(k - 1)
                        square(l, POST_FFN, y_t, k - 1)
                ready2(KT - 1)
                square(l, POST_FFN, y_t, KT - 1)
                roots(("ms", l, POST_FFN), both)

            for l in range(DEPTH):
                layer(l)
            for i in range(LT):
                full_of(act, "out", i, 0)
                act.activation(h_tok[:, i, 0:512], bank("out", i, 0)[:, :], ACT.Copy) \
                    .then_inc(is_drained("out", i, 0), 1)

        @block.vector
        def _(dve):
            steps = [0]

            def link(ins):
                steps[0] += 1
                ins.then_inc(dve_step, 1)
                dve.wait_ge(dve_step, steps[0])

            def mark(ins):
                steps[0] += 1
                ins.then_inc(dve_step, 1)
                return steps[0]

            def reciprocals(key, parts):
                for part in parts:
                    drained_of(dve, *key, part[0])
                    r = rb[:, part[1]:part[1] + part[2]]
                    link(dve.reciprocal(r, r))

            def normed(l, norm):
                if norm != PRE_MIX:
                    reciprocals(("ms", l, norm), parts_of(l, norm))
                pi = 2 * l + (0 if norm == PRE_MIX else 1)
                n = TOK if len(parts_of(l, norm)) == 2 else SEQ
                if norm == PRE_MIX:
                    for k in range(KT + 1):
                        if k < KT:
                            if k >= 2:
                                dve.wait_ge(h_ready, 8 * pi + k - 1)
                            dve.tensor_tensor(sq[k % 2], x_t[:, k, :], rb, ALU.mult).then_inc(xr_ready, 1)
                        if k:
                            dve.wait_ge(xr_ready, 8 * pi + k)
                            for w, first, cols in (LAT, CON):
                                cols = slice(first, first + cols)
                                op = dve.tensor_scalar(h_t[:, k - 1, cols], sq[(k - 1) % 2][:, cols],
                                                       scl[l][:, 0, k - 1, w:w + 1], mods[l][:, k - 1, w:w + 1],
                                                       ALU.mult, ALU.add)
                            op.then_inc(h_ready, 1)
                    return
                for k in range(KT):
                    if k >= 2:
                        dve.wait_ge(h_ready, 8 * pi + k - 1)
                    dve.tensor_tensor(sq[k % 2][:, 0:n], x_t[:, k, 0:n], rb[:, 0:n], ALU.mult).then_inc(xr_ready, 1)

            def sum_squares(l, norm):
                n = TOK if len(parts_of(l, norm)) == 2 else SEQ
                for k in range(1, KT):
                    dve.wait_ge(sq_ready, SQ0(l, norm) + k + 1)
                    if k > 1:
                        dve.wait_ge(sq_used, SQU(l, norm) + k - 1)
                    so_far = rb if k > 1 else sq[0]
                    dve.tensor_tensor(rb[:, 0:n], so_far[:, 0:n], sq[k % 2][:, 0:n], ALU.add).then_inc(sq_used, 1)

            def add_to_stream(l, norm, src):
                parts = parts_of(l, norm)
                reciprocals(("ms", l, norm), parts)
                n = TOK if len(parts) == 2 else SEQ
                m = 1 if norm == POST_MIX else 3
                for k in range(KT):
                    if k >= 2:
                        dve.wait_ge(x_updated, 8 * (2 * l + (norm == POST_FFN)) + k - 1)
                    link(dve.tensor_tensor(tmp[k % 2][:, 0:n], src[:, k, 0:n], rb[:, 0:n], ALU.mult))
                    for part in parts:
                        w, cols = part[0], slice(part[1], part[1] + part[2])
                        op = dve.scalar_tensor_tensor(x_t[:, k, cols], tmp[k % 2][:, cols], scl[l][:, m, k, w:w + 1],
                                                      x_t[:, k, cols], ALU.mult, ALU.add)
                    op.then_inc(x_updated, 1)

            for i in range(TT):
                full_of(dve, "xin", i, 1)
                dve.tensor_copy(x_t[:, 4:8, i * P:(i + 1) * P],
                                bank("xin", i, 1)[:, :].rearrange("p (k t) -> p k t", k=4)) \
                    .then_inc(is_drained("xin", i, 1), 1)
            for l in range(DEPTH):
                for r, (first, n) in enumerate(((0, NR1), (NR1, NR2), (NR1 + NR2, NR3))):
                    full_of(dve, "par", l, r)
                    dve.tensor_copy(par[l][:, first:first + n], bank("par", l, r)[:, 0:n]) \
                        .then_inc(is_drained("par", l, r), 1)
            for l in range(DEPTH):
                for r in range(3):
                    drained_of(dve, "par", l, r)
            dve.wait_ge(par_loaded, 16 * 25)
            link(dve.tensor_scalar(nsink, nsink, -1.0, None, ALU.mult))

            def modulation(l, c):
                full_of(dve, "mod", l, c)
                b = par[l][:, R_ADAB + 4 * c:R_ADAB + 4 * c + 4]
                dve.tensor_tensor(mods[l][:, 4 * c:4 * c + 4, :],
                                  bank("mod", l, c)[:, 0:8].rearrange("p (c w) -> p c w", w=2),
                                  b.unsqueeze(2).broadcast_to([P, 4, 2]), ALU.add).then_inc(is_drained("mod", l, c), 1)
                drained_of(dve, "mod", l, c)

            def modulation_at(*key):
                if row_before(key):
                    modulation(*row_before(key))
                if key in MOD_AT:
                    modulation(*MOD_AT[key])

            def vectors(l, v):
                return mods[l][:, v * KT:(v + 1) * KT, :]

            def gain(l, row):
                return par[l][:, row:row + KT].unsqueeze(2).broadcast_to([P, KT, 2])

            def norm_scale(l, m, v, row):
                link(dve.tensor_scalar(scl[l][:, m], vectors(l, v), 1.0, None, ALU.add))
                link(dve.tensor_tensor(scl[l][:, m], scl[l][:, m], gain(l, row), ALU.mult))

            def layer(l):
                both = parts_of(l)
                reciprocals(("ms", l, PRE_MIX), parts_of(l, PRE_MIX))
                if l == 0:
                    for c in range(MOD_FIRST):
                        modulation(l, c)
                    norm_scale(l, 0, 1, R_PM)
                normed(l, PRE_MIX)
                for pad, sizes, half in ((cpad, PADC, HC), (bpad, PADS, HS)):
                    for w in range(2):
                        first = sizes[0] * w
                        dve.memset(pad[:, :, first:first + half], 0.0)
                        z = dve.memset(pad[:, :, first + sizes[w] - half:first + sizes[w]], 0.0)
                z.then_inc(conv_zero, 1)
                for t in range(CT):
                    for part in both:
                        key = ("win", l, C_AG, t, part[0])
                        drained_of(dve, "win", l, C_AV, t, part[0])
                        drained_of(dve, *key)
                        j = GLU(l, t, part[0])
                        dst = cpad[:, t, PADC[0] * part[0] + HC:PADC[0] * part[0] + HC + part[2]]
                        dve.tensor_tensor(dst, dst, sq[j % 2][:, 0:part[2]], ALU.mult).then_inc(glu_done, 1)
                dve.wait_ge(glu_done, GLU(l, CT - 1, both[-1][0]) + 1)
                dve.wait_ge(conv_zero, l + 1)

                def conv_taps():
                    marks = {}
                    for j in range(CONV_K):
                        for t in range(CT):
                            for part in both:
                                first = PADC[0] * part[0] + j
                                src = cpad[:, t, first:first + part[2]]
                                dst = a_t[:, t, part[1]:part[1] + part[2]]
                                w = par[l][:, NR1 + j * CT + t:NR1 + j * CT + t + 1]
                                if j == 0:
                                    b = par[l][:, R_CB + t:R_CB + t + 1]
                                    op = dve.tensor_scalar(dst, src, w, b, ALU.mult, ALU.add)
                                else:
                                    dve.wait_ge(dve_step, marks[t, part[0]])
                                    op = dve.scalar_tensor_tensor(dst, src, w, dst, ALU.mult, ALU.add)
                                if j < CONV_K - 1:
                                    marks[t, part[0]] = mark(op)
                                else:
                                    op.then_inc(conv_done, 1)
                                yield

                taps = conv_taps()

                def convolve(n):
                    for _ in range(n):
                        next(taps, None)

                convolve(16)
                convolve(16)
                for t in range(CT):
                    for part in both:
                        convolve(8)
                        key = ("win", l, C_HV, t, part[0])
                        full_of(dve, *key)
                        drained_of(dve, "win", l, C_CG, t, part[0])
                        dst = bpad[:, t, PADS[0] * part[0] + HS:PADS[0] * part[0] + HS + part[2]]
                        dve.tensor_tensor(dst, bank(*key)[:, 0:part[2]], dst, ALU.mult).then_inc(is_drained(*key), 1)
                for t in range(CT):
                    if t >= 2:
                        dve.wait_ge(short_done, 4 * l + t - 1)
                    for part in both:
                        drained_of(dve, "win", l, C_HV, t, part[0])
                        drained_of(dve, "win", l, C_BG, t, part[0])
                        cols = slice(part[1], part[1] + part[2])
                        for j in range(SHORT_K):
                            first = PADS[0] * part[0] + j
                            src = bpad[:, t, first:first + part[2]]
                            c0 = NR1 + NR2 + j * CT + t
                            w = par[l][:, c0:c0 + 1]
                            if j == 0:
                                link(dve.tensor_scalar(sq[t % 2][:, cols], src, w, None, ALU.mult))
                            else:
                                link(dve.scalar_tensor_tensor(sq[t % 2][:, cols], src, w, sq[t % 2][:, cols], ALU.mult, ALU.add))
                        op = dve.tensor_tensor(b_t[:, t, cols], b_t[:, t, cols], sq[t % 2][:, cols], ALU.mult)
                    op.then_inc(short_done, 1)
                for t in range(CT + 1):
                    convolve(8)
                    if t == 0:
                        dve.wait_ge(short_done, 4 * (l + 1))
                    full_of(dve, "rope", l, t)
                    dst = q_t[:, t, 0:SEQ] if t < CT else k_t[:, 0, 0:SEQ]
                    if t >= 2:
                        dve.wait_ge(rope_done, 5 * l + t - 1)
                    dve.tensor_tensor(sq[t % 2][:, 0:SEQ], bank("rope", l, t)[:, :], sinT, ALU.mult) \
                        .then_inc(is_drained("rope", l, t), 1)
                    link(dve.tensor_tensor(dst, dst, cosT, ALU.mult))
                    drained_of(dve, "rope", l, t)
                    dve.tensor_tensor(dst, dst, sq[t % 2][:, 0:SEQ], ALU.add).then_inc(rope_done, 1)
                dve.wait_ge(rope_done, 5 * (l + 1))
                drained_of(dve, "k", l, 1)
                dve.tensor_copy(k_t[0:HD, 1, :], k_t[HD:P, 0, :]).then_inc(swapped, 1)
                dve.tensor_copy(k_t[HD:P, 1, :], k_t[0:HD, 0, :]).then_inc(swapped, 1)
                convolve(32)
                for g in range(1, CT):
                    modulation_at("fo", l, g)
                    convolve(24)
                units = att_units(l)

                def local_scores(u):
                    con, n, g = units[u]
                    lo, hi, _ = band(units[u])
                    if con:
                        return
                    if u == 0:
                        full_of(dve, "fo", l, CT - 1, both[-1][0])
                    for h in range(GRP):
                        full_of(dve, "sl", l, u, h)
                        if u >= 2 and h == 0:
                            full_of(dve, "pt", l, u - 2, band(units[u - 2])[2] - 1)
                        m0 = (lo - (n - 1)) * P
                        nl = (hi - lo) * P
                        dve.tensor_tensor(S_buf[u % 2][:, h, 0:nl], bank("sl", l, u, h)[:, 0:nl],
                                          maskT[:, m0:m0 + nl], ALU.add).then_inc(is_drained("sl", l, u, h), 1)

                def stats(u):
                    con, n, g = units[u]
                    nk = band(units[u])[2] * P
                    for h in range(GRP):
                        if not con:
                            drained_of(dve, "sl", l, u, h)
                        drained_of(dve, "sc", l, u, h)
                    link(dve.tensor_reduce(st[:, 0, :], S_buf[u % 2][:, :, 0:nk], AX.X, ALU.max))
                    ns = nsink[:, l * HEADS + GRP * g:l * HEADS + GRP * g + GRP]
                    link(dve.scalar_tensor_tensor(st[:, 1, :], st[:, 0, :], -(HD ** -0.5), ns, ALU.mult, ALU.min))
                    dve.tensor_tensor(st[:, 2, :], st[:, 1, :], ns, ALU.subtract).then_inc(stats_done, 1)

                def scale(u):
                    nk = band(units[u])[2] * P
                    for h in range(GRP):
                        dve.wait_ge(exps_done, 5 * (PROBS0[l] + u) + h + 2)
                        link(dve.tensor_tensor(st[:, 6, h:h + 1], st[:, 3, h:h + 1], st[:, 4, h:h + 1], ALU.add))
                        link(dve.reciprocal(st[:, 7, h:h + 1], st[:, 6, h:h + 1]))
                        S = S_buf[u % 2][:, h, 0:nk]
                        op = dve.tensor_scalar(S, S, st[:, 7, h:h + 1], None, ALU.mult)
                    op.then_inc(probs_done, 1)

                def turned(u):
                    for kt in range(1, band(units[u])[2], 2):
                        full_of(dve, "pt", l, u, kt)
                        if u:
                            full_of(dve, "av", l, u - 1)
                        dve.tensor_copy(probs_t[:, kt, :], bank("pt", l, u, kt)[:, :]) \
                            .then_inc(is_drained("pt", l, u, kt), 1)

                local_scores(0)
                for u in range(len(units)):
                    stats(u)
                    scale(u)
                    if u + 1 < len(units):
                        local_scores(u + 1)
                    modulation_at("att", l, u)
                    turned(u)
                    convolve(4)
                modulation_at("rows", l)
                convolve(CONV_K * CT * 2)
                dve.wait_ge(conv_done, CONV[l])
                for part in both:
                    full_of(dve, "lm", l, part[0])
                for k in range(CT):
                    for part in both:
                        cols = slice(part[1], part[1] + part[2])
                        op = dve.tensor_tensor(a_t[:, k, cols], a_t[:, k, cols], bank("lm", l, part[0])[:, 0:part[2]],
                                               ALU.subtract)
                        if k == CT - 1:
                            op.then_inc(is_drained("lm", l, part[0]), 1)
                        elif part is both[-1]:
                            op.then_inc(centred, 1)
                reciprocals(("lv", l), both)
                for k in range(CT):
                    n = TOK if l == 0 else SEQ
                    dve.tensor_tensor(a_t[:, k, 0:n], a_t[:, k, 0:n], rb[:, 0:n], ALU.mult).then_inc(lnorm_done, 1)
                modulation_at("lv", l)
                at_ = -1
                for b in range(4):
                    for dp in range(KT // 2):
                        for t in range(2):
                            at_ += 1
                            for part in both:
                                cols = slice(part[1], part[1] + part[2])
                                key = ("w", l, dp, b, t, part[0])
                                full_of(dve, *key)
                                drained_of(dve, "g", l, dp, b, t, part[0])
                                gate, y = sq[at_ % 2][:, cols], y_t[:, 2 * dp + t, cols]
                                dst = y if b == 0 else rb[:, cols]
                                dve.tensor_tensor(dst, gate, bank(*key)[:, 0:part[2]], ALU.mult) \
                                    .then_inc(is_drained(*key), 1)
                                if b:
                                    drained_of(dve, *key)
                                    if b == 3 and part is both[-1]:
                                        dve.tensor_tensor(y, y, rb[:, cols], ALU.add).then_inc(merged, 1)
                                        dve.wait_ge(merged, 8 * l + 2 * dp + t + 1)
                                    else:
                                        link(dve.tensor_tensor(y, y, rb[:, cols], ALU.add))
                                else:
                                    drained_of(dve, *key)
                v = [mark(dve.tensor_tensor(scl[l][:, m], vectors(l, at), gain(l, row), ALU.mult))
                     for m, at, row in ((1, 2, R_QM), (3, 5, R_QF))]
                dve.wait_ge(dve_step, v[-1])
                norm_scale(l, 2, 4, R_PF)
                sum_squares(l, POST_MIX)
                dve.wait_ge(x_back, 16 * (l + 1))
                add_to_stream(l, POST_MIX, yo_t)
                modulation_at("post", l)
                dve.wait_ge(x_updated, 8 * (2 * l + 1))
                normed(l, PRE_FFN)
                modulation_at("pre", l, 0)
                modulation_at("pre", l, 1)
                nt = TT if l == 0 else LT
                full_of(dve, "rl", l)
                lg = bank("rl", l)[:, 0:nt * NE].rearrange("p (i e) -> p i e", e=NE)
                link(dve.tensor_reduce(rs[:, 0, 0:nt], lg, AX.X, ALU.max))
                dve.tensor_tensor(aff[:, 0:nt, :], lg, rs[:, 0, 0:nt].unsqueeze(2).broadcast_to([P, nt, NE]),
                                  ALU.subtract).then_inc(is_drained("rl", l), 1)
                drained_of(dve, "rl", l)
                dve.wait_ge(aff_exp, l + 1)
                link(dve.tensor_reduce(rs[:, 0, 0:nt], aff[:, 0:nt, :], AX.X, ALU.add))
                link(dve.reciprocal(rs[:, 1, 0:nt], rs[:, 0, 0:nt]))
                dve.tensor_tensor(aff[:, 0:nt, :], aff[:, 0:nt, :],
                                  rs[:, 1, 0:nt].unsqueeze(2).broadcast_to([P, nt, NE]), ALU.mult) \
                    .then_inc(aff_done, 1)
                E = slice(0, NE)
                link(dve.memset(sel_e[E, 0, :], 1.0))
                for w, (_, first, n) in enumerate(both):
                    cols = slice(first, first + n)
                    full_of(dve, "at", l, w)
                    dve.tensor_copy(sel_e[E, 1, cols], bank("at", l, w)[0:NE, 0:n]) \
                        .then_inc(is_drained("at", l, w), 1)
                    drained_of(dve, "at", l, w)
                    for _ in range(CAP[w] // 8):
                        link(dve.max(top8[E, 0:8], sel_e[E, 1, cols]))
                        link(dve.match_replace(sel_e[E, 1, cols], top8[E, 0:8], sel_e[E, 1, cols], -1.0))
                    link(dve.tensor_scalar(sel_e[E, 2, cols], sel_e[E, 1, cols], 0.0, None, ALU.is_lt))
                    link(dve.tensor_tensor_scan(sel_e[E, 3, cols], sel_e[E, 0, cols], sel_e[E, 2, cols], 0.0,
                                                ALU.mult, ALU.add))
                    link(dve.tensor_tensor(sel_e[E, 3, cols], sel_e[E, 3, cols], sel_e[E, 2, cols], ALU.mult))
                    dve.tensor_scalar(sel_e[E, 3, cols], sel_e[E, 3, cols], -1.0, None, ALU.add) \
                        .then_inc(pos_done, 1)
                modulation_at("ht", l)
                full_of(dve, "pos", l)
                dve.tensor_copy(pos_t[:, 0:nt, :], bank("pos", l)[:, 0:nt * NE].rearrange("p (i e) -> p i e", e=NE)) \
                    .then_inc(is_drained("pos", l), 1)
                drained_of(dve, "pos", l)

                def per_tile(i):
                    w = 0 if i < LT else 1
                    return w, onehot[w][:, i - w * LT, :].rearrange("p (e s) -> p e s", e=NE)

                for i in range(nt):
                    w, oh = per_tile(i)
                    oh = onehot_r[w][:, i - w * LT, :].rearrange("p (e s) -> p e s", e=NE)
                    dve.tensor_tensor(oh, iota[:, 0:CAP[w]].unsqueeze(1).broadcast_to([P, NE, CAP[w]]),
                                      pos_t[:, i, :].unsqueeze(2).broadcast_to([P, NE, CAP[w]]), ALU.is_equal) \
                        .then_inc(onehot_done, 1)
                ns = sum(CAP) if l == 0 else CAP[0]
                for k in range(KT):
                    gather_out(dve, l, k, 1, ns, dve.tensor_copy)
                full_of(dve, "ga", l, KT - 1, 2 if l == 0 else 1)
                for i in range(nt):
                    w, oh = per_tile(i)
                    ones_zeros = onehot_r[w][:, i - w * LT, :].bitcast(F32).rearrange("p (e s) -> p e s", e=NE)
                    dve.tensor_tensor(oh, ones_zeros, aff[:, i, :].unsqueeze(2).broadcast_to([P, NE, CAP[w]]), ALU.mult) \
                        .then_inc(og_done, 1)
                if l + 1 < DEPTH:
                    norm_scale(l + 1, 0, 1, R_PM)
                for t in (hid_hi, hid_lo):
                    dve.tensor_scalar(t[:, KT * ns:(KT - 1) * ns + P], iota[:, 0:P - ns], 0.0, None, ALU.mult)
                with dve.Fori(0, NE // 4) as turn:
                    for e in range(4):
                        for h in range(2):
                            full_of(dve, "h3", l, e, h, turn=turn)
                            drained_of(dve, "h1", l, e, h, turn=turn)
                            if e:
                                full_of(dve, "y", l, e - 1, 1, turn=turn)
                            else:
                                full_of(dve, "y", l, 3, 1, turn=turn - 1)
                            t, cols = silu_t[h][:, 0:4 * ns], slice(4 * ns * h, 4 * ns * (h + 1))
                            n = 16 * NE // 4 * l + 4 * e + 2 * h
                            dve.tensor_tensor(t, t, bank("h3", l, e, h)[:, 0:4 * ns], ALU.mult).then_inc(hid_step, 1)
                            dve.wait_ge(hid_step, n + 1 + 16 * turn)
                            dve.tensor_copy(hid_hi[:, cols], t).then_inc(hid_step, 1)
                            dve.wait_ge(hid_step, n + 2 + 16 * turn)
                            dve.tensor_tensor(hid_lo[:, cols], t, hid_hi[:, cols].bitcast(F32), ALU.subtract) \
                                .then_inc(is_drained("h3", l, e, h), 1)
                        lower_parts(dve, l, e, 1, turn)
                        y_out(dve, l, e, 1, turn, dve.tensor_copy)
                for part, npair in ((0, NE // 2), (1, NE // 4))[:len(both)]:
                    for p in range(1, npair, 2):
                        full_of(dve, "sg", l, p, part)
                        dve.tensor_copy(sg[part][:, p, :], bank("sg", l, p, part)[:, 0:(SEQ, CTX)[part]]) \
                            .then_inc(is_drained("sg", l, p, part), 1)
                sum_squares(l, POST_FFN)
                add_to_stream(l, POST_FFN, y_t)

            for l in range(DEPTH):
                layer(l)
            for i in range(LT):
                full_of(dve, "out", i, 1)
                dve.tensor_copy(h_tok[:, i, 512:1024], bank("out", i, 1)[:, :]) \
                    .then_inc(is_drained("out", i, 1), 1)


def tables():
    f = np.float32
    ident = np.eye(P, dtype=f)
    perm = np.zeros((P, P), f)
    for m in range(P):
        if m % 32 < 16:
            perm[m + 16, m] = -1
        else:
            perm[m - 16, m] = 1
    t = np.arange(SEQ)
    inv = (10000.0 ** (-np.arange(16, dtype=f) / f(16))).astype(f)
    ar = ((t // GRID_W).astype(f)[:, None] * inv).astype(f)
    ac = ((t % GRID_W).astype(f)[:, None] * inv).astype(f)
    ang = np.concatenate([ar, ar, ac, ac], 1).T.astype(np.float64)
    ang = np.concatenate([ang, ang], 0)
    kj, qi = np.arange(3 * P)[None, :], np.arange(P)[:, None]
    mask = np.where(np.abs(kj - P - qi) <= P, 0.0, -1e30).astype(f)

    def dft(n, fn, by):
        k = np.arange(n)
        m = fn(2 * np.pi * ((k[:, None] * k[None, :]) % n) / n) * by
        return m.reshape(n // P, P, n).transpose(1, 0, 2).reshape(P, -1)

    d = np.concatenate([dft(SEQ, np.cos, SEQ ** -0.5), dft(SEQ, np.sin, SEQ ** -0.5),
                        dft(CTX, np.cos, CTX ** -0.5), dft(CTX, np.sin, CTX ** -0.5),
                        dft(P, np.cos, P ** -0.5), dft(P, np.sin, -P ** -0.5)], 1).astype(f)
    return {"ident": ident, "ones_d": np.full((P, P), 1 / D, f), "ones_c": np.full((P, P), 1 / DC, f), "perm": perm,
            "cos": np.cos(ang).astype(f), "sin": np.sin(ang).astype(f), "mask": mask,
            "iota": np.broadcast_to(np.arange(CAP[0], dtype=f), (P, CAP[0])).copy(), "dft": d}


def kernel(**inputs):
    import concourse.bacc as bacc
    from concourse.bass_utils import run_bass_kernel_spmd

    nc = bacc.Bacc("TRN2", target_bir_lowering=False, num_devices=1)
    arrays, ins, consts = {}, {}, {}
    for group, prefix, source in ((ins, "in", inputs), (consts, "const", tables())):
        for name, a in source.items():
            a = np.ascontiguousarray(a)
            arrays[f"{prefix}_{name}"] = a
            group[name] = nc.dram_tensor(f"{prefix}_{name}", a.shape, mybir.dt.from_np(a.dtype),
                                         kind="ExternalInput").ap()
    out = nc.dram_tensor("out", (1, SEQ, D), F32, kind="ExternalOutput").ap()
    x_dram = nc.dram_tensor("x_dram", (P, KT, TOK), F32, kind="Internal").ap()
    build(nc, ins, consts, x_dram, out)
    r = run_bass_kernel_spmd(nc, [arrays], core_ids=[0])
    return r.results[0]["out"]
```
